# Optimizing a Trainium2 kernel written in Bass

```python
import math
import jax, jax.numpy as jnp
from jax import lax
import numpy as np

D_MODEL = 1024
BATCH = 1
SEQ = 128
DEPTH = 1
DEC_BATCH = 1
DEC_SEQ = 512
PAST_LEN = 128

GRID_W = 64
N_DIFF_HEADS = 4
DIFF_HEAD_DIM = 64
ATT_WIDTH = N_DIFF_HEADS * 2 * DIFF_HEAD_DIM
N_FOURIER_GROUPS = 4
FOURIER_GROUP_DIM = 128
FOURIER_WIDTH = N_FOURIER_GROUPS * FOURIER_GROUP_DIM
MIX_WIDTH = ATT_WIDTH + FOURIER_WIDTH
IN_WIDTH = 3 * ATT_WIDTH + FOURIER_WIDTH
ROPE_BASE = 10000.0
Q_BLOCK = 128
N_PEER_HEADS = 8
PEER_KEY_DIM = 256
N_KEYS = 128
N_EXPERTS = N_KEYS * N_KEYS
PEER_TOPK = 16
TOKEN_BLOCK = 128
EPS = 1e-6

kernel_name = "hybrid_diffattn_fnet_peer_dit_step"

def rmsnorm(x, g):
    x32 = x.astype(jnp.float32)
    y = x32 * lax.rsqrt(jnp.mean(x32 * x32, axis=-1, keepdims=True) + EPS)
    return y.astype(x.dtype) * g

def modulation(cond, w_mod, b_mod):
    m = jax.nn.silu(cond) @ w_mod + b_mod
    return jnp.split(m[..., None, :], 6, axis=-1)

def axial_rope(n_tok):
    rows = n_tok // GRID_W
    row = jnp.repeat(jnp.arange(rows), GRID_W).astype(jnp.float32)
    col = jnp.tile(jnp.arange(GRID_W), rows).astype(jnp.float32)
    nf = DIFF_HEAD_DIM // 4
    inv = ROPE_BASE ** (-jnp.arange(nf, dtype=jnp.float32) / nf)
    ar = row[:, None] * inv
    ac = col[:, None] * inv
    ang = jnp.concatenate([ar, ar, ac, ac], axis=-1)
    return jnp.cos(ang)[:, None, None, :], jnp.sin(ang)[:, None, None, :]

def apply_rope(x, cos, sin):
    a, b, c, d = jnp.split(x, 4, axis=-1)
    rot = jnp.concatenate([-b, a, -d, c], axis=-1)
    return (x.astype(jnp.float32) * cos + rot.astype(jnp.float32) * sin).astype(x.dtype)

def split_in(h, w_in):
    B, S, _ = h.shape
    z = h @ w_in
    q = z[..., :ATT_WIDTH].reshape(B, S, N_DIFF_HEADS, 2, DIFF_HEAD_DIM)
    k = z[..., ATT_WIDTH:2 * ATT_WIDTH].reshape(B, S, N_DIFF_HEADS, 2, DIFF_HEAD_DIM)
    v = z[..., 2 * ATT_WIDTH:3 * ATT_WIDTH].reshape(B, S, N_DIFF_HEADS, 2 * DIFF_HEAD_DIM)
    f = z[..., 3 * ATT_WIDTH:]
    return q, k, v, f

def diff_lambda(lq1, lk1, lq2, lk2, lam_init):
    return (jnp.exp(jnp.sum((lq1 * lk1).astype(jnp.float32)))
            - jnp.exp(jnp.sum((lq2 * lk2).astype(jnp.float32))) + lam_init)

def diff_attention(q, k, v, lam):
    B, Sq, H, _, d = q.shape
    nb = Sq // Q_BLOCK
    scale = d ** -0.5
    qb = q.reshape(B, nb, Q_BLOCK, H, 2, d).swapaxes(0, 1)

    def block(qblk):
        s = jnp.einsum('bqhmd,bkhmd->mbhqk', qblk, k).astype(jnp.float32) * scale
        p = jax.nn.softmax(s, axis=-1)
        w = p[0] - lam * p[1]
        return jnp.einsum('bhqk,bkhe->bqhe', w.astype(v.dtype), v)

    o = lax.map(block, qb)
    return o.swapaxes(0, 1).reshape(B, Sq, H, 2 * d)

def fourier_mix(f, w_f):
    B, S, _ = f.shape
    fg = f.reshape(B, S, N_FOURIER_GROUPS, FOURIER_GROUP_DIM).astype(jnp.float32)
    spec = jnp.fft.fft2(fg, axes=(1, 3), norm='ortho').real.astype(f.dtype)
    return jnp.einsum('bsgc,gce->bsge', spec, w_f).reshape(B, S, FOURIER_WIDTH)

def mixer_merge(att, four, subln_g, lam_init, w_out):
    B, S = att.shape[:2]
    a = rmsnorm(att, subln_g) * (1.0 - lam_init)
    m = jnp.concatenate([a.reshape(B, S, ATT_WIDTH), four], axis=-1)
    return m @ w_out

def peer(h, w_query, sub_keys, expert_u, expert_v):
    B, S, D = h.shape
    T = B * S
    hf = h.reshape(T, D)
    q = (hf @ w_query).reshape(T, N_PEER_HEADS, 2, PEER_KEY_DIM // 2)
    s = jnp.einsum('thpk,hpnk->thpn', q, sub_keys)
    s1, i1 = lax.top_k(s[:, :, 0], PEER_TOPK)
    s2, i2 = lax.top_k(s[:, :, 1], PEER_TOPK)
    cand = (s1[..., :, None] + s2[..., None, :]).reshape(T, N_PEER_HEADS, PEER_TOPK * PEER_TOPK)
    cand_idx = (i1[..., :, None] * N_KEYS + i2[..., None, :]).reshape(T, N_PEER_HEADS, PEER_TOPK * PEER_TOPK)
    top_s, pos = lax.top_k(cand, PEER_TOPK)
    idx = jnp.take_along_axis(cand_idx, pos, axis=-1)
    g = jax.nn.softmax(top_s.astype(jnp.float32), axis=-1).astype(h.dtype)
    nb = T // TOKEN_BLOCK
    nk = N_PEER_HEADS * PEER_TOPK
    hb = hf.reshape(nb, TOKEN_BLOCK, D)
    ib = idx.reshape(nb, TOKEN_BLOCK, nk)
    gb = g.reshape(nb, TOKEN_BLOCK, nk)

    def block(args):
        hx, ix, gx = args
        a = jax.nn.gelu(jnp.einsum('tkd,td->tk', expert_u[ix], hx), approximate=False)
        return jnp.einsum('tk,tkd->td', gx * a, expert_v[ix])

    out = lax.map(block, (hb, ib, gb))
    return out.reshape(B, S, D)

def setup_inputs(seed: int = 0) -> dict:
    key = jax.random.key(seed)
    ks = jax.random.split(key, 24)
    f32 = jnp.float32
    nrm = lambda k, shp, sc: jax.random.normal(k, shp, f32) * sc
    D = D_MODEL
    cshape = (DEC_BATCH, DEPTH, PAST_LEN, N_DIFF_HEADS, 2 * DIFF_HEAD_DIM)
    return {
        "x_prompt": nrm(ks[0], (BATCH, SEQ, D), 1.0),
        "x_sample": nrm(ks[1], (DEC_BATCH, DEC_SEQ, D), 1.0),
        "cache_k": nrm(ks[2], cshape, 1.0),
        "cache_v": nrm(ks[3], cshape, 1.0),
        "c": nrm(ks[4], (DEC_BATCH, D), 1.0),
        "c_ctx": nrm(ks[5], (D,), 1.0),
        "w_mod": nrm(ks[6], (DEPTH, D, 6 * D), D ** -0.5),
        "b_mod": nrm(ks[7], (DEPTH, 6 * D), 0.01),
        "norm1_g": 1.0 + nrm(ks[8], (DEPTH, D), 0.05),
        "w_in": nrm(ks[9], (DEPTH, D, IN_WIDTH), D ** -0.5),
        "lam_q1": nrm(ks[10], (DEPTH, DIFF_HEAD_DIM), 0.1),
        "lam_k1": nrm(ks[11], (DEPTH, DIFF_HEAD_DIM), 0.1),
        "lam_q2": nrm(ks[12], (DEPTH, DIFF_HEAD_DIM), 0.1),
        "lam_k2": nrm(ks[13], (DEPTH, DIFF_HEAD_DIM), 0.1),
        "subln_g": 1.0 + nrm(ks[14], (DEPTH, 2 * DIFF_HEAD_DIM), 0.05),
        "w_fourier": nrm(ks[15], (DEPTH, N_FOURIER_GROUPS, FOURIER_GROUP_DIM, FOURIER_GROUP_DIM), FOURIER_GROUP_DIM ** -0.5),
        "w_out": nrm(ks[16], (DEPTH, MIX_WIDTH, D), MIX_WIDTH ** -0.5),
        "norm2_g": 1.0 + nrm(ks[17], (DEPTH, D), 0.05),
        "w_query": nrm(ks[18], (DEPTH, D, N_PEER_HEADS * PEER_KEY_DIM), D ** -0.5),
        "sub_keys": nrm(ks[19], (DEPTH, N_PEER_HEADS, 2, N_KEYS, PEER_KEY_DIM // 2), (PEER_KEY_DIM // 2) ** -0.5),
        "expert_u": nrm(ks[20], (DEPTH, N_EXPERTS, D), D ** -0.5),
        "expert_v": nrm(ks[21], (DEPTH, N_EXPERTS, D), 0.5),
        "final_g": 1.0 + nrm(ks[22], (D,), 0.05),
    }

def reference(x_prompt, x_sample, cache_k, cache_v, c, c_ctx, w_mod, b_mod, norm1_g, w_in,
              lam_q1, lam_k1, lam_q2, lam_k2, subln_g, w_fourier, w_out, norm2_g,
              w_query, sub_keys, expert_u, expert_v, final_g):
    B, S, _ = x_prompt.shape
    Bd, Sd, _ = x_sample.shape
    P = cache_k.shape[2]
    cos, sin = axial_rope(Sd)
    xp, xs = x_prompt, x_sample
    new_k, new_v = [], []
    for l in range(DEPTH):
        lam_init = 0.8 - 0.6 * math.exp(-0.3 * l)
        lam = diff_lambda(lam_q1[l], lam_k1[l], lam_q2[l], lam_k2[l], lam_init)

        sh1, sc1, g1, sh2, sc2, g2 = modulation(c_ctx, w_mod[l], b_mod[l])
        h = rmsnorm(xp, norm1_g[l]) * (1 + sc1) + sh1
        q, k, v, f = split_in(h, w_in[l])
        att = diff_attention(q, k, v, lam)
        four = fourier_mix(f, w_fourier[l])
        xp = xp + g1 * mixer_merge(att, four, subln_g[l], lam_init, w_out[l])
        h2 = rmsnorm(xp, norm2_g[l]) * (1 + sc2) + sh2
        xp = xp + g2 * peer(h2, w_query[l], sub_keys[l], expert_u[l], expert_v[l])
        new_k.append(k.reshape(B, S, N_DIFF_HEADS, 2 * DIFF_HEAD_DIM))
        new_v.append(v)

        sh1, sc1, g1, sh2, sc2, g2 = modulation(c, w_mod[l], b_mod[l])
        h = rmsnorm(xs, norm1_g[l]) * (1 + sc1) + sh1
        q, k, v, f = split_in(h, w_in[l])
        q = apply_rope(q, cos, sin)
        k = apply_rope(k, cos, sin)
        ck = cache_k[:, l].reshape(Bd, P, N_DIFF_HEADS, 2, DIFF_HEAD_DIM)
        k_all = jnp.concatenate([ck, k], axis=1)
        v_all = jnp.concatenate([cache_v[:, l], v], axis=1)
        att = diff_attention(q, k_all, v_all, lam)
        four = fourier_mix(f, w_fourier[l])
        xs = xs + g1 * mixer_merge(att, four, subln_g[l], lam_init, w_out[l])
        h2 = rmsnorm(xs, norm2_g[l]) * (1 + sc2) + sh2
        xs = xs + g2 * peer(h2, w_query[l], sub_keys[l], expert_u[l], expert_v[l])

    y_prompt = rmsnorm(xp, final_g)
    y_sample = rmsnorm(xs, final_g)
    state_k = jnp.stack(new_k, axis=1)
    state_v = jnp.stack(new_v, axis=1)
    return (y_prompt, y_sample, state_k, state_v)


_drawn_inputs = setup_inputs


def setup_inputs(seed=0):
    import zlib

    import numpy as np

    out = dict(_drawn_inputs(seed))
    spreads = {}
    factors = {'lam_q1': 5.712}
    for name, (base, spread) in spreads.items():
        noise = np.random.default_rng([zlib.crc32(name.encode()), seed]).standard_normal(out[name].shape)
        drawn = base * np.exp(spread * noise) if base else spread * noise
        out[name] = __import__('jax').numpy.asarray(drawn.astype(out[name].dtype))
    for name, factor in factors.items():
        out[name] = (out[name] * factor).astype(out[name].dtype)
    return out
```

```python
import math
from contextlib import ExitStack

import numpy as np
import concourse.bass as bass
from concourse import mybir

P = 128
D = 1024
KD = D // P
NBLK = 5
NSMP = 4
H = 4
DH = 64
NC = 512
MOD_CH = 12
IN_CH = 4
OUT_CH = 2
KEYS_S = 640
PH = 8
TOPK = 16
NKEY = 128
SLOTS = PH * TOPK
LAM_INIT = 0.8 - 0.6 * math.exp(-0.3 * 0)
EPS = 1e-6
NEG = -3.0e38
WRING = 3
UR = 4
VR = 4


def _phase1_jobs():
    jobs = [(("mod", j), "act") for j in range(MOD_CH)]
    jobs.append((("keyT", "cache"), "act"))
    jobs += [(("hT", b, half), "act") for b in range(NBLK) for half in range(2)]
    for c in ("k", "q"):
        for b in range(NBLK):
            jobs.append((("z", c, b), "act" if b == 0 else "dve"))
            if b >= 1:
                jobs.append((("headT", c, b - 1), "act"))
        jobs.append((("headT", c, NBLK - 1), "act"))
    jobs += [(("z", c, b), "act") for c in ("v", "f") for b in range(NBLK)]
    jobs += [(("fold", 0), "act"), (("fold", 1), "dve")]
    units = [(s, g) for s in range(2) for g in range(4)]
    for i, u in enumerate(units):
        jobs += [(("fcos",) + u, "act"), (("fsin",) + u, "dve")]
        if i:
            jobs.append((("fmix",) + units[i - 1], "act"))
    jobs.append((("fmix",) + units[-1], "act"))
    return jobs


def _phase2_jobs():
    jobs = []
    for b in range(NBLK):
        jobs += [(("merge", b, half), "dve") for half in range(2)]
    for b in range(NBLK):
        jobs += [(("h2T", b, half), "act") for half in range(2)]
        for g in range(4):
            jobs += [(("query", b, g), "act"), (("score", b, g), "dve")]
    return jobs


class Banks:

    def __init__(self, jobs, nbanks):
        self.pos = {name: n for n, (name, _) in enumerate(jobs)}
        self.who = [w for _, w in jobs]
        self.nbanks = nbanks
        self.total = len(jobs)

    def emptied(self, n):
        return self.who[n], sum(w == self.who[n] for w in self.who[:n + 1])

    def count(self, who):
        return sum(w == who for w in self.who)


def program(nc, xall, condT, w_mod, b_mod, norm1_g, w_in, lam4, subln_g, w_fourier, w_out, norm2_g,
            w_query, keysT, expert_u, expert_v, final_g, cache_k, cache_v,
            ident_d, cos_d, sin_d, dft_seq_d, dft_ch_d, y, state_k, state_v):
    f32, u32 = mybir.dt.float32, mybir.dt.uint32
    ALU, ACT, AX = mybir.AluOpType, mybir.ActivationFunctionType, mybir.AxisListType
    B1, B2 = Banks(_phase1_jobs(), 8), Banks(_phase2_jobs(), 4)

    ctx = ExitStack()
    with ctx:
        def sb(name, shape, dt=f32):
            return ctx.enter_context(nc.sbuf_tensor(name, shape, dt))

        def sem(name):
            return ctx.enter_context(nc.semaphore(name))

        xreg = sb("xreg", [P, NBLK * D])
        X = xreg[:, :].rearrange("p (b d) -> p b d", b=NBLK)
        F = xreg[:, 0:NBLK * NC].rearrange("p (b n) -> p b n", b=NBLK)
        fstage = xreg[:, 2560:4608].rearrange("p (r m n) -> p r m n", r=2, m=2)
        Wt = xreg[:, 0:1280].rearrange("p (r n) -> p r n", r=2)
        probs = xreg[:, 2560:3840].rearrange("p (m n) -> p m n", m=2)
        breg = sb("breg", [P, NBLK * D])
        HT = breg[:, :].rearrange("p (k t) -> p k t", k=KD)
        H2 = breg[:, :].rearrange("p (b d) -> p b d", b=NBLK)
        dftS = breg[:, 0:4096].rearrange("p (m s n) -> p m s n", m=2, s=NSMP)
        dftC = breg[:, 4096:4480].rearrange("p (m n) -> p m n", m=3)
        wf = breg[:, 4480:4992].rearrange("p (g n) -> p g n", g=4)
        wreg = sb("wreg", [P, WRING * KD * NC + NBLK * D])
        chunk = wreg[:, 0:WRING * KD * NC].rearrange("p (r k n) -> p r k n", r=WRING, k=KD)
        H1 = wreg[:, WRING * KD * NC:].rearrange("p (b d) -> p b d", b=NBLK)
        mixT = wreg[:, WRING * KD * NC:].rearrange("p (k t) -> p k t", k=KD)
        wq = wreg[:, 0:KD * 2048].rearrange("p (k n) -> p k n", k=KD)
        diag = wreg[:, 16384:16384 + VR * P].rearrange("p (r n) -> p r n", r=VR)
        modt = sb("modt", [P, 2 * 4 * D])
        M = modt[:, :].rearrange("p (c w d) -> p c w d", c=2, w=4)
        SC2, SH2, G1, G2 = range(4)
        fing = M[:, 0, SC2, :]
        creg = sb("creg", [P, 15360])
        bmod = creg[0:1, 0:6144]
        gbc = creg[:, 6144:8192].rearrange("p (w d) -> p w d", w=2)
        rows = creg[0:33, 8192:9216].rearrange("p (r n) -> p r n", r=2)
        M1 = creg[:, 9216:13312].rearrange("p (c w d) -> p c w d", c=2, w=2)
        sil = creg[:, 13824:14088].rearrange("p (k c) -> p k c", k=KD)
        cond = creg[:, 14088:14104].rearrange("p (k c) -> p k c", k=KD)
        lamv = creg[:, 14104:14360].rearrange("p (w e) -> p w e", w=4)
        kT = creg[:, 0:3072].rearrange("p (h t) -> p h t", h=H)
        qT = creg[:, 3072:5632].rearrange("p (h t) -> p h t", h=H)
        V = creg[:, 5632:8704].rearrange("p (b n) -> p b n", b=6)
        WtT = creg[:, 8704:9984].rearrange("p (r s n) -> p r s n", r=2, s=5)
        ropet = creg[:, 9984:11008].rearrange("p (w n) -> p w n", w=2)
        heads = creg[:, 11008:12032].rearrange("p (r n) -> p r n", r=2)
        ropec = creg[:, 12032:12544].rearrange("p (w b e) -> p w b e", w=2, b=NSMP)
        ktc = creg[:, 13312:13824]
        att = creg[:, 12544:13056]
        fold = creg[:, 13824:14848].rearrange("p (m g n) -> p m g n", m=2, g=4)
        h2T = creg[:, 0:2048].rearrange("p (r k t) -> p r k t", r=2, k=KD)
        keys = creg[:, 2048:4096].rearrange("p (g n) -> p g n", g=16)
        onehot = creg[:, 4096:6144].rearrange("p (s j) -> p s j", j=TOPK)
        Ur = creg[:, 6144:10240].rearrange("p (r d) -> p r d", r=UR)
        Vr = creg[:, 10240:14336].rearrange("p (r d) -> p r d", r=VR)
        cand = creg[:, 14336:14592]
        top = creg[:, 14592:14720].rearrange("p (h j) -> p h j", h=PH)
        posf = creg[:, 14720:14848]
        cand2 = creg[:, 14848:15104]
        rest = creg[:, 14848:15104].rearrange("p (w n) -> p w n", w=2)
        idxf = creg[:, 15104:15360].rearrange("p (h w j) -> p h w j", h=PH, w=2)
        qTq = wreg[:, 16896:17408].rearrange("p (g t) -> p g t", g=4)

        ident = sb("ident", [P, P])
        ones = sb("ones", [1, 33])
        lam = sb("lam", [P, 8])
        gsub = sb("gsub", [P, 1])
        powe = sb("powe", [P, 8])
        ss = sb("ss", [P, NBLK])
        rstd = sb("rstd", [P, NBLK])
        amax = sb("amax", [P, 2, 2])
        asum = sb("asum", [P, 2, 2])
        ss4 = sb("ss4", [P, 2, H])
        iota = sb("iota", [P, TOPK])
        idx = sb("idx", [P, 2, SLOTS], u32)
        idxn = sb("idxn", [P, 2, UR], u32)
        gates = sb("gates", [P, SLOTS])
        dots = sb("dots", [P, SLOTS])
        coef = sb("coef", [P, SLOTS])
        best = sb("best", [P, PH, 2, TOPK])
        besti = sb("besti", [P, PH, 2, TOPK], u32)
        pos = sb("pos", [P, PH, TOPK], u32)
        posb = sb("posb", [P, PH, TOPK], u32)
        sel = sb("sel", [P, 2, SLOTS])
        gsum = sb("gsum", [P, 2, PH])

        ps = ctx.enter_context(nc.psum_tensor("ps", [P, 8, NC], f32))

        s_x = sem("s_x"); s_cond = sem("s_cond"); s_const = sem("s_const"); s_bmod = sem("s_bmod")
        s_gbc = sem("s_gbc"); s_kc = sem("s_kc"); s_vc = sem("s_vc"); s_rope = sem("s_rope")
        s_dft = sem("s_dft"); s_wf = sem("s_wf"); s_wq = sem("s_wq"); s_keys = sem("s_keys"); s_fing = sem("s_fing")
        s_chunk = [sem(f"s_chunk{i}") for i in range(WRING)]
        s_chunk_used = sem("s_chunk_used")
        s_xr = [sem(f"s_xr{b}") for b in range(NBLK)]
        s_out = sem("s_out")
        s_set = sem("s_set"); s_exps = sem("s_exps"); s_sil = sem("s_sil")
        s_lamsum = sem("s_lamsum"); s_lamexp = sem("s_lamexp"); s_lam = sem("s_lam")
        s_fill1 = sem("s_fill1"); s_act1 = sem("s_act1"); s_dve1 = sem("s_dve1")
        s_rows = sem("s_rows"); s_bc = sem("s_bc")
        s_sq1 = sem("s_sq1"); s_var1 = sem("s_var1"); s_rstd1 = sem("s_rstd1"); s_h1 = sem("s_h1"); s_mod2 = sem("s_mod2")
        s_head = sem("s_head")
        s_scores = sem("s_scores"); s_amax = sem("s_amax"); s_exp = sem("s_exp"); s_w = sem("s_w")
        s_wT = sem("s_wT"); s_wTc = sem("s_wTc"); s_pv = sem("s_pv"); s_asq = sem("s_asq"); s_avar = sem("s_avar")
        s_arstd = sem("s_arstd"); s_att = sem("s_att"); s_attT = sem("s_attT"); s_mix = sem("s_mix")
        s_fill2 = sem("s_fill2"); s_act2 = sem("s_act2"); s_dve2 = sem("s_dve2")
        s_x1 = sem("s_x1"); s_sq2 = sem("s_sq2"); s_var2 = sem("s_var2"); s_rstd2 = sem("s_rstd2"); s_h2 = sem("s_h2")
        s_top = sem("s_top"); s_gexp = sem("s_gexp"); s_idx = sem("s_idx"); s_gate = sem("s_gate")
        s_staged = sem("s_staged"); s_ixu = sem("s_ixu"); s_ixv = sem("s_ixv")
        s_u = [sem(f"s_u{i}") for i in range(UR)]
        s_v = [sem(f"s_v{i}") for i in range(VR)]
        s_dot = sem("s_dot"); s_gelu = sem("s_gelu"); s_coef = sem("s_coef")
        s_diag = sem("s_diag"); s_acc = sem("s_acc")
        s_x2 = sem("s_x2"); s_sq3 = sem("s_sq3"); s_var3 = sem("s_var3"); s_rstd3 = sem("s_rstd3"); s_y = sem("s_y")
        s_step = sem("s_step"); s_accfree = sem("s_accfree"); s_setp = sem("s_setp")

        CHUNKS = MOD_CH + IN_CH + OUT_CH
        IN_ORDER = {"k": 0, "q": 1, "v": 2, "f": 3}
        IN_COL = {"q": 0, "k": 1, "v": 2, "f": 3}
        w_mod_v = w_mod.rearrange("(k p) n -> p k n", p=P)
        w_in_v = w_in.rearrange("(k p) n -> p k n", p=P)
        w_out_v = w_out.rearrange("(k p) n -> p k n", p=P)
        w_query_v = w_query.rearrange("(k p) n -> p k n", p=P)
        UNITS = [(b, h) for b in range(NBLK) for h in range(H)]

        def seq(u):
            return 1 if u[0] else 0

        block = ctx.enter_context(nc.Block())

        @block.sync
        def _(sp):
            sp.dma_start(X, xall.rearrange("(b p) d -> p b d", p=P)).then_inc(s_x, 16)
            for i in range(CHUNKS):
                if i >= WRING:
                    sp.wait_ge(s_chunk_used, i - WRING + 1)
                if i < MOD_CH:
                    src = w_mod_v[:, :, i * NC:(i + 1) * NC]
                elif i < MOD_CH + IN_CH:
                    c = [IN_COL[x] for x in ("k", "q", "v", "f")][i - MOD_CH]
                    src = w_in_v[:, :, c * NC:(c + 1) * NC]
                else:
                    c = i - MOD_CH - IN_CH
                    src = w_out_v[:, :, c * NC:(c + 1) * NC]
                sp.dma_start(chunk[:, i % WRING], src).then_inc(s_chunk[i % WRING], 16)
                if i == MOD_CH + IN_CH - 1:
                    sp.wait_ge(s_fill1, B1.pos[("z", "f", NBLK - 1)] + 1)
                    sp.dma_start(dftS, dft_seq_d).then_inc(s_dft, 16)
                    sp.dma_start(dftC, dft_ch_d).then_inc(s_dft, 16)
                    sp.dma_start(wf, w_fourier).then_inc(s_dft, 16)
            sp.wait_ge(s_wT, len(UNITS))
            for b in range(NBLK):
                sp.dma_start(X[:, b], xall[b * P:(b + 1) * P, :]).then_inc(s_xr[b], 16)
            sp.wait_ge(s_mix, NBLK)
            sp.dma_start(keys, keysT).then_inc(s_keys, 16)
            sp.wait_ge(s_fill2, 2 * NBLK)
            sp.dma_start(wq, w_query_v).then_inc(s_wq, 16)
            sp.wait_ge(s_h2, 1)
            sp.dma_start(fing, final_g.unsqueeze(0).broadcast_to([P, D])).then_inc(s_fing, 16)
            for b in range(NBLK):
                sp.wait_ge(s_y, b + 1)
                sp.dma_start(y[b * P:(b + 1) * P, :], X[:, b]).then_inc(s_out, 16)
            sp.wait_ge(s_out, 16 * (NBLK + 2))

        @block.gpsimd
        def _(pool):
            pool.iota(iota[:, :], pattern=[[1, TOPK]], base=0, channel_multiplier=0,
                      allow_small_or_imprecise_dtypes=True).then_inc(s_setp, 1)
            pool.memset(powe[:, :], -0.5).then_inc(s_setp, 1)
            pool.wait_ge(s_setp, 2)

            def spread_mod(j):
                pool.wait_ge(s_rows, j + 1)
                part, half = j // 2, j % 2
                cols = slice(half * NC, (half + 1) * NC)
                for c in range(2):
                    if part < 2:
                        dst = M1[:, c, 1 - part, cols]
                    else:
                        w = {2: G1, 3: SH2, 4: SC2, 5: G2}[part]
                        dst = M[:, c, w, cols]
                    pool.partition_broadcast(dst, rows[32 * c:32 * c + 1, j % 2, :], P).then_inc(s_bc, 1)

            for j in range(4):
                spread_mod(j)
            pool.wait_ge(s_bc, 8)
            pool.wait_ge(s_var1, 1)
            pool.tensor_tensor(rstd[:, :], ss[:, :], powe[:, 0:NBLK], ALU.pow).then_inc(s_rstd1, 1)
            pool.wait_ge(s_rstd1, 1)
            for j in range(4, MOD_CH):
                spread_mod(j)
            pool.wait_ge(s_bc, 2 * MOD_CH)
            for b in range(NBLK):
                pool.wait_ge(s_avar, b + 1)
                if b >= 2:
                    pass
                pool.tensor_tensor(ss4[:, 1, :], ss4[:, 0, :], powe[:, 0:H], ALU.pow).then_inc(s_arstd, 1)
            for b in range(NBLK):
                pool.wait_ge(s_var2, b + 1)
                pool.tensor_tensor(rstd[:, b:b + 1], ss[:, b:b + 1], powe[:, 0:1], ALU.pow).then_inc(s_rstd2, 1)

            def gathers(b, table, ring, n, arrived, ix_sem, used, unit):
                base = b * (SLOTS // n)
                steps = SLOTS // n

                def step(g, first):
                    if not first:
                        pool.wait_ge(used, g * n)
                    pool.tensor_copy(idxn[:, unit, :], idx[:, b % 2, bass.ds((g - base) * n, n)]).then_inc(ix_sem, 1)
                    pool.wait_ge(ix_sem, g + 1)
                    pool.sem_inc(s_staged, 1)
                    for r in range(n):
                        pool.indirect_dma_start(
                            out=ring[:, r, :], out_offset=None, in_=table,
                            in_offset=bass.IndirectOffsetOnAxis(ap=idxn[:, unit, r:r + 1], axis=0)
                        ).then_inc(arrived[r], 16)

                if b == 0:
                    step(0, True)
                    with pool.Fori(1, steps) as g:
                        step(g, False)
                else:
                    with pool.Fori(base, base + steps) as g:
                        step(g, False)

            for b in range(NBLK):
                pool.wait_ge(s_idx, b + 1)
                gathers(b, expert_u, Ur, UR, s_u, s_ixu, s_dot, 0)
                gathers(b, expert_v, Vr, VR, s_v, s_ixv, s_acc, 1)
                pool.wait_ge(s_var3, b + 1)
                pool.tensor_tensor(rstd[:, b:b + 1], ss[:, b:b + 1], powe[:, 0:1], ALU.pow).then_inc(s_rstd3, 1)

        @block.scalar
        def _(act):
            act.dma_start(cond[:, :, :], condT).then_inc(s_cond, 16)
            act.dma_start(bmod, b_mod).then_inc(s_bmod, 16)
            act.dma_start(ident[:, :], ident_d).then_inc(s_const, 16)
            act.dma_start(lamv[:, :, :], lam4.unsqueeze(0).broadcast_to([P, 4, DH])).then_inc(s_const, 16)
            act.dma_start(gsub[:, :], subln_g.unsqueeze(1)).then_inc(s_const, 16)
            act.dma_start(gbc[:, 0, :], norm1_g.unsqueeze(0).broadcast_to([P, D])).then_inc(s_gbc, 16)
            act.dma_start(gbc[:, 1, :], norm2_g.unsqueeze(0).broadcast_to([P, D])).then_inc(s_gbc, 16)
            act.dma_start(ktc, cache_k).then_inc(s_kc, 16)
            n = {"act": 0}

            def emptied1():
                return s_act1

            act.wait_ge(s_cond, 16)
            act.wait_ge(s_set, 1)
            act.activation(sil[:, :, 0:2], cond[:, :, :], ACT.Exp, scale=-1.0).then_inc(s_exps, 1)
            act.wait_ge(s_lamsum, 1)
            act.activation(lam[:, 2:4], lam[:, 0:2], ACT.Exp).then_inc(s_lamexp, 1)
            act.wait_ge(s_x, 16)
            for b in range(NBLK):
                if b:
                    act.wait_ge(s_sq1, b)
                act.activation(breg[:, 0:D], X[:, b], ACT.Square, accum_out=ss[:, b:b + 1]).then_inc(s_sq1, 1)

            def bank1(*name):
                i = B1.pos[name]
                act.wait_ge(s_fill1, i + 1)
                return ps[:, i % 8, :]

            for j in range(MOD_CH):
                src = bank1("mod", j)
                if j >= 2:
                    act.wait_ge(s_bc, 2 * (j - 1))
                act.copy(rows[0:33, j % 2, :], src[0:33, :]).then_inc(s_rows, 1)
                act.sem_inc(s_act1, 1) if False else None
                act.wait_ge(s_rows, j + 1)
                act.nop().then_inc(s_act1, 1)

            def heads_out(name, dst):
                act.copy(dst, bank1(*name).rearrange("p (h t) -> p h t", h=H)).then_inc(s_act1, 1)

            act.wait_ge(s_mod2, 1)
            act.wait_ge(s_h1, NBLK)
            act.dma_start(ropec[:, 0], cos_d).then_inc(s_rope, 16)
            act.dma_start(ropec[:, 1], sin_d).then_inc(s_rope, 16)
            act.dma_start(V[:, 1, :], cache_v).then_inc(s_vc, 16)
            heads_out(("keyT", "cache"), kT[:, :, P:2 * P])
            for b in range(NBLK):
                for half in range(2):
                    src = bank1("hT", b, half).rearrange("p (k t) -> p k t", k=4)
                    act.copy(HT[:, 4 * half:4 * half + 4, b * P:(b + 1) * P], src).then_inc(s_act1, 1)
            for ci, c in enumerate(("k", "q")):
                for b in range(NBLK):
                    if b == 0:
                        if ci:
                            act.wait_ge(s_fill1, B1.pos[("headT", "k", NBLK - 1)] + 1)
                            act.wait_ge(s_out, 16)
                        act.copy(heads[:, 0, :], bank1("z", c, 0)).then_inc(s_act1, 1)
                        if ci == 0:
                            act.wait_ge(s_act1, B1.emptied(B1.pos[("z", "k", 0)])[1])
                            act.dma_start(state_k, heads[:, 0, :]).then_inc(s_out, 16)
                    else:
                        dst = kT if c == "k" else qT
                        at = (b - 1) * P if c == "q" or b == 1 else b * P
                        heads_out(("headT", c, b - 1), dst[:, :, at:at + P])
                dst, at = (kT, 5 * P) if c == "k" else (qT, 4 * P)
                heads_out(("headT", c, NBLK - 1), dst[:, :, at:at + P])
            for b in range(NBLK):
                vb = 0 if b == 0 else b + 1
                act.copy(V[:, vb, :], bank1("z", "v", b)).then_inc(s_act1, 1)
                if b == 0:
                    act.wait_ge(s_act1, B1.emptied(B1.pos[("z", "v", 0)])[1])
                    act.dma_start(state_v, V[:, 0, :]).then_inc(s_out, 16)
            for b in range(NBLK):
                act.copy(F[:, b, :], bank1("z", "f", b)).then_inc(s_act1, 1)
            act.copy(fold[:, 0], bank1("fold", 0).rearrange("p (g n) -> p g n", g=4)).then_inc(s_act1, 1)
            units = [(s, g) for s in range(2) for g in range(4)]

            def mix_out(u):
                s, g = u
                src = bank1("fmix", s, g)
                if s == 0:
                    act.copy(mixT[:, 4 + g, 0:P], src[:, 0:P]).then_inc(s_act1, 1)
                else:
                    act.copy(mixT[:, 4 + g, P:NBLK * P], src).then_inc(s_act1, 1)

            for i, u in enumerate(units):
                w = NC if u[0] else P
                src = bank1("fcos", *u)
                act.copy(fstage[:, i % 2, 0, 0:w], src[:, 0:w]).then_inc(s_act1, 1)
                if i:
                    mix_out(units[i - 1])
            mix_out(units[-1])

            def keys_of(b):
                return P if b == 0 else KEYS_S // 2

            def exps(i):
                b, h = UNITS[i]
                for m in range(2):
                    act.wait_ge(s_scores, 2 * i + m + 1)
                    act.wait_ge(s_amax, i + 1)
                    if i >= 1:
                        act.wait_ge(s_w, i)
                    n_ = keys_of(b)
                    src = ps[:, 2 * m:2 * m + (1 if b == 0 else 2), 0:n_]
                    dst = probs[:, m, 0:(1 if b == 0 else 2) * n_].rearrange("p (z n) -> p z n", n=n_)
                    act.activation(dst, src, ACT.Exp, bias=amax[:, i % 2, m:m + 1], scale=DH ** -0.5,
                                   accum_out=asum[:, i % 2, m:m + 1]).then_inc(s_exp, 1)

            def weights_out(i):
                b, h = UNITS[i]
                act.wait_ge(s_wT, i + 1)
                if i >= 2:
                    act.wait_ge(s_pv, i - 1)
                if b == 0:
                    act.copy(WtT[:, i % 2, 0, :], ps[:, 4, 0:P]).then_inc(s_wTc, 1)
                else:
                    act.copy(WtT[:, i % 2, 0:4, :], ps[:, 4, :].rearrange("p (s n) -> p s n", s=4))
                    act.copy(WtT[:, i % 2, 4, :], ps[:, 5, 0:P]).then_inc(s_wTc, 1)

            def att_squares(b):
                act.wait_ge(s_pv, H * (b + 1))
                if b:
                    act.wait_ge(s_attT, b)
                for h in range(H):
                    ins = act.activation(att[:, h * P:(h + 1) * P], ps[:, 6, h * P:(h + 1) * P], ACT.Square,
                                         accum_out=ss4[:, 0, h:h + 1])
                ins.then_inc(s_asq, 1)

            def att_out(b):
                act.wait_ge(s_attT, b + 1)
                act.activation(mixT[:, 0:4, b * P:(b + 1) * P], ps[:, 7, :].rearrange("p (h t) -> p h t", h=H),
                               ACT.Copy, scale=lam[:, 7:8]).then_inc(s_mix, 1)

            act.wait_ge(s_lam, 1)
            for i in range(len(UNITS) + 1):
                if i < len(UNITS):
                    exps(i)
                if i >= 1:
                    weights_out(i - 1)
                    if i % H == 0:
                        att_squares(i // H - 1)
                if i % H == 1 and i > H:
                    att_out(i // H - 1)
            att_out(NBLK - 1)

            for b in range(NBLK):
                act.wait_ge(s_x1, 2 * (b + 1))
                act.activation(H2[:, b], X[:, b], ACT.Square, accum_out=ss[:, b:b + 1]).then_inc(s_sq2, 1)

            def bank2(*name):
                i = B2.pos[name]
                act.wait_ge(s_fill2, i + 1)
                return ps[:, i % 4, :]

            def front(b):
                for half in range(2):
                    src = bank2("h2T", b, half).rearrange("p (k t) -> p k t", k=4)
                    act.copy(h2T[:, b % 2, 4 * half:4 * half + 4, :], src).then_inc(s_act2, 1)
                for g in range(4):
                    act.copy(qTq, bank2("query", b, g).rearrange("p (g t) -> p g t", g=4)).then_inc(s_act2, 1)
                act.wait_ge(s_top, b + 1)
                act.activation(top[:, :, :], top[:, :, :], ACT.Exp).then_inc(s_gexp, 1)

            def diags(b):
                base = b * SLOTS

                def step(g, first):
                    for r in range(VR):
                        if not first:
                            act.wait_ge(s_acc, g * VR + r - VR + 1)
                        act.activation(diag[:, r, :], ident[:, :], ACT.Copy,
                                       scale=coef[:, bass.ds(g * VR + r - base, 1)]).then_inc(s_diag, 1)
                act.wait_ge(s_coef, b + 1)
                if b == 0:
                    step(0, True)
                    with act.Fori(1, SLOTS // VR) as g:
                        step(g, False)
                else:
                    with act.Fori(base // VR, (base + SLOTS) // VR) as g:
                        step(g, False)

            front(0)
            for b in range(NBLK):
                act.wait_ge(s_dot, (b + 1) * SLOTS)
                if b:
                    act.wait_ge(s_acc, b * SLOTS)
                act.activation(dots[:, :], dots[:, :], ACT.Gelu).then_inc(s_gelu, 1)
                if b + 1 < NBLK:
                    front(b + 1)
                diags(b)
                act.wait_ge(s_x2, b + 1)
                act.activation(H2[:, b], X[:, b], ACT.Square, accum_out=ss[:, b:b + 1]).then_inc(s_sq3, 1)

        @block.vector
        def _(dve):
            steps = [0]

            def link(ins):
                steps[0] += 1
                ins.then_inc(s_step, 1)
                dve.wait_ge(s_step, steps[0])

            link(dve.memset(sil[:, :, :], 0.0))
            dve.memset(ones[:, :], 1.0).then_inc(s_set, 1)
            dve.wait_ge(s_const, 48)
            link(dve.tensor_tensor(lamv[:, 0:2, :], lamv[:, 0:2, :], lamv[:, 2:4, :], ALU.mult))
            dve.tensor_reduce(lam[:, 0:2], lamv[:, 0:2, :], AX.X, ALU.add).then_inc(s_lamsum, 1)
            dve.wait_ge(s_exps, 1)
            link(dve.tensor_scalar(sil[:, :, 0:2], sil[:, :, 0:2], 1.0, None, ALU.add))
            link(dve.reciprocal(sil[:, :, 0:2], sil[:, :, 0:2]))
            link(dve.tensor_tensor(cond[:, :, :], cond[:, :, :], sil[:, :, 0:2], ALU.mult))
            link(dve.memset(sil[:, :, 0:2], 0.0))
            link(dve.tensor_copy(sil[:, :, 0:1], cond[:, :, 0:1]))
            dve.tensor_copy(sil[:, :, 32:33], cond[:, :, 1:2]).then_inc(s_sil, 1)
            dve.wait_ge(s_lamexp, 1)
            link(dve.tensor_tensor(lam[:, 4:5], lam[:, 3:4], lam[:, 2:3], ALU.subtract))
            link(dve.tensor_scalar(lam[:, 5:6], lam[:, 4:5], -LAM_INIT, None, ALU.add))
            dve.tensor_scalar(lam[:, 7:8], gsub[:, :], 1.0 - LAM_INIT, None, ALU.mult).then_inc(s_lam, 1)
            dve.wait_ge(s_sq1, NBLK)
            dve.tensor_scalar(ss[:, :], ss[:, :], 1.0 / D, EPS, ALU.mult, ALU.add).then_inc(s_var1, 1)
            dve.wait_ge(s_bc, 8)
            dve.wait_ge(s_gbc, 32)
            for c in range(2):
                link(dve.scalar_tensor_tensor(out=M1[:, c, 0, :], in0=M1[:, c, 0, :], scalar=1.0,
                                              in1=gbc[:, 0, :], op0=ALU.add, op1=ALU.mult))
            dve.wait_ge(s_rstd1, 1)
            for b in range(NBLK):
                c = min(b, 1)
                link(dve.scalar_tensor_tensor(out=H1[:, b], in0=X[:, b], scalar=rstd[:, b:b + 1],
                                              in1=M1[:, c, 0, :], op0=ALU.mult, op1=ALU.mult))
                dve.tensor_tensor(H1[:, b], H1[:, b], M1[:, c, 1, :], ALU.add).then_inc(s_h1, 1)
            dve.wait_ge(s_bc, 2 * MOD_CH)
            for c in range(2):
                link(dve.scalar_tensor_tensor(out=M[:, c, SC2, :], in0=M[:, c, SC2, :], scalar=1.0,
                                              in1=gbc[:, 1, :], op0=ALU.add, op1=ALU.mult))
            dve.sem_inc(s_mod2, 1) if False else dve.nop().then_inc(s_mod2, 1)

            def bank1(*name):
                i = B1.pos[name]
                dve.wait_ge(s_fill1, i + 1)
                return ps[:, i % 8, :]

            def rope(c, b, count):
                z = bank1("z", c, b)
                if b >= 2:
                    dve.wait_ge(s_fill1, B1.pos[("headT", c, b - 2)] + 1)
                elif c == "q":
                    dve.wait_ge(s_fill1, B1.pos[("headT", "k", 3)] + 1)
                if count:
                    dve.wait_ge(s_dve1, count)
                out = heads[:, b % 2, :]
                zg = z.rearrange("p (g e) -> p g e", g=8)
                zs = z.rearrange("p (g w e) -> p g w e", g=16, w=2)
                t0 = ropet[:, 0, :].rearrange("p (g e) -> p g e", g=8)
                t1 = ropet[:, 1, :].rearrange("p (g u w e) -> p g u w e", g=8, u=2, w=2)
                zu = z.rearrange("p (g u w e) -> p g u w e", g=8, u=2, w=2)
                cos = ropec[:, 0, b - 1, :].unsqueeze(1).broadcast_to([P, 8, DH])
                sin = ropec[:, 1, b - 1, :].rearrange("p (u w e) -> p u w e", u=2, w=2)
                dve.tensor_tensor(t0, zg, cos, ALU.mult)
                for w in range(2):
                    sw = sin[:, :, w, :].unsqueeze(1).broadcast_to([P, 8, 2, 16])
                    ins = dve.tensor_tensor(t1[:, :, :, w, :], zu[:, :, :, 1 - w, :], sw, ALU.mult)
                steps[0] += 1
                ins.then_inc(s_step, 1)
                dve.wait_ge(s_step, steps[0])
                dve.tensor_tensor(out, ropet[:, 0, :], ropet[:, 1, :], ALU.add).then_inc(s_dve1, 1)

            dve.wait_ge(s_rope, 32)
            count = 0
            for c in ("k", "q"):
                for b in range(1, NBLK):
                    if b == 2 and c == "k":
                        dve.wait_ge(s_out, 16)
                    rope(c, b, count)
                    count += 1
            dve.tensor_copy(fold[:, 1], bank1("fold", 1).rearrange("p (g n) -> p g n", g=4)).then_inc(s_dve1, 1)
            units = [(s, g) for s in range(2) for g in range(4)]
            for i, u in enumerate(units):
                w = NC if u[0] else P
                src = bank1("fsin", *u)
                if i >= 2:
                    dve.wait_ge(s_fill1, B1.pos[("fmix",) + units[i - 2]] + 1)
                dve.tensor_copy(fstage[:, i % 2, 1, 0:w], src[:, 0:w]).then_inc(s_dve1, 1)

            dve.wait_ge(s_lam, 1)

            def neg_max(i):
                b, h = UNITS[i]
                dve.wait_ge(s_scores, 2 * i + 2)
                if i >= 2:
                    dve.wait_ge(s_exp, 2 * (i - 1))
                z, n_ = (1, P) if b == 0 else (2, KEYS_S // 2)
                src = ps[:, 0:4, :].rearrange("p (m z) n -> p m z n", m=2)[:, :, 0:z, 0:n_]
                link(dve.tensor_reduce(amax[:, i % 2, :], src, AX.XY, ALU.max, negate=True))
                dve.tensor_scalar(amax[:, i % 2, :], amax[:, i % 2, :], DH ** -0.5, None, ALU.mult).then_inc(s_amax, 1)

            def combine(i):
                b, h = UNITS[i]
                n_ = P if b == 0 else KEYS_S
                dve.wait_ge(s_exp, 2 * i + 2)
                link(dve.reciprocal(asum[:, i % 2, :], asum[:, i % 2, :]))
                dve.tensor_tensor(asum[:, i % 2, 1:2], asum[:, i % 2, 1:2], lam[:, 5:6], ALU.mult)
                if i >= 2:
                    dve.wait_ge(s_wT, i - 1)
                link(dve.tensor_scalar(Wt[:, i % 2, 0:n_], probs[:, 0, 0:n_], asum[:, i % 2, 0:1], None, ALU.mult))
                dve.scalar_tensor_tensor(out=Wt[:, i % 2, 0:n_], in0=probs[:, 1, 0:n_], scalar=asum[:, i % 2, 1:2],
                                         in1=Wt[:, i % 2, 0:n_], op0=ALU.mult, op1=ALU.add).then_inc(s_w, 1)

            def att_norm(b):
                dve.wait_ge(s_asq, b + 1)
                dve.tensor_scalar(ss4[:, 0, :], ss4[:, 0, :], 1.0 / P, EPS, ALU.mult, ALU.add).then_inc(s_avar, 1)
                dve.wait_ge(s_arstd, b + 1)
                dve.tensor_tensor(att.rearrange("p (h e) -> p h e", h=H), ps[:, 6, :].rearrange("p (h e) -> p h e", h=H),
                                  ss4[:, 1, :].unsqueeze(2).broadcast_to([P, H, P]), ALU.mult).then_inc(s_att, 1)

            for i in range(len(UNITS)):
                neg_max(i)
                if i:
                    pass
                combine(i)
                if i % H == 0 and i:
                    att_norm(i // H - 1)
            att_norm(NBLK - 1)

            def bank2(*name):
                i = B2.pos[name]
                dve.wait_ge(s_fill2, i + 1)
                return ps[:, i % 4, :]

            dve.wait_ge(s_sq2, 0) if False else None
            for b in range(NBLK):
                c = min(b, 1)
                dve.wait_ge(s_xr[b], 16)
                for half in range(2):
                    cols = slice(half * NC, (half + 1) * NC)
                    src = bank2("merge", b, half)
                    dve.tensor_tensor(H2[:, b, cols], src, M[:, c, G1, cols], ALU.mult).then_inc(s_dve2, 1)
                    dve.wait_ge(s_dve2, B2.emptied(B2.pos[("merge", b, half)])[1])
                    dve.tensor_tensor(X[:, b, cols], X[:, b, cols], H2[:, b, cols], ALU.add).then_inc(s_x1, 1)
            for b in range(NBLK):
                c = min(b, 1)
                dve.wait_ge(s_sq2, b + 1)
                dve.tensor_scalar(ss[:, b:b + 1], ss[:, b:b + 1], 1.0 / D, EPS, ALU.mult, ALU.add).then_inc(s_var2, 1)
                dve.wait_ge(s_rstd2, b + 1)
                link(dve.scalar_tensor_tensor(out=H2[:, b], in0=X[:, b], scalar=rstd[:, b:b + 1],
                                              in1=M[:, c, SC2, :], op0=ALU.mult, op1=ALU.mult))
                dve.tensor_tensor(H2[:, b], H2[:, b], M[:, c, SH2, :], ALU.add).then_inc(s_h2, 1)

            def retrieve(b):
                for g in range(4):
                    bank = bank2("score", b, g).rearrange("p (h w n) -> p h w n", h=2, w=2)
                    for hh in range(2):
                        h = 2 * g + hh
                        for w in range(2):
                            s = bank[:, hh, w, :]
                            link(dve.max(best[:, h, w, 0:8], s))
                            dve.max_index(besti[:, h, w, 0:8], best[:, h, w, 0:8], s)
                            link(dve.match_replace(rest[:, w, :], best[:, h, w, 0:8], s, NEG))
                        for w in range(2):
                            link(dve.max(best[:, h, w, 8:16], rest[:, w, :]))
                            ins = dve.max_index(besti[:, h, w, 8:16], best[:, h, w, 8:16], rest[:, w, :])
                        if hh == 1:
                            ins.then_inc(s_dve2, 1)
                        c3 = cand.rearrange("p (i j) -> p i j", i=TOPK)
                        link(dve.tensor_tensor(c3, best[:, h, 0, :].unsqueeze(2).broadcast_to([P, TOPK, TOPK]),
                                               best[:, h, 1, :].unsqueeze(1).broadcast_to([P, TOPK, TOPK]), ALU.add))
                        link(dve.max(top[:, h, 0:8], cand))
                        dve.max_index(pos[:, h, 0:8], top[:, h, 0:8], cand)
                        link(dve.match_replace(cand2, top[:, h, 0:8], cand, NEG))
                        link(dve.max(top[:, h, 8:16], cand2))
                        link(dve.max_index(pos[:, h, 8:16], top[:, h, 8:16], cand2))
                link(dve.tensor_copy(gsum[:, 1, :], top[:, :, 0]))
                dve.tensor_tensor(top[:, :, :], top[:, :, :],
                                  gsum[:, 1, :].unsqueeze(2).broadcast_to([P, PH, TOPK]),
                                  ALU.subtract).then_inc(s_top, 1)
                link(dve.tensor_copy(idxf.rearrange("p h w j -> p (h w j)"), besti[:, :, :, :].rearrange("p h w j -> p (h w j)")))
                link(dve.tensor_scalar(posb[:, :, :], pos[:, :, :], 4, None, ALU.logical_shift_right))
                link(dve.tensor_scalar(pos[:, :, :], pos[:, :, :], 15, None, ALU.bitwise_and))
                for w, source in ((0, posb), (1, pos)):
                    link(dve.tensor_copy(posf[:, :], source[:, :, :].rearrange("p h j -> p (h j)")))
                    link(dve.tensor_tensor(onehot, posf[:, :].unsqueeze(2).broadcast_to([P, SLOTS, TOPK]),
                                           iota[:, :].unsqueeze(1).broadcast_to([P, SLOTS, TOPK]), ALU.is_equal))
                    o4 = onehot.rearrange("p (h s) j -> p h s j", h=PH)
                    link(dve.tensor_tensor(o4, o4, idxf[:, :, w, :].unsqueeze(2).broadcast_to([P, PH, TOPK, TOPK]), ALU.mult))
                    link(dve.tensor_reduce(sel[:, w, :], onehot, AX.X, ALU.add))
                if b >= 2:
                    pass
                dve.scalar_tensor_tensor(out=idx[:, b % 2, :], in0=sel[:, 0, :], scalar=float(NKEY), in1=sel[:, 1, :],
                                         op0=ALU.mult, op1=ALU.add).then_inc(s_idx, 1)

            def gate_weights(b):
                dve.wait_ge(s_gexp, b + 1)
                link(dve.tensor_reduce(gsum[:, 0, :], top[:, :, :], AX.X, ALU.add))
                link(dve.reciprocal(gsum[:, 0, :], gsum[:, 0, :]))
                dve.tensor_tensor(gates[:, :].rearrange("p (h j) -> p h j", h=PH), top[:, :, :],
                                  gsum[:, 0, :].unsqueeze(2).broadcast_to([P, PH, TOPK]), ALU.mult).then_inc(s_gate, 1)

            def dot_rows(b):
                with dve.Fori(b * (SLOTS // UR), (b + 1) * (SLOTS // UR)) as g:
                    for r in range(UR):
                        dve.wait_ge(s_u[r], g * 16 + 16)
                        dve.scalar_tensor_tensor(out=Ur[:, r, :], in0=Ur[:, r, :], scalar=1.0, in1=H2[:, b, :],
                                                 op0=ALU.mult, op1=ALU.mult,
                                                 accum_out=dots[:, bass.ds(g * UR + r - b * SLOTS, 1)]).then_inc(s_dot, 1)

            dve.wait_ge(s_out, 32)
            retrieve(0)
            gate_weights(0)
            for b in range(NBLK):
                dot_rows(b)
                dve.wait_ge(s_gelu, b + 1)
                if b:
                    dve.wait_ge(s_diag, b * SLOTS)
                dve.wait_ge(s_gate, b + 1)
                dve.tensor_tensor(coef[:, :], dots[:, :], gates[:, :], ALU.mult).then_inc(s_coef, 1)
                dve.wait_ge(s_coef, b + 1)
                if b + 1 < NBLK:
                    retrieve(b + 1)
                    gate_weights(b + 1)
                c = min(b, 1)
                dve.wait_ge(s_acc, (b + 1) * SLOTS)
                link(dve.tensor_tensor(H2[:, b].rearrange("p (z n) -> p z n", z=2), ps[:, 4 + 2 * (b % 2):6 + 2 * (b % 2), :],
                                       M[:, c, G2, :].rearrange("p (z n) -> p z n", z=2), ALU.mult))
                dve.tensor_tensor(X[:, b], X[:, b], H2[:, b], ALU.add).then_inc(s_x2, 1)
                dve.wait_ge(s_sq3, b + 1)
                dve.tensor_scalar(ss[:, b:b + 1], ss[:, b:b + 1], 1.0 / D, EPS, ALU.mult, ALU.add).then_inc(s_var3, 1)
                dve.wait_ge(s_rstd3, b + 1)
                dve.wait_ge(s_fing, 16)
                dve.scalar_tensor_tensor(out=X[:, b], in0=X[:, b], scalar=rstd[:, b:b + 1], in1=fing,
                                         op0=ALU.mult, op1=ALU.mult).then_inc(s_y, 1)

        @block.tensor
        def _(pe):
            def bank1(*name):
                i = B1.pos[name]
                if i >= 8:
                    who, n = B1.emptied(i - 8)
                    pe.wait_ge(s_act1 if who == "act" else s_dve1, n)
                return ps[:, i % 8, :]

            def chunk_ready(i):
                pe.wait_ge(s_chunk[i % WRING], 16 * (i // WRING + 1))

            pe.wait_ge(s_sil, 1)
            pe.wait_ge(s_set, 1)
            pe.wait_ge(s_bmod, 16)
            for j in range(MOD_CH):
                out = bank1("mod", j)
                chunk_ready(j)
                for k in range(KD):
                    last = nc.tensor.matmul(out[0:33, :], sil[:, k, :], chunk[:, j % WRING, k, :], start=(k == 0), stop=False)
                last.then_inc(s_chunk_used, 1)
                nc.tensor.matmul(out[0:33, :], ones[:, :], bmod[:, j * NC:(j + 1) * NC], start=False,
                                 stop=True).then_inc(s_fill1, 1)
            pe.wait_ge(s_const, 48)
            pe.wait_ge(s_kc, 16)
            out = bank1("keyT", "cache")
            for h in range(H):
                last = nc.tensor.transpose(out[:, h * P:(h + 1) * P], ktc[:, h * P:(h + 1) * P], ident[:, :])
            last.then_inc(s_fill1, 1)
            for b in range(NBLK):
                pe.wait_ge(s_h1, b + 1)
                for half in range(2):
                    out = bank1("hT", b, half)
                    for k in range(4):
                        last = nc.tensor.transpose(out[:, k * P:(k + 1) * P],
                                                   H1[:, b, (4 * half + k) * P:(4 * half + k + 1) * P], ident[:, :])
                    last.then_inc(s_fill1, 1)

            def z(c, b):
                i = MOD_CH + IN_ORDER[c]
                out = bank1("z", c, b)
                if b == 0:
                    chunk_ready(i)
                pe.wait_ge(s_act1, B1.emptied(B1.pos[("hT", b, 1)])[1])
                for k in range(KD):
                    last = nc.tensor.matmul(out, HT[:, k, b * P:(b + 1) * P], chunk[:, i % WRING, k, :],
                                            start=(k == 0), stop=(k == KD - 1))
                last.then_inc(s_fill1, 1)
                if b == NBLK - 1:
                    pe.wait_ge(s_fill1, B1.pos[("z", c, b)] + 1)
                    pe.nop().then_inc(s_chunk_used, 1)

            def headT(c, b):
                out = bank1("headT", c, b)
                who, n = B1.emptied(B1.pos[("z", c, b)])
                pe.wait_ge(s_act1 if who == "act" else s_dve1, n)
                for h in range(H):
                    last = nc.tensor.transpose(out[:, h * P:(h + 1) * P], heads[:, b % 2, h * P:(h + 1) * P], ident[:, :])
                last.then_inc(s_fill1, 1)

            for c in ("k", "q"):
                for b in range(NBLK):
                    z(c, b)
                    if b:
                        headT(c, b - 1)
                headT(c, NBLK - 1)
            for c in ("v", "f"):
                for b in range(NBLK):
                    z(c, b)

            pe.wait_ge(s_dft, 48)
            for m in range(2):
                nc.tensor.matmul(bank1("fold", m), dftC[:, 2 * m, :], wf, start=True, stop=True).then_inc(s_fill1, 1)
            units = [(s, g) for s in range(2) for g in range(4)]

            def fourier_pos(u):
                s, g = u
                for m, name in enumerate(("fcos", "fsin")):
                    out = bank1(name, s, g)
                    fcols = slice(g * P, (g + 1) * P)
                    if s == 0:
                        last = nc.tensor.matmul(out[:, 0:P], F[:, 0, fcols], dftC[:, m, :], start=True, stop=True)
                    else:
                        for b in range(NSMP):
                            last = nc.tensor.matmul(out, F[:, 1 + b, fcols], dftS[:, m, b, :], start=(b == 0), stop=(b == NSMP - 1))
                    last.then_inc(s_fill1, 1)

            def fourier_ch(u):
                s, g = u
                i = units.index(u)
                w = NC if s else P
                out = bank1("fmix", s, g)
                pe.wait_ge(s_act1, B1.emptied(B1.pos[("fcos", s, g)])[1])
                pe.wait_ge(s_dve1, B1.emptied(B1.pos[("fsin", s, g)])[1])
                nc.tensor.matmul(out[:, 0:w], fold[:, 0, g, :], fstage[:, i % 2, 0, 0:w], start=True, stop=False)
                nc.tensor.matmul(out[:, 0:w], fold[:, 1, g, :], fstage[:, i % 2, 1, 0:w], start=False, stop=True).then_inc(s_fill1, 1)

            pe.wait_ge(s_act1, B1.emptied(B1.pos[("z", "f", NBLK - 1)])[1])
            for i, u in enumerate(units):
                fourier_pos(u)
                if i:
                    fourier_ch(units[i - 1])
            fourier_ch(units[-1])

            pe.wait_ge(s_act1, B1.count("act"))
            pe.wait_ge(s_dve1, B1.count("dve"))
            pe.wait_ge(s_vc, 16)

            def scores(i):
                b, h = UNITS[i]
                for m in range(2):
                    if i:
                        pe.wait_ge(s_exp, 2 * (i - 1) + m + 1)
                        pe.wait_ge(s_amax, i)
                    part = slice(DH * m, DH * m + DH)
                    q = qT[part, h, b * P:(b + 1) * P]
                    if b == 0:
                        last = nc.tensor.matmul(ps[:, 2 * m, 0:P], q, kT[part, h, 0:P], start=True, stop=True)
                    else:
                        for z_ in range(2):
                            k0 = P + z_ * (KEYS_S // 2)
                            last = nc.tensor.matmul(ps[:, 2 * m + z_, 0:KEYS_S // 2], q, kT[part, h, k0:k0 + KEYS_S // 2],
                                                    start=True, stop=True)
                    last.then_inc(s_scores, 1)

            def products(i):
                b, h = UNITS[i]
                nk = 1 if b == 0 else 5
                pe.wait_ge(s_w, i + 1)
                if i:
                    pe.wait_ge(s_wTc, i)
                for s in range(nk):
                    last = nc.tensor.transpose(ps[:, 4 + s // 4, (s % 4) * P:(s % 4) * P + P],
                                               Wt[:, i % 2, s * P:(s + 1) * P], ident[:, :])
                last.then_inc(s_wT, 1)
                pe.wait_ge(s_wTc, i + 1)
                if h == 0 and b:
                    pe.wait_ge(s_att, b)
                for s in range(nk):
                    vb = 0 if b == 0 else 1 + s
                    last = nc.tensor.matmul(ps[:, 6, h * P:(h + 1) * P], WtT[:, i % 2, s, :], V[:, vb, h * P:(h + 1) * P],
                                            start=(s == 0), stop=(s == nk - 1))
                last.then_inc(s_pv, 1)

            def attT(b):
                pe.wait_ge(s_att, b + 1)
                if b:
                    pe.wait_ge(s_mix, b)
                for h in range(H):
                    last = nc.tensor.transpose(ps[:, 7, h * P:(h + 1) * P], att[:, h * P:(h + 1) * P], ident[:, :])
                last.then_inc(s_attT, 1)

            scores(0)
            for i in range(len(UNITS)):
                if i + 1 < len(UNITS):
                    scores(i + 1)
                if i % H == 0 and i:
                    attT(i // H - 1)
                products(i)
            attT(NBLK - 1)

            def bank2(*name):
                i = B2.pos[name]
                if i >= 4:
                    who, n = B2.emptied(i - 4)
                    pe.wait_ge(s_act2 if who == "act" else s_dve2, n)
                return ps[:, i % 4, :]

            pe.wait_ge(s_mix, NBLK)
            pe.wait_ge(s_exp, 2 * len(UNITS))
            chunk_ready(16)
            chunk_ready(17)
            for b in range(NBLK):
                for half in range(2):
                    out = bank2("merge", b, half)
                    for k in range(KD):
                        last = nc.tensor.matmul(out, mixT[:, k, b * P:(b + 1) * P], chunk[:, (16 + half) % WRING, k, :],
                                                start=(k == 0), stop=(k == KD - 1))
                    last.then_inc(s_fill2, 1)

            def front(b):
                pe.wait_ge(s_h2, b + 1)
                for half in range(2):
                    out = bank2("h2T", b, half)
                    for k in range(4):
                        last = nc.tensor.transpose(out[:, k * P:(k + 1) * P],
                                                   H2[:, b, (4 * half + k) * P:(4 * half + k + 1) * P], ident[:, :])
                    last.then_inc(s_fill2, 1)
                pe.wait_ge(s_wq, 16)
                pe.wait_ge(s_keys, 16)
                pe.wait_ge(s_act2, B2.emptied(B2.pos[("h2T", b, 1)])[1])
                for g in range(4):
                    out = bank2("query", b, g)
                    for j in range(4):
                        for k in range(KD):
                            c = (4 * g + j) * P
                            last = nc.tensor.matmul(out[:, j * P:(j + 1) * P], wq[:, k, c:c + P], h2T[:, b % 2, k, :],
                                                    start=(k == 0), stop=(k == KD - 1))
                    last.then_inc(s_fill2, 1)
                    out = bank2("score", b, g)
                    pe.wait_ge(s_act2, B2.emptied(B2.pos[("query", b, g)])[1])
                    for j in range(4):
                        last = nc.tensor.matmul(out[:, j * P:(j + 1) * P], qTq[:, j, :], keys[:, 4 * g + j, :],
                                                start=True, stop=True)
                    last.then_inc(s_fill2, 1)

            def sum_rows(b):
                a = 4 + 2 * (b % 2)

                def step(g, first, final):
                    for r in range(VR):
                        pe.wait_ge(s_diag, g * VR + r + 1)
                        pe.wait_ge(s_v[r], g * 16 + 16)
                        for z_ in range(2):
                            last = nc.tensor.matmul(ps[:, a + z_, :], diag[:, r, :], Vr[:, r, z_ * NC:(z_ + 1) * NC],
                                                    start=(first and r == 0), stop=(final and r == VR - 1),
                                                    skip_group_check=True)
                        last.then_inc(s_acc, 1)
                lo = b * (SLOTS // VR)
                hi = lo + SLOTS // VR
                if b >= 2:
                    pe.wait_ge(s_x2, b - 1)
                step(lo, True, False)
                with pe.Fori(lo + 1, hi - 1) as g:
                    step(g, False, False)
                step(hi - 1, False, True)

            front(0)
            for b in range(NBLK):
                if b + 1 < NBLK:
                    front(b + 1)
                sum_rows(b)


def _constants():
    ident = np.eye(P, dtype=np.float32)
    t = np.arange(NSMP * P)
    nf = DH // 4
    inv = (np.float32(10000.0) ** (-np.arange(nf, dtype=np.float32) / np.float32(nf))).astype(np.float32)
    ar = (t // 64).astype(np.float32)[:, None] * inv
    ac = (t % 64).astype(np.float32)[:, None] * inv
    ang = np.concatenate([ar, ar, ac, ac], -1)
    sign = np.concatenate([-np.ones(16), np.ones(16)] * 2).astype(np.float32)
    cos = np.cos(ang).astype(np.float32).reshape(NSMP, P, DH).transpose(1, 0, 2)
    sin = (np.sin(ang).astype(np.float32) * sign).reshape(NSMP, P, DH).transpose(1, 0, 2)

    def dft(n):
        a = 2 * np.pi * ((np.arange(n)[:, None] * np.arange(n)[None, :]) % n) / n
        return np.cos(a) / np.sqrt(n), np.sin(a) / np.sqrt(n)
    c5, s5 = dft(NSMP * P)
    seq = np.stack([c5, s5]).reshape(2, NSMP, P, NSMP * P).transpose(2, 0, 1, 3).astype(np.float32)
    c1, s1 = dft(P)
    ch = np.stack([c1, s1, -s1]).transpose(1, 0, 2).astype(np.float32)
    return [np.ascontiguousarray(a) for a in (ident, cos, sin, seq, ch)]


def kernel(**inputs):
    import concourse.bacc as bacc
    from concourse.bass_utils import run_bass_kernel_spmd

    g = {k: np.asarray(v) for k, v in inputs.items()}
    ident, cos, sin, seq, ch = _constants()
    arrays = {
        "xall": np.concatenate([g["x_prompt"].reshape(P, D), g["x_sample"].reshape(NSMP * P, D)]),
        "condT": np.stack([g["c_ctx"].reshape(D), g["c"].reshape(D)]).reshape(2, KD, P).transpose(2, 1, 0),
        "w_mod": g["w_mod"][0], "b_mod": g["b_mod"], "norm1_g": g["norm1_g"][0], "w_in": g["w_in"][0],
        "lam4": np.stack([g["lam_q1"][0], g["lam_q2"][0], g["lam_k1"][0], g["lam_k2"][0]]),
        "subln_g": g["subln_g"][0], "w_fourier": g["w_fourier"][0].transpose(1, 0, 2), "w_out": g["w_out"][0],
        "norm2_g": g["norm2_g"][0], "w_query": g["w_query"][0],
        "keysT": g["sub_keys"][0].transpose(3, 0, 1, 2).reshape(P, 16, NKEY),
        "expert_u": g["expert_u"][0], "expert_v": g["expert_v"][0], "final_g": g["final_g"],
        "cache_k": g["cache_k"].reshape(P, NC), "cache_v": g["cache_v"].reshape(P, NC),
        "ident": ident, "cos": cos, "sin": sin, "dft_seq": seq, "dft_ch": ch,
    }
    arrays = {k: np.ascontiguousarray(v) for k, v in arrays.items()}
    nc = bacc.Bacc("TRN2", target_bir_lowering=False, num_devices=1)
    f32 = mybir.dt.float32
    args = [nc.dram_tensor(f"in_{k}", v.shape, f32, kind="ExternalInput").ap() for k, v in arrays.items()]
    outs = {"y": (NBLK * P, D), "state_k": (P, NC), "state_v": (P, NC)}
    args += [nc.dram_tensor(f"out_{k}", s, f32, kind="ExternalOutput").ap() for k, s in outs.items()]
    program(nc, *args)
    r = run_bass_kernel_spmd(nc, [{f"in_{k}": v for k, v in arrays.items()}], core_ids=[0]).results[0]
    yy = r["out_y"]
    return (yy[:P].reshape(1, P, D), yy[P:].reshape(1, NSMP * P, D),
            r["out_state_k"].reshape(1, 1, P, H, 2 * DH), r["out_state_v"].reshape(1, 1, P, H, 2 * DH))
```

```python
import math
from contextlib import ExitStack

import numpy as np
import concourse.bass as bass
from concourse import mybir

ds = bass.ds

P = 128
D = 1024
KD = D // P
NBLK = 5
NSMP = 4
H = 4
DH = 64
NC = 512
MOD_CH = 12
IN_CH = 4
OUT_CH = 2
KEYS_S = 640
PH = 8
TOPK = 16
NKEY = 128
SLOTS = PH * TOPK
LAM_INIT = 0.8 - 0.6 * math.exp(-0.3 * 0)
EPS = 1e-6
NEG = -3.0e38
WRING = 3
NB1 = NKEY
GRP = 4
NGRP = NB1 // GRP
TS = NSMP * P
ROWS = 8
RR = 4


def _phase1_jobs():
    jobs = [(("mod", j), "act") for j in range(MOD_CH)]
    jobs.append((("keyT", "cache"), "act"))
    jobs += [(("hT", b, half), "act") for b in range(NBLK) for half in range(2)]
    for c in ("k", "q"):
        for b in range(NBLK):
            jobs.append((("z", c, b), "act" if b == 0 else "dve"))
            if b >= 1:
                jobs.append((("headT", c, b - 1), "act"))
        jobs.append((("headT", c, NBLK - 1), "act"))
    jobs += [(("z", c, b), "act") for c in ("v", "f") for b in range(NBLK)]
    jobs += [(("fold", 0), "act"), (("fold", 1), "dve")]
    units = [(s, g) for s in range(2) for g in range(4)]
    for i, u in enumerate(units):
        jobs += [(("fcos",) + u, "act"), (("fsin",) + u, "dve")]
        if i:
            jobs.append((("fmix",) + units[i - 1], "act"))
    jobs.append((("fmix",) + units[-1], "act"))
    return jobs


def _phase2_jobs():
    jobs = []
    for b in range(NBLK):
        jobs += [(("merge", b, half), "dve") for half in range(2)]
    for b in range(NBLK):
        jobs += [(("h2T", b, half), "act") for half in range(2)]
    for b in range(NBLK):
        for g in range(4):
            jobs += [(("query", b, g), "act"), (("score", b, g), "dve")]
        if b >= 2:
            jobs.append((("selT", b - 1), "act"))
    jobs.append((("selT", NBLK - 1), "act"))
    return jobs


class Banks:

    def __init__(self, jobs, nbanks):
        self.pos = {name: n for n, (name, _) in enumerate(jobs)}
        self.who = [w for _, w in jobs]
        self.nbanks = nbanks
        self.total = len(jobs)

    def emptied(self, n):
        return self.who[n], sum(w == self.who[n] for w in self.who[:n + 1])

    def count(self, who):
        return sum(w == who for w in self.who)


def program(nc, xall, condT, w_mod, b_mod, norm1_g, w_in, lam4, subln_g, w_fourier, w_out, norm2_g,
            w_query, keysT, expert_u, expert_uT, expert_v, final_g, cache_k, cache_v,
            ident_d, cos_d, sin_d, dft_seq_d, dft_ch_d, y, state_k, state_v):
    f32, u32, f32r = mybir.dt.float32, mybir.dt.uint32, mybir.dt.float32r
    ALU, ACT, AX = mybir.AluOpType, mybir.ActivationFunctionType, mybir.AxisListType
    B1, B2 = Banks(_phase1_jobs(), 8), Banks(_phase2_jobs(), 4)

    ctx = ExitStack()
    with ctx:
        def sb(name, shape, dt=f32):
            return ctx.enter_context(nc.sbuf_tensor(name, shape, dt))

        def sem(name):
            return ctx.enter_context(nc.semaphore(name))

        ident = sb("ident", [P, P])
        ones = sb("ones", [1, 33])
        lam = sb("lam", [P, 8])
        gsub = sb("gsub", [P, 1])
        powe = sb("powe", [P, 8])
        ss = sb("ss", [P, NBLK])
        rstd = sb("rstd", [P, NBLK])
        amax = sb("amax", [P, 2, 2])
        asum = sb("asum", [P, 2, 2])
        ss4 = sb("ss4", [P, 2, H])
        iota = sb("iota", [P, NKEY])
        idx = sb("idx", [P, SLOTS], u32)
        idxn = sb("idxn", [P, 2, 2], u32)
        gates = sb("gates", [P, 2, SLOTS])
        dots = sb("dots", [P, SLOTS])
        coef = sb("coef", [P, SLOTS])
        sel = sb("sel", [P, 2, SLOTS])
        gsum = sb("gsum", [P, 2, PH])

        XO, G2O, MO, BO, WO, CO = 0, 5120, 7168, 13312, 18432, 35840
        ARENA = 51200
        arena = sb("arena", [P, WO])
        with nc.sbuf_tensor("arena_w", [P, ARENA - WO], f32) as arena_w:
            pass

        def cutout(lo, n, rows=slice(0, P)):
            return arena[rows, lo:lo + n] if lo < WO else arena_w[rows, lo - WO:lo - WO + n]

        X = cutout(XO, 5120).rearrange("p (b d) -> p b d", b=NBLK)
        F = cutout(XO, 2560).rearrange("p (b n) -> p b n", b=NBLK)
        fstage = cutout(XO + 2560, 2048).rearrange("p (r m n) -> p r m n", r=2, m=2)
        dftC = cutout(XO + 4608, 384).rearrange("p (m n) -> p m n", m=3)
        Wt = cutout(XO, 1280).rearrange("p (r n) -> p r n", r=2)
        probs = cutout(XO + 2560, 1280).rearrange("p (m n) -> p m n", m=2)
        junk = cutout(BO, D)
        HT = cutout(BO, 5120).rearrange("p (k t) -> p k t", k=KD)
        H2 = cutout(BO, 5120).rearrange("p (b d) -> p b d", b=NBLK)
        chunk = cutout(WO, WRING * KD * NC).rearrange("p (r k n) -> p r k n", r=WRING, k=KD)
        H1 = cutout(WO + WRING * KD * NC, 5120).rearrange("p (b d) -> p b d", b=NBLK)
        mixT = cutout(WO + WRING * KD * NC, 5120).rearrange("p (k t) -> p k t", k=KD)
        G2 = cutout(G2O, 2048).rearrange("p (c d) -> p c d", c=2)
        M = cutout(MO, 6144).rearrange("p (c w d) -> p c w d", c=2, w=3)
        SC2, SH2, G1 = range(3)
        h2T = cutout(MO, 5120).rearrange("p (k t) -> p k t", k=KD)
        fing = cutout(MO + 5120, 1024)
        wq7 = cutout(BO + 1024, 2048)
        wq = cutout(CO, 7 * 2048).rearrange("p (k n) -> p k n", k=7)
        keys = cutout(BO + 3072, 2048).rearrange("p (g n) -> p g n", g=16)
        gbuf = cutout(WO, NKEY * P).rearrange("p (i t) -> p i t", i=NKEY)
        lhs1 = cutout(WO + 16384, 1024).rearrange("p (r t n) -> p r t n", r=2, t=4)
        rhs1 = cutout(CO + 14336, 1024).rearrange("p (r t n) -> p r t n", r=2, t=4)
        onehot = cutout(XO, 2048).rearrange("p (s j) -> p s j", j=TOPK)
        cand = cutout(XO + 2048, 256)
        rest = cutout(XO + 2304, 256).rearrange("p (w n) -> p w n", w=2)
        cand2 = cutout(XO + 2304, 256)
        idxf = cutout(XO + 2560, 256).rearrange("p (h w j) -> p h w j", h=PH, w=2)
        top = cutout(XO + 2816, 128).rearrange("p (h j) -> p h j", h=PH)
        posf = cutout(XO + 2944, 128)
        qTq = cutout(XO + 3072, 512).rearrange("p (g t) -> p g t", g=4)
        selT = cutout(XO + 3584, 768).rearrange("p (r w t) -> p r w t", r=2, w=3)
        best = cutout(XO + 4352, 256).rearrange("p (h w j) -> p h w j", h=PH, w=2)
        besti = cutout(XO + 4608, 256).bitcast(u32).rearrange("p (h w j) -> p h w j", h=PH, w=2)
        pos = cutout(XO + 4864, 128).bitcast(u32).rearrange("p (h j) -> p h j", h=PH)
        posb = cutout(XO + 4992, 128).bitcast(u32).rearrange("p (h j) -> p h j", h=PH)
        acc = cutout(XO, 4096).rearrange("p (b d) -> p b d", b=NSMP)
        acc0 = cutout(XO + 4096, 1024)
        XF = cutout(MO, 5120).rearrange("p (b d) -> p b d", b=NBLK)
        rowr = cutout(BO + 1024, RR * D).rearrange("p (r d) -> p r d", r=RR)

        hT_hi, hT_lo = sb("hT_hi", [P, KD, TS], f32r), sb("hT_lo", [P, KD, TS], f32r)
        U_hi, U_lo = sb("U_hi", [P, 2, KD, P], f32r), sb("U_lo", [P, 2, KD, P], f32r)
        U_in, V_in = sb("U_in", [P, 2, KD, P]), sb("V_in", [P, 2, D])
        V_hi, V_lo = sb("V_hi", [P, GRP, D], f32r), sb("V_lo", [P, GRP, D], f32r)
        C_hi, C_lo = sb("C_hi", [P, GRP, TS], f32r), sb("C_lo", [P, GRP, TS], f32r)
        gate_in = sb("gate_in", [P, GRP, TS])
        act_t = sb("act_t", [P, 2, TS])
        creg = cutout(CO, 15360)
        bmod = cutout(CO, 6144, slice(0, 1))
        gbc = creg[:, 6144:8192].rearrange("p (w d) -> p w d", w=2)
        rows = cutout(CO + 8192, 1024, slice(0, 33)).rearrange("p (r n) -> p r n", r=2)
        M1 = creg[:, 9216:13312].rearrange("p (c w d) -> p c w d", c=2, w=2)
        sil = creg[:, 13824:14088].rearrange("p (k c) -> p k c", k=KD)
        cond = creg[:, 14088:14104].rearrange("p (k c) -> p k c", k=KD)
        lamv = creg[:, 14104:14360].rearrange("p (w e) -> p w e", w=4)
        kT = creg[:, 0:3072].rearrange("p (h t) -> p h t", h=H)
        qT = creg[:, 3072:5632].rearrange("p (h t) -> p h t", h=H)
        V = creg[:, 5632:8704].rearrange("p (b n) -> p b n", b=6)
        WtT = creg[:, 8704:9984].rearrange("p (r s n) -> p r s n", r=2, s=5)
        ropet = creg[:, 9984:11008].rearrange("p (w n) -> p w n", w=2)
        heads = creg[:, 11008:12032].rearrange("p (r n) -> p r n", r=2)
        ropec = creg[:, 12032:12544].rearrange("p (w b e) -> p w b e", w=2, b=NSMP)
        ktc = creg[:, 13312:13824]
        att = creg[:, 12544:13056]
        fold = creg[:, 13824:14848].rearrange("p (m g n) -> p m g n", m=2, g=4)
        wf = creg[:, 14848:15360].rearrange("p (g n) -> p g n", g=4)

        x1_d = nc.dram_tensor("x1_scratch", (NBLK * P, D), f32, kind="Internal").ap()
        gates_d = nc.dram_tensor("gates_scratch", (NB1, P, TS), f32, kind="Internal").ap()

        ps = ctx.enter_context(nc.psum_tensor("ps", [P, 8, NC], f32))

        s_x = sem("s_x"); s_cond = sem("s_cond"); s_const = sem("s_const"); s_bmod = sem("s_bmod")
        s_gbc = sem("s_gbc"); s_kc = sem("s_kc"); s_vc = sem("s_vc"); s_rope = sem("s_rope")
        s_dft = sem("s_dft"); s_wf = sem("s_wf"); s_wq = sem("s_wq"); s_keys = sem("s_keys"); s_fing = sem("s_fing")
        s_chunk = [sem(f"s_chunk{i}") for i in range(WRING)]
        s_chunk_used = sem("s_chunk_used")
        s_xr = [sem(f"s_xr{b}") for b in range(NBLK)]
        s_out = sem("s_out")
        s_set = sem("s_set"); s_exps = sem("s_exps"); s_sil = sem("s_sil")
        s_lamsum = sem("s_lamsum"); s_lamexp = sem("s_lamexp"); s_lam = sem("s_lam")
        s_fill1 = sem("s_fill1"); s_act1 = sem("s_act1"); s_dve1 = sem("s_dve1")
        s_rows = sem("s_rows"); s_bc = sem("s_bc")
        s_sq1 = sem("s_sq1"); s_var1 = sem("s_var1"); s_rstd1 = sem("s_rstd1"); s_h1 = sem("s_h1"); s_mod2 = sem("s_mod2")
        s_head = sem("s_head")
        s_scores = sem("s_scores"); s_amax = sem("s_amax"); s_exp = sem("s_exp"); s_w = sem("s_w")
        s_wT = sem("s_wT"); s_wTc = sem("s_wTc"); s_pv = sem("s_pv"); s_asq = sem("s_asq"); s_avar = sem("s_avar")
        s_arstd = sem("s_arstd"); s_att = sem("s_att"); s_attT = sem("s_attT"); s_mix = sem("s_mix")
        s_fill2 = sem("s_fill2"); s_act2 = sem("s_act2"); s_dve2 = sem("s_dve2")
        s_x1 = sem("s_x1"); s_sq2 = sem("s_sq2"); s_var2 = sem("s_var2"); s_rstd2 = sem("s_rstd2"); s_h2 = sem("s_h2")
        s_top = sem("s_top"); s_gexp = sem("s_gexp"); s_idx = sem("s_idx"); s_gate = sem("s_gate")
        s_staged = sem("s_staged"); s_ix = sem("s_ix")
        s_spill = sem("s_spill"); s_xf = sem("s_xf"); s_wq7 = sem("s_wq7")
        s_sel = sem("s_sel"); s_selT = sem("s_selT"); s_lhs1 = sem("s_lhs1"); s_rhs1 = sem("s_rhs1")
        s_gq = sem("s_gq"); s_gev = sem("s_gev"); s_gout = sem("s_gout")
        s_hThi = sem("s_hThi"); s_hTlo = sem("s_hTlo"); s_acc0 = sem("s_acc0")
        s_uin = [sem(f"s_uin{i}") for i in range(2)]
        s_vin = [sem(f"s_vin{i}") for i in range(2)]
        s_gin = [sem(f"s_gin{i}") for i in range(4)]
        s_uhi = sem("s_uhi"); s_ulo = sem("s_ulo"); s_vhi = sem("s_vhi"); s_vlo = sem("s_vlo")
        s_a = sem("s_a"); s_ge = sem("s_ge"); s_c = sem("s_c"); s_chi = sem("s_chi"); s_clo = sem("s_clo")
        s_vb = sem("s_vb"); s_flush = sem("s_flush")
        s_row = [sem(f"s_row{i}") for i in range(RR)]
        s_used = sem("s_used"); s_gelu = sem("s_gelu"); s_coef = sem("s_coef")
        s_x2 = sem("s_x2"); s_sq3 = sem("s_sq3"); s_var3 = sem("s_var3"); s_rstd3 = sem("s_rstd3"); s_y = sem("s_y")
        s_step = sem("s_step"); s_accfree = sem("s_accfree"); s_setp = sem("s_setp")

        DFT_C = MOD_CH + IN_CH
        OUT_C = DFT_C + 1
        CHUNKS = OUT_C + OUT_CH
        IN_ORDER = {"k": 0, "q": 1, "v": 2, "f": 3}
        IN_COL = {"q": 0, "k": 1, "v": 2, "f": 3}
        w_mod_v = w_mod.rearrange("(k p) n -> p k n", p=P)
        w_in_v = w_in.rearrange("(k p) n -> p k n", p=P)
        w_out_v = w_out.rearrange("(k p) n -> p k n", p=P)
        dftS = chunk[:, DFT_C % WRING].rearrange("p (m s) n -> p m s n", m=2)
        w_query_v = w_query.rearrange("(k p) n -> p k n", p=P)
        UNITS = [(b, h) for b in range(NBLK) for h in range(H)]

        def seq(u):
            return 1 if u[0] else 0

        block = ctx.enter_context(nc.Block())

        @block.sync
        def _(sp):
            sp.dma_start(X, xall.rearrange("(b p) d -> p b d", p=P)).then_inc(s_x, 16)
            for i in range(CHUNKS):
                if i >= WRING:
                    sp.wait_ge(s_chunk_used, i - WRING + 1)
                if i < MOD_CH:
                    src = w_mod_v[:, :, i * NC:(i + 1) * NC]
                elif i < DFT_C:
                    c = [IN_COL[x] for x in ("k", "q", "v", "f")][i - MOD_CH]
                    src = w_in_v[:, :, c * NC:(c + 1) * NC]
                elif i == DFT_C:
                    src = dft_seq_d
                else:
                    c = i - OUT_C
                    src = w_out_v[:, :, c * NC:(c + 1) * NC]
                sp.dma_start(chunk[:, i % WRING], src).then_inc(s_chunk[i % WRING], 16)
                if i == WRING:
                    sp.wait_ge(s_h1, NBLK)
                    sp.dma_start(dftC, dft_ch_d).then_inc(s_dft, 16)
                    sp.dma_start(wf, w_fourier).then_inc(s_dft, 16)
            sp.wait_ge(s_wT, len(UNITS))
            for b in range(NBLK):
                sp.dma_start(X[:, b], xall[b * P:(b + 1) * P, :]).then_inc(s_xr[b], 16)
            sp.wait_ge(s_mix, NBLK)
            sp.wait_ge(s_out, 32)
            sp.dma_start(wq, w_query_v[:, 0:7, :]).then_inc(s_wq, 16)
            sp.wait_ge(s_x1, 2 * NBLK)
            sp.dma_start(x1_d.rearrange("(b p) d -> p b d", p=P), X).then_inc(s_spill, 16)
            sp.dma_start(fing, final_g.unsqueeze(0).broadcast_to([P, D])).then_inc(s_fing, 16)
            sp.wait_ge(s_fill2, B2.pos[("h2T", NBLK - 1, 1)] + 1)
            sp.dma_start(wq7, w_query_v[:, 7, :]).then_inc(s_wq7, 16)
            sp.dma_start(keys, keysT).then_inc(s_keys, 16)
            for b in range(1, NBLK):
                sp.wait_ge(s_gev, 32 * b)
                sp.dma_start(gates_d[:, :, (b - 1) * P:b * P].rearrange("i p t -> p i t"), gbuf).then_inc(s_gout, 16)

            def load(i, j, first):
                n = i * GRP + j
                r = j % 2
                if not (first and j < 2):
                    sp.wait_ge(s_ulo, n - 1)
                sp.dma_start(U_in[:, r], expert_uT[ds(n, 1)].rearrange("a p k n -> (a p) k n") if not isinstance(n, int)
                             else expert_uT[n]).then_inc(s_uin[r], 16)
                if not (first and j < 2):
                    sp.wait_ge(s_vlo, n - 1)
                sp.dma_start(V_in[:, r], expert_v[ds(n * P, P), :] if not isinstance(n, int)
                             else expert_v[n * P:(n + 1) * P, :]).then_inc(s_vin[r], 16)
                if not first:
                    sp.wait_ge(s_c, n - 3)
                sp.dma_start(gate_in[:, j], gates_d[ds(n, 1)].rearrange("a p t -> (a p) t") if not isinstance(n, int)
                             else gates_d[n]).then_inc(s_gin[j], 16)

            sp.wait_ge(s_gout, 16 * NSMP)
            sp.wait_ge(s_act2, B2.count("act"))
            for j in range(GRP):
                load(0, j, True)
            with sp.Fori(1, NGRP) as i:
                for j in range(GRP):
                    load(i, j, False)
            sp.wait_ge(s_hTlo, 1)
            sp.dma_start(XF, x1_d.rearrange("(b p) d -> p b d", p=P)).then_inc(s_xf, 16)
            for b in range(NBLK):
                sp.wait_ge(s_y, b + 1)
                sp.dma_start(y[b * P:(b + 1) * P, :], XF[:, b]).then_inc(s_out, 16)
            sp.wait_ge(s_out, 16 * (NBLK + 2))

        @block.gpsimd
        def _(pool):
            pool.iota(iota[:, :], pattern=[[1, NKEY]], base=0, channel_multiplier=0,
                      allow_small_or_imprecise_dtypes=True).then_inc(s_setp, 1)
            pool.memset(powe[:, :], -0.5).then_inc(s_setp, 1)
            pool.wait_ge(s_setp, 2)

            def spread_mod(j):
                pool.wait_ge(s_rows, j + 1)
                part, half = j // 2, j % 2
                cols = slice(half * NC, (half + 1) * NC)
                for c in range(2):
                    if part < 2:
                        dst = M1[:, c, 1 - part, cols]
                    else:
                        dst = G2[:, c, cols] if part == 5 else M[:, c, {2: G1, 3: SH2, 4: SC2}[part], cols]
                    pool.partition_broadcast(dst, rows[32 * c:32 * c + 1, j % 2, :], P).then_inc(s_bc, 1)

            for j in range(4):
                spread_mod(j)
            pool.wait_ge(s_bc, 8)
            pool.wait_ge(s_var1, 1)
            pool.tensor_tensor(rstd[:, :], ss[:, :], powe[:, 0:NBLK], ALU.pow).then_inc(s_rstd1, 1)
            pool.wait_ge(s_rstd1, 1)
            for j in range(4, MOD_CH):
                spread_mod(j)
            pool.wait_ge(s_bc, 2 * MOD_CH)
            for b in range(NBLK):
                pool.wait_ge(s_avar, b + 1)
                pool.tensor_tensor(ss4[:, 1, :], ss4[:, 0, :], powe[:, 0:H], ALU.pow).then_inc(s_arstd, 1)
            for b in range(NBLK):
                pool.wait_ge(s_var2, b + 1)
                pool.tensor_tensor(rstd[:, b:b + 1], ss[:, b:b + 1], powe[:, 0:1], ALU.pow).then_inc(s_rstd2, 1)

            def fetch(table, i, t, first, base):
                st = i * (ROWS // 2) + t
                if not first:
                    pool.wait_ge(s_used, 2 * st - 2)
                at = (i - base) * ROWS + 2 * t
                src = idx[:, ds(at, 2)] if not isinstance(i, int) else idx[:, at:at + 2]
                pool.tensor_copy(idxn[:, t % 2, :], src).then_inc(s_ix, 1)
                pool.wait_ge(s_ix, st + 1)
                pool.sem_inc(s_staged, 1)
                for r in range(2):
                    row = 2 * (t % 2) + r
                    pool.indirect_dma_start(
                        out=rowr[:, row, :], out_offset=None, in_=table,
                        in_offset=bass.IndirectOffsetOnAxis(ap=idxn[:, t % 2, r:r + 1], axis=0)
                    ).then_inc(s_row[row], 16)

            pool.wait_ge(s_idx, 1)
            pool.wait_ge(s_fill2, B2.total)
            for t in range(ROWS // 2):
                fetch(expert_u, 0, t, t < 2, 0)
            with pool.Fori(1, NGRP // 2) as i:
                for t in range(ROWS // 2):
                    fetch(expert_u, i, t, False, 0)
            with pool.Fori(NGRP // 2, NGRP) as i:
                for t in range(ROWS // 2):
                    fetch(expert_v, i, t, False, NGRP // 2)
            for b in range(NBLK):
                pool.wait_ge(s_var3, b + 1)
                pool.tensor_tensor(rstd[:, b:b + 1], ss[:, b:b + 1], powe[:, 0:1], ALU.pow).then_inc(s_rstd3, 1)

        @block.scalar
        def _(act):
            act.dma_start(cond[:, :, :], condT).then_inc(s_cond, 16)
            act.dma_start(bmod, b_mod).then_inc(s_bmod, 16)
            act.dma_start(ident[:, :], ident_d).then_inc(s_const, 16)
            act.dma_start(lamv[:, :, :], lam4.unsqueeze(0).broadcast_to([P, 4, DH])).then_inc(s_const, 16)
            act.dma_start(gsub[:, :], subln_g.unsqueeze(1)).then_inc(s_const, 16)
            act.dma_start(gbc[:, 0, :], norm1_g.unsqueeze(0).broadcast_to([P, D])).then_inc(s_gbc, 16)
            act.dma_start(gbc[:, 1, :], norm2_g.unsqueeze(0).broadcast_to([P, D])).then_inc(s_gbc, 16)
            act.dma_start(ktc, cache_k).then_inc(s_kc, 16)
            n = {"act": 0}

            def emptied1():
                return s_act1

            act.wait_ge(s_cond, 16)
            act.wait_ge(s_set, 1)
            act.activation(sil[:, :, 0:2], cond[:, :, :], ACT.Exp, scale=-1.0).then_inc(s_exps, 1)
            act.wait_ge(s_lamsum, 1)
            act.activation(lam[:, 2:4], lam[:, 0:2], ACT.Exp).then_inc(s_lamexp, 1)
            act.wait_ge(s_x, 16)
            for b in range(NBLK):
                if b:
                    act.wait_ge(s_sq1, b)
                act.activation(junk, X[:, b], ACT.Square, accum_out=ss[:, b:b + 1]).then_inc(s_sq1, 1)

            def bank1(*name):
                i = B1.pos[name]
                act.wait_ge(s_fill1, i + 1)
                return ps[:, i % 8, :]

            for j in range(MOD_CH):
                src = bank1("mod", j)
                if j >= 2:
                    act.wait_ge(s_bc, 2 * (j - 1))
                act.copy(rows[0:33, j % 2, :], src[0:33, :]).then_inc(s_rows, 1)
                act.wait_ge(s_rows, j + 1)
                act.nop().then_inc(s_act1, 1)

            def heads_out(name, dst):
                act.copy(dst, bank1(*name).rearrange("p (h t) -> p h t", h=H)).then_inc(s_act1, 1)

            act.wait_ge(s_mod2, 1)
            act.wait_ge(s_h1, NBLK)
            act.dma_start(ropec[:, 0], cos_d).then_inc(s_rope, 16)
            act.dma_start(ropec[:, 1], sin_d).then_inc(s_rope, 16)
            act.dma_start(V[:, 1, :], cache_v).then_inc(s_vc, 16)
            heads_out(("keyT", "cache"), kT[:, :, P:2 * P])
            for b in range(NBLK):
                for half in range(2):
                    src = bank1("hT", b, half).rearrange("p (k t) -> p k t", k=4)
                    act.copy(HT[:, 4 * half:4 * half + 4, b * P:(b + 1) * P], src).then_inc(s_act1, 1)
            for ci, c in enumerate(("k", "q")):
                for b in range(NBLK):
                    if b == 0:
                        if ci:
                            act.wait_ge(s_fill1, B1.pos[("headT", "k", NBLK - 1)] + 1)
                            act.wait_ge(s_out, 16)
                        act.copy(heads[:, 0, :], bank1("z", c, 0)).then_inc(s_act1, 1)
                        if ci == 0:
                            act.wait_ge(s_act1, B1.emptied(B1.pos[("z", "k", 0)])[1])
                            act.dma_start(state_k, heads[:, 0, :]).then_inc(s_out, 16)
                    else:
                        dst = kT if c == "k" else qT
                        at = (b - 1) * P if c == "q" or b == 1 else b * P
                        heads_out(("headT", c, b - 1), dst[:, :, at:at + P])
                dst, at = (kT, 5 * P) if c == "k" else (qT, 4 * P)
                heads_out(("headT", c, NBLK - 1), dst[:, :, at:at + P])
            for b in range(NBLK):
                vb = 0 if b == 0 else b + 1
                act.copy(V[:, vb, :], bank1("z", "v", b)).then_inc(s_act1, 1)
                if b == 0:
                    act.wait_ge(s_act1, B1.emptied(B1.pos[("z", "v", 0)])[1])
                    act.dma_start(state_v, V[:, 0, :]).then_inc(s_out, 16)
            for b in range(NBLK):
                act.copy(F[:, b, :], bank1("z", "f", b)).then_inc(s_act1, 1)
            act.copy(fold[:, 0], bank1("fold", 0).rearrange("p (g n) -> p g n", g=4)).then_inc(s_act1, 1)
            units = [(s, g) for s in range(2) for g in range(4)]

            def mix_out(u):
                s, g = u
                src = bank1("fmix", s, g)
                if s == 0:
                    act.copy(mixT[:, 4 + g, 0:P], src[:, 0:P]).then_inc(s_act1, 1)
                else:
                    act.copy(mixT[:, 4 + g, P:NBLK * P], src).then_inc(s_act1, 1)

            for i, u in enumerate(units):
                w = NC if u[0] else P
                src = bank1("fcos", *u)
                act.copy(fstage[:, i % 2, 0, 0:w], src[:, 0:w]).then_inc(s_act1, 1)
                if i:
                    mix_out(units[i - 1])
            mix_out(units[-1])

            def keys_of(b):
                return P if b == 0 else KEYS_S // 2

            def exps(i):
                b, h = UNITS[i]
                for m in range(2):
                    act.wait_ge(s_scores, 2 * i + m + 1)
                    act.wait_ge(s_amax, i + 1)
                    if i >= 1:
                        act.wait_ge(s_w, i)
                    n_ = keys_of(b)
                    src = ps[:, 2 * m:2 * m + (1 if b == 0 else 2), 0:n_]
                    dst = probs[:, m, 0:(1 if b == 0 else 2) * n_].rearrange("p (z n) -> p z n", n=n_)
                    act.activation(dst, src, ACT.Exp, bias=amax[:, i % 2, m:m + 1], scale=DH ** -0.5,
                                   accum_out=asum[:, i % 2, m:m + 1]).then_inc(s_exp, 1)

            def weights_out(i):
                b, h = UNITS[i]
                act.wait_ge(s_wT, i + 1)
                if i >= 2:
                    act.wait_ge(s_pv, i - 1)
                if b == 0:
                    act.copy(WtT[:, i % 2, 0, :], ps[:, 4, 0:P]).then_inc(s_wTc, 1)
                else:
                    act.copy(WtT[:, i % 2, 0:4, :], ps[:, 4, :].rearrange("p (s n) -> p s n", s=4))
                    act.copy(WtT[:, i % 2, 4, :], ps[:, 5, 0:P]).then_inc(s_wTc, 1)

            def att_squares(b):
                act.wait_ge(s_pv, H * (b + 1))
                if b:
                    act.wait_ge(s_attT, b)
                for h in range(H):
                    ins = act.activation(att[:, h * P:(h + 1) * P], ps[:, 6, h * P:(h + 1) * P], ACT.Square,
                                         accum_out=ss4[:, 0, h:h + 1])
                ins.then_inc(s_asq, 1)

            def att_out(b):
                act.wait_ge(s_attT, b + 1)
                act.activation(mixT[:, 0:4, b * P:(b + 1) * P], ps[:, 7, :].rearrange("p (h t) -> p h t", h=H),
                               ACT.Copy, scale=lam[:, 7:8]).then_inc(s_mix, 1)

            act.wait_ge(s_lam, 1)
            for i in range(len(UNITS) + 1):
                if i < len(UNITS):
                    exps(i)
                if i >= 1:
                    weights_out(i - 1)
                    if i % H == 0:
                        att_squares(i // H - 1)
                if i % H == 1 and i > H:
                    att_out(i // H - 1)
            att_out(NBLK - 1)

            for b in range(NBLK):
                act.wait_ge(s_x1, 2 * (b + 1))
                act.activation(H2[:, b], X[:, b], ACT.Square, accum_out=ss[:, b:b + 1]).then_inc(s_sq2, 1)

            def bank2(*name):
                i = B2.pos[name]
                act.wait_ge(s_fill2, i + 1)
                return ps[:, i % 4, :]

            act.wait_ge(s_h2, NBLK)
            for b in range(NBLK):
                for half in range(2):
                    src = bank2("h2T", b, half).rearrange("p (k t) -> p k t", k=4)
                    act.copy(h2T[:, 4 * half:4 * half + 4, b * P:(b + 1) * P], src).then_inc(s_act2, 1)

            def gates_out(b):
                act.copy(selT[:, b % 2], bank2("selT", b)[:, 0:3 * P].rearrange("p (w t) -> p w t", w=3)).then_inc(s_act2, 1)
                act.wait_ge(s_act2, B2.emptied(B2.pos[("selT", b)])[1])
                act.nop().then_inc(s_selT, 1)
                if b >= 2:
                    act.wait_ge(s_gout, 16 * (b - 1))
                with act.Fori(0, 16) as it:
                    for u in range(2):
                        act.wait_ge(s_gq, (b - 1) * 32 + it * 2 + u + 1)
                        act.copy(gbuf[:, :, ds(it * 8 + 4 * u, 4)],
                                 ps[:, 4 + u, :].rearrange("p (t n) -> p n t", t=4)).then_inc(s_gev, 1)

            act.wait_ge(s_spill, 16)
            for b in range(NBLK):
                for g in range(4):
                    act.copy(qTq, bank2("query", b, g).rearrange("p (g t) -> p g t", g=4)).then_inc(s_act2, 1)
                act.wait_ge(s_top, b + 1)
                act.activation(top[:, :, :], top[:, :, :], ACT.Exp).then_inc(s_gexp, 1)
                if b >= 2:
                    gates_out(b - 1)
            gates_out(NBLK - 1)

            act.wait_ge(s_gout, 16 * NSMP)
            act.copy(hT_hi[:, :, :], h2T[:, :, P:]).then_inc(s_hThi, 1)

            def split_u(n, r, k, first):
                act.wait_ge(s_uin[r], k)
                if not first:
                    act.wait_ge(s_a, n - 1)
                act.copy(U_hi[:, r], U_in[:, r]).then_inc(s_uhi, 1)

            def experts(i, first, last):
                for j in range(GRP):
                    n = i * GRP + j
                    if not (last and j == GRP - 1):
                        split_u(n + 1, (j + 1) % 2, 16 * (i * 2 + (j + 1) // 2 + 1), first and j == 0)
                    act.wait_ge(s_vin[j % 2], 16 * (i * 2 + j // 2 + 1))
                    if not first:
                        act.wait_ge(s_vb, 8 * i)
                    act.copy(V_hi[:, j], V_in[:, j % 2]).then_inc(s_vhi, 1)
                    act.wait_ge(s_a, n + 1)
                    if not (first and j < 2):
                        act.wait_ge(s_clo, n - 1)
                    act.activation(act_t[:, j % 2], ps[:, j % 2, :], ACT.Gelu).then_inc(s_ge, 1)
                    act.wait_ge(s_c, n + 1)
                    act.copy(C_hi[:, j], act_t[:, j % 2]).then_inc(s_chi, 1)

            split_u(0, 0, 16, True)
            experts(0, True, False)
            with act.Fori(1, NGRP // 2) as i:
                experts(i, False, False)
            act.wait_ge(s_used, SLOTS)
            act.activation(dots[:, :], dots[:, :], ACT.Gelu).then_inc(s_gelu, 1)
            with act.Fori(NGRP // 2, NGRP - 1) as i:
                experts(i, False, False)
            experts(NGRP - 1, False, True)
            for b in range(NBLK):
                act.wait_ge(s_x2, b + 1)
                act.activation(acc0 if b == 0 else acc[:, b - 1], XF[:, b], ACT.Square, accum_out=ss[:, b:b + 1]).then_inc(s_sq3, 1)

        @block.vector
        def _(dve):
            steps = [0]

            def link(ins):
                steps[0] += 1
                ins.then_inc(s_step, 1)
                dve.wait_ge(s_step, steps[0])

            link(dve.memset(sil[:, :, :], 0.0))
            dve.memset(ones[:, :], 1.0).then_inc(s_set, 1)
            dve.wait_ge(s_const, 48)
            link(dve.tensor_tensor(lamv[:, 0:2, :], lamv[:, 0:2, :], lamv[:, 2:4, :], ALU.mult))
            dve.tensor_reduce(lam[:, 0:2], lamv[:, 0:2, :], AX.X, ALU.add).then_inc(s_lamsum, 1)
            dve.wait_ge(s_exps, 1)
            link(dve.tensor_scalar(sil[:, :, 0:2], sil[:, :, 0:2], 1.0, None, ALU.add))
            link(dve.reciprocal(sil[:, :, 0:2], sil[:, :, 0:2]))
            link(dve.tensor_tensor(cond[:, :, :], cond[:, :, :], sil[:, :, 0:2], ALU.mult))
            link(dve.memset(sil[:, :, 0:2], 0.0))
            link(dve.tensor_copy(sil[:, :, 0:1], cond[:, :, 0:1]))
            dve.tensor_copy(sil[:, :, 32:33], cond[:, :, 1:2]).then_inc(s_sil, 1)
            dve.wait_ge(s_lamexp, 1)
            link(dve.tensor_tensor(lam[:, 4:5], lam[:, 3:4], lam[:, 2:3], ALU.subtract))
            link(dve.tensor_scalar(lam[:, 5:6], lam[:, 4:5], -LAM_INIT, None, ALU.add))
            dve.tensor_scalar(lam[:, 7:8], gsub[:, :], 1.0 - LAM_INIT, None, ALU.mult).then_inc(s_lam, 1)
            dve.wait_ge(s_sq1, NBLK)
            dve.tensor_scalar(ss[:, :], ss[:, :], 1.0 / D, EPS, ALU.mult, ALU.add).then_inc(s_var1, 1)
            dve.wait_ge(s_bc, 8)
            dve.wait_ge(s_gbc, 32)
            for c in range(2):
                link(dve.scalar_tensor_tensor(out=M1[:, c, 0, :], in0=M1[:, c, 0, :], scalar=1.0,
                                              in1=gbc[:, 0, :], op0=ALU.add, op1=ALU.mult))
            dve.wait_ge(s_rstd1, 1)
            for b in range(NBLK):
                c = min(b, 1)
                link(dve.scalar_tensor_tensor(out=H1[:, b], in0=X[:, b], scalar=rstd[:, b:b + 1],
                                              in1=M1[:, c, 0, :], op0=ALU.mult, op1=ALU.mult))
                dve.tensor_tensor(H1[:, b], H1[:, b], M1[:, c, 1, :], ALU.add).then_inc(s_h1, 1)
            dve.wait_ge(s_bc, 2 * MOD_CH)
            for c in range(2):
                link(dve.scalar_tensor_tensor(out=M[:, c, SC2, :], in0=M[:, c, SC2, :], scalar=1.0,
                                              in1=gbc[:, 1, :], op0=ALU.add, op1=ALU.mult))
            dve.nop().then_inc(s_mod2, 1)

            def bank1(*name):
                i = B1.pos[name]
                dve.wait_ge(s_fill1, i + 1)
                return ps[:, i % 8, :]

            def rope(c, b, count):
                z = bank1("z", c, b)
                if b >= 2:
                    dve.wait_ge(s_fill1, B1.pos[("headT", c, b - 2)] + 1)
                elif c == "q":
                    dve.wait_ge(s_fill1, B1.pos[("headT", "k", 3)] + 1)
                if count:
                    dve.wait_ge(s_dve1, count)
                out = heads[:, b % 2, :]
                zg = z.rearrange("p (g e) -> p g e", g=8)
                zs = z.rearrange("p (g w e) -> p g w e", g=16, w=2)
                t0 = ropet[:, 0, :].rearrange("p (g e) -> p g e", g=8)
                t1 = ropet[:, 1, :].rearrange("p (g u w e) -> p g u w e", g=8, u=2, w=2)
                zu = z.rearrange("p (g u w e) -> p g u w e", g=8, u=2, w=2)
                cos = ropec[:, 0, b - 1, :].unsqueeze(1).broadcast_to([P, 8, DH])
                sin = ropec[:, 1, b - 1, :].rearrange("p (u w e) -> p u w e", u=2, w=2)
                dve.tensor_tensor(t0, zg, cos, ALU.mult)
                for w in range(2):
                    sw = sin[:, :, w, :].unsqueeze(1).broadcast_to([P, 8, 2, 16])
                    ins = dve.tensor_tensor(t1[:, :, :, w, :], zu[:, :, :, 1 - w, :], sw, ALU.mult)
                steps[0] += 1
                ins.then_inc(s_step, 1)
                dve.wait_ge(s_step, steps[0])
                dve.tensor_tensor(out, ropet[:, 0, :], ropet[:, 1, :], ALU.add).then_inc(s_dve1, 1)

            dve.wait_ge(s_rope, 32)
            count = 0
            for c in ("k", "q"):
                for b in range(1, NBLK):
                    if b == 2 and c == "k":
                        dve.wait_ge(s_out, 16)
                    rope(c, b, count)
                    count += 1
            dve.tensor_copy(fold[:, 1], bank1("fold", 1).rearrange("p (g n) -> p g n", g=4)).then_inc(s_dve1, 1)
            units = [(s, g) for s in range(2) for g in range(4)]
            for i, u in enumerate(units):
                w = NC if u[0] else P
                src = bank1("fsin", *u)
                if i >= 2:
                    dve.wait_ge(s_fill1, B1.pos[("fmix",) + units[i - 2]] + 1)
                dve.tensor_copy(fstage[:, i % 2, 1, 0:w], src[:, 0:w]).then_inc(s_dve1, 1)

            dve.wait_ge(s_lam, 1)

            def neg_max(i):
                b, h = UNITS[i]
                dve.wait_ge(s_scores, 2 * i + 2)
                if i >= 2:
                    dve.wait_ge(s_exp, 2 * (i - 1))
                z, n_ = (1, P) if b == 0 else (2, KEYS_S // 2)
                src = ps[:, 0:4, :].rearrange("p (m z) n -> p m z n", m=2)[:, :, 0:z, 0:n_]
                link(dve.tensor_reduce(amax[:, i % 2, :], src, AX.XY, ALU.max, negate=True))
                dve.tensor_scalar(amax[:, i % 2, :], amax[:, i % 2, :], DH ** -0.5, None, ALU.mult).then_inc(s_amax, 1)

            def combine(i):
                b, h = UNITS[i]
                n_ = P if b == 0 else KEYS_S
                dve.wait_ge(s_exp, 2 * i + 2)
                link(dve.reciprocal(asum[:, i % 2, :], asum[:, i % 2, :]))
                dve.tensor_tensor(asum[:, i % 2, 1:2], asum[:, i % 2, 1:2], lam[:, 5:6], ALU.mult)
                if i >= 2:
                    dve.wait_ge(s_wT, i - 1)
                link(dve.tensor_scalar(Wt[:, i % 2, 0:n_], probs[:, 0, 0:n_], asum[:, i % 2, 0:1], None, ALU.mult))
                dve.scalar_tensor_tensor(out=Wt[:, i % 2, 0:n_], in0=probs[:, 1, 0:n_], scalar=asum[:, i % 2, 1:2],
                                         in1=Wt[:, i % 2, 0:n_], op0=ALU.mult, op1=ALU.add).then_inc(s_w, 1)

            def att_norm(b):
                dve.wait_ge(s_asq, b + 1)
                dve.tensor_scalar(ss4[:, 0, :], ss4[:, 0, :], 1.0 / P, EPS, ALU.mult, ALU.add).then_inc(s_avar, 1)
                dve.wait_ge(s_arstd, b + 1)
                dve.tensor_tensor(att.rearrange("p (h e) -> p h e", h=H), ps[:, 6, :].rearrange("p (h e) -> p h e", h=H),
                                  ss4[:, 1, :].unsqueeze(2).broadcast_to([P, H, P]), ALU.mult).then_inc(s_att, 1)

            for i in range(len(UNITS)):
                neg_max(i)
                if i:
                    pass
                combine(i)
                if i % H == 0 and i:
                    att_norm(i // H - 1)
            att_norm(NBLK - 1)

            def bank2(*name):
                i = B2.pos[name]
                dve.wait_ge(s_fill2, i + 1)
                return ps[:, i % 4, :]

            for b in range(NBLK):
                c = min(b, 1)
                dve.wait_ge(s_xr[b], 16)
                for half in range(2):
                    cols = slice(half * NC, (half + 1) * NC)
                    src = bank2("merge", b, half)
                    dve.tensor_tensor(H2[:, b, cols], src, M[:, c, G1, cols], ALU.mult).then_inc(s_dve2, 1)
                    dve.wait_ge(s_dve2, B2.emptied(B2.pos[("merge", b, half)])[1])
                    dve.tensor_tensor(X[:, b, cols], X[:, b, cols], H2[:, b, cols], ALU.add).then_inc(s_x1, 1)
            for b in range(NBLK):
                c = min(b, 1)
                dve.wait_ge(s_sq2, b + 1)
                dve.tensor_scalar(ss[:, b:b + 1], ss[:, b:b + 1], 1.0 / D, EPS, ALU.mult, ALU.add).then_inc(s_var2, 1)
                dve.wait_ge(s_rstd2, b + 1)
                link(dve.scalar_tensor_tensor(out=H2[:, b], in0=X[:, b], scalar=rstd[:, b:b + 1],
                                              in1=M[:, c, SC2, :], op0=ALU.mult, op1=ALU.mult))
                dve.tensor_tensor(H2[:, b], H2[:, b], M[:, c, SH2, :], ALU.add).then_inc(s_h2, 1)

            def retrieve(b):
                for g in range(4):
                    bank = bank2("score", b, g).rearrange("p (h w n) -> p h w n", h=2, w=2)
                    for hh in range(2):
                        h = 2 * g + hh
                        for w in range(2):
                            s = bank[:, hh, w, :]
                            link(dve.max(best[:, h, w, 0:8], s))
                            dve.max_index(besti[:, h, w, 0:8], best[:, h, w, 0:8], s)
                            link(dve.match_replace(rest[:, w, :], best[:, h, w, 0:8], s, NEG))
                        for w in range(2):
                            link(dve.max(best[:, h, w, 8:16], rest[:, w, :]))
                            ins = dve.max_index(besti[:, h, w, 8:16], best[:, h, w, 8:16], rest[:, w, :])
                        if hh == 1:
                            ins.then_inc(s_dve2, 1)
                        c3 = cand.rearrange("p (i j) -> p i j", i=TOPK)
                        link(dve.tensor_tensor(c3, best[:, h, 0, :].unsqueeze(2).broadcast_to([P, TOPK, TOPK]),
                                               best[:, h, 1, :].unsqueeze(1).broadcast_to([P, TOPK, TOPK]), ALU.add))
                        link(dve.max(top[:, h, 0:8], cand))
                        dve.max_index(pos[:, h, 0:8], top[:, h, 0:8], cand)
                        link(dve.match_replace(cand2, top[:, h, 0:8], cand, NEG))
                        link(dve.max(top[:, h, 8:16], cand2))
                        link(dve.max_index(pos[:, h, 8:16], top[:, h, 8:16], cand2))
                link(dve.tensor_copy(gsum[:, 1, :], top[:, :, 0]))
                dve.tensor_tensor(top[:, :, :], top[:, :, :],
                                  gsum[:, 1, :].unsqueeze(2).broadcast_to([P, PH, TOPK]),
                                  ALU.subtract).then_inc(s_top, 1)
                link(dve.tensor_copy(idxf.rearrange("p h w j -> p (h w j)"), besti[:, :, :, :].rearrange("p h w j -> p (h w j)")))
                link(dve.tensor_scalar(posb[:, :, :], pos[:, :, :], 4, None, ALU.logical_shift_right))
                link(dve.tensor_scalar(pos[:, :, :], pos[:, :, :], 15, None, ALU.bitwise_and))
                if b == 1:
                    dve.wait_ge(s_idx, 1)
                if b >= 2:
                    dve.wait_ge(s_fill2, B2.pos[("selT", b - 1)] + 1)
                for w, source in ((0, posb), (1, pos)):
                    link(dve.tensor_copy(posf[:, :], source[:, :, :].rearrange("p h j -> p (h j)")))
                    link(dve.tensor_tensor(onehot, posf[:, :].unsqueeze(2).broadcast_to([P, SLOTS, TOPK]),
                                           iota[:, 0:TOPK].unsqueeze(1).broadcast_to([P, SLOTS, TOPK]), ALU.is_equal))
                    o4 = onehot.rearrange("p (h s) j -> p h s j", h=PH)
                    link(dve.tensor_tensor(o4, o4, idxf[:, :, w, :].unsqueeze(2).broadcast_to([P, PH, TOPK, TOPK]), ALU.mult))
                    link(dve.tensor_reduce(sel[:, w, :], onehot, AX.X, ALU.add))
                if b == 0:
                    dve.scalar_tensor_tensor(out=idx[:, :], in0=sel[:, 0, :], scalar=float(NKEY), in1=sel[:, 1, :],
                                             op0=ALU.mult, op1=ALU.add).then_inc(s_idx, 1)

            def gate_weights(b):
                dve.wait_ge(s_gexp, b + 1)
                link(dve.tensor_reduce(gsum[:, 0, :], top[:, :, :], AX.X, ALU.add))
                link(dve.reciprocal(gsum[:, 0, :], gsum[:, 0, :]))
                dve.tensor_tensor(gates[:, min(b, 1), :].rearrange("p (h j) -> p h j", h=PH), top[:, :, :],
                                  gsum[:, 0, :].unsqueeze(2).broadcast_to([P, PH, TOPK]), ALU.mult).then_inc(s_gate, 1)

            def key_gates(b, it, u, first):
                q = (b - 1) * 32 + it * 2 + u
                if not first:
                    dve.wait_ge(s_gq, q - 1)
                at = it * 8 + 4 * u
                part = slice(at, at + 4) if isinstance(at, int) else ds(at, 4)
                dve.tensor_tensor(lhs1[:, u], iota[:, :].unsqueeze(1).broadcast_to([P, 4, NKEY]),
                                  selT[:, b % 2, 1, part].unsqueeze(2).broadcast_to([P, 4, NKEY]),
                                  ALU.is_equal).then_inc(s_lhs1, 1)
                for t in range(4):
                    one = slice(at + t, at + t + 1) if isinstance(at, int) else ds(at + t, 1)
                    ins = dve.tensor_scalar(rhs1[:, u, t, :], iota[:, :], selT[:, b % 2, 0, one],
                                            selT[:, b % 2, 2, one], ALU.is_equal, ALU.mult)
                ins.then_inc(s_rhs1, 1)

            def gate_rows(b):
                dve.wait_ge(s_selT, b)
                if b == 1:
                    for u in range(2):
                        key_gates(b, 0, u, True)
                with dve.Fori(1 if b == 1 else 0, 16) as it:
                    for u in range(2):
                        key_gates(b, it, u, False)

            dve.wait_ge(s_out, 32)
            dve.wait_ge(s_spill, 16)
            for b in range(NBLK):
                retrieve(b)
                gate_weights(b)
                if b >= 2:
                    gate_rows(b - 1)
            gate_rows(NBLK - 1)

            dve.wait_ge(s_hThi, 1)
            dve.tensor_tensor(hT_lo[:, :, :], h2T[:, :, P:], hT_hi[:, :, :].bitcast(f32), ALU.subtract).then_inc(s_hTlo, 1)
            dve.wait_ge(s_act2, B2.count("act"))
            dve.wait_ge(s_gq, 32 * NSMP)
            dve.memset(cutout(XO, 5120), 0.0).then_inc(s_acc0, 1)
            dve.wait_ge(s_acc0, 1)

            def split_u(n, r, first):
                dve.wait_ge(s_uhi, n + 1)
                dve.tensor_tensor(U_lo[:, r], U_in[:, r], U_hi[:, r].bitcast(f32), ALU.subtract).then_inc(s_ulo, 1)

            def experts(i, first, last, prompt_row):
                for j in range(GRP):
                    n = i * GRP + j
                    if not (last and j == GRP - 1):
                        split_u(n + 1, (j + 1) % 2, False)
                    dve.wait_ge(s_vhi, n + 1)
                    dve.tensor_tensor(V_lo[:, j], V_in[:, j % 2], V_hi[:, j].bitcast(f32), ALU.subtract).then_inc(s_vlo, 1)
                    dve.wait_ge(s_gin[j], 16 * (i + 1))
                    dve.wait_ge(s_ge, n + 1)
                    dve.tensor_tensor(act_t[:, j % 2], act_t[:, j % 2], gate_in[:, j], ALU.mult).then_inc(s_c, 1)
                    dve.wait_ge(s_chi, n + 1)
                    dve.tensor_tensor(C_lo[:, j], act_t[:, j % 2], C_hi[:, j].bitcast(f32), ALU.subtract).then_inc(s_clo, 1)
                for q in range(8):
                    prompt_row(i, q)
                    dve.wait_ge(s_vb, 8 * i + q + 1)
                    part = acc[:, q // 2, (q % 2) * NC:(q % 2 + 1) * NC]
                    dve.tensor_tensor(part, part, ps[:, 4 + q % 4, :], ALU.add).then_inc(s_flush, 1)

            def dot_row(i, q):
                r = q % RR
                dve.wait_ge(s_row[r], 16 * (2 * i + q // RR + 1))
                at = i * ROWS + q
                dst = dots[:, at:at + 1] if isinstance(at, int) else dots[:, ds(at, 1)]
                dve.scalar_tensor_tensor(out=rowr[:, r, :], in0=rowr[:, r, :], scalar=1.0, in1=H2[:, 0],
                                         op0=ALU.mult, op1=ALU.mult, accum_out=dst).then_inc(s_used, 1)

            def add_row(i, q):
                r = q % RR
                dve.wait_ge(s_row[r], 16 * (2 * i + q // RR + 1))
                dve.wait_ge(s_used, i * ROWS + q)
                at = (i - NGRP // 2) * ROWS + q
                c = coef[:, at:at + 1] if isinstance(at, int) else coef[:, ds(at, 1)]
                dve.scalar_tensor_tensor(out=acc0, in0=rowr[:, r, :], scalar=c, in1=acc0,
                                         op0=ALU.mult, op1=ALU.add).then_inc(s_used, 1)

            split_u(0, 0, True)
            experts(0, True, False, dot_row)
            with dve.Fori(1, NGRP // 2) as i:
                experts(i, False, False, dot_row)
            dve.wait_ge(s_gelu, 1)
            dve.tensor_tensor(coef[:, :], dots[:, :], gates[:, 0, :], ALU.mult).then_inc(s_coef, 1)
            dve.wait_ge(s_coef, 1)
            with dve.Fori(NGRP // 2, NGRP - 1) as i:
                experts(i, False, False, add_row)
            experts(NGRP - 1, False, True, add_row)

            dve.wait_ge(s_xf, 16)
            dve.wait_ge(s_flush, 8 * NGRP)
            dve.wait_ge(s_used, 2 * SLOTS)
            for b in range(NBLK):
                a = acc0 if b == 0 else acc[:, b - 1]
                link(dve.tensor_tensor(a, a, G2[:, min(b, 1), :], ALU.mult))
                dve.tensor_tensor(XF[:, b], XF[:, b], a, ALU.add).then_inc(s_x2, 1)
            dve.wait_ge(s_fing, 16)
            for b in range(NBLK):
                dve.wait_ge(s_sq3, b + 1)
                dve.tensor_scalar(ss[:, b:b + 1], ss[:, b:b + 1], 1.0 / D, EPS, ALU.mult, ALU.add).then_inc(s_var3, 1)
                dve.wait_ge(s_rstd3, b + 1)
                dve.scalar_tensor_tensor(out=XF[:, b], in0=XF[:, b], scalar=rstd[:, b:b + 1], in1=fing,
                                         op0=ALU.mult, op1=ALU.mult).then_inc(s_y, 1)

        @block.tensor
        def _(pe):
            def bank1(*name):
                i = B1.pos[name]
                if i >= 8:
                    who, n = B1.emptied(i - 8)
                    pe.wait_ge(s_act1 if who == "act" else s_dve1, n)
                return ps[:, i % 8, :]

            def chunk_ready(i):
                pe.wait_ge(s_chunk[i % WRING], 16 * (i // WRING + 1))

            pe.wait_ge(s_sil, 1)
            pe.wait_ge(s_set, 1)
            pe.wait_ge(s_bmod, 16)
            for j in range(MOD_CH):
                out = bank1("mod", j)
                chunk_ready(j)
                for k in range(KD):
                    last = nc.tensor.matmul(out[0:33, :], sil[:, k, :], chunk[:, j % WRING, k, :], start=(k == 0), stop=False)
                last.then_inc(s_chunk_used, 1)
                nc.tensor.matmul(out[0:33, :], ones[:, :], bmod[:, j * NC:(j + 1) * NC], start=False,
                                 stop=True).then_inc(s_fill1, 1)
            pe.wait_ge(s_const, 48)
            pe.wait_ge(s_kc, 16)
            out = bank1("keyT", "cache")
            for h in range(H):
                last = nc.tensor.transpose(out[:, h * P:(h + 1) * P], ktc[:, h * P:(h + 1) * P], ident[:, :])
            last.then_inc(s_fill1, 1)
            for b in range(NBLK):
                pe.wait_ge(s_h1, b + 1)
                for half in range(2):
                    out = bank1("hT", b, half)
                    for k in range(4):
                        last = nc.tensor.transpose(out[:, k * P:(k + 1) * P],
                                                   H1[:, b, (4 * half + k) * P:(4 * half + k + 1) * P], ident[:, :])
                    last.then_inc(s_fill1, 1)

            def z(c, b):
                i = MOD_CH + IN_ORDER[c]
                out = bank1("z", c, b)
                if b == 0:
                    chunk_ready(i)
                pe.wait_ge(s_act1, B1.emptied(B1.pos[("hT", b, 1)])[1])
                for k in range(KD):
                    last = nc.tensor.matmul(out, HT[:, k, b * P:(b + 1) * P], chunk[:, i % WRING, k, :],
                                            start=(k == 0), stop=(k == KD - 1))
                last.then_inc(s_fill1, 1)
                if b == NBLK - 1:
                    pe.wait_ge(s_fill1, B1.pos[("z", c, b)] + 1)
                    pe.nop().then_inc(s_chunk_used, 1)

            def headT(c, b):
                out = bank1("headT", c, b)
                who, n = B1.emptied(B1.pos[("z", c, b)])
                pe.wait_ge(s_act1 if who == "act" else s_dve1, n)
                for h in range(H):
                    last = nc.tensor.transpose(out[:, h * P:(h + 1) * P], heads[:, b % 2, h * P:(h + 1) * P], ident[:, :])
                last.then_inc(s_fill1, 1)

            for c in ("k", "q"):
                for b in range(NBLK):
                    z(c, b)
                    if b:
                        headT(c, b - 1)
                headT(c, NBLK - 1)
            for c in ("v", "f"):
                for b in range(NBLK):
                    z(c, b)

            pe.wait_ge(s_dft, 32)
            chunk_ready(DFT_C)
            for m in range(2):
                nc.tensor.matmul(bank1("fold", m), dftC[:, 2 * m, :], wf, start=True, stop=True).then_inc(s_fill1, 1)
            units = [(s, g) for s in range(2) for g in range(4)]

            def fourier_pos(u):
                s, g = u
                for m, name in enumerate(("fcos", "fsin")):
                    out = bank1(name, s, g)
                    fcols = slice(g * P, (g + 1) * P)
                    if s == 0:
                        last = nc.tensor.matmul(out[:, 0:P], F[:, 0, fcols], dftC[:, m, :], start=True, stop=True)
                    else:
                        for b in range(NSMP):
                            last = nc.tensor.matmul(out, F[:, 1 + b, fcols], dftS[:, m, b, :], start=(b == 0), stop=(b == NSMP - 1))
                    last.then_inc(s_fill1, 1)

            def fourier_ch(u):
                s, g = u
                i = units.index(u)
                w = NC if s else P
                out = bank1("fmix", s, g)
                pe.wait_ge(s_act1, B1.emptied(B1.pos[("fcos", s, g)])[1])
                pe.wait_ge(s_dve1, B1.emptied(B1.pos[("fsin", s, g)])[1])
                nc.tensor.matmul(out[:, 0:w], fold[:, 0, g, :], fstage[:, i % 2, 0, 0:w], start=True, stop=False)
                nc.tensor.matmul(out[:, 0:w], fold[:, 1, g, :], fstage[:, i % 2, 1, 0:w], start=False, stop=True).then_inc(s_fill1, 1)

            pe.wait_ge(s_act1, B1.emptied(B1.pos[("z", "f", NBLK - 1)])[1])
            for i, u in enumerate(units):
                fourier_pos(u)
                if i:
                    fourier_ch(units[i - 1])
            fourier_ch(units[-1])
            pe.wait_ge(s_fill1, B1.total)
            pe.nop().then_inc(s_chunk_used, 1)

            pe.wait_ge(s_act1, B1.count("act"))
            pe.wait_ge(s_dve1, B1.count("dve"))
            pe.wait_ge(s_vc, 16)

            def scores(i):
                b, h = UNITS[i]
                for m in range(2):
                    if i:
                        pe.wait_ge(s_exp, 2 * (i - 1) + m + 1)
                        pe.wait_ge(s_amax, i)
                    part = slice(DH * m, DH * m + DH)
                    q = qT[part, h, b * P:(b + 1) * P]
                    if b == 0:
                        last = nc.tensor.matmul(ps[:, 2 * m, 0:P], q, kT[part, h, 0:P], start=True, stop=True)
                    else:
                        for z_ in range(2):
                            k0 = P + z_ * (KEYS_S // 2)
                            last = nc.tensor.matmul(ps[:, 2 * m + z_, 0:KEYS_S // 2], q, kT[part, h, k0:k0 + KEYS_S // 2],
                                                    start=True, stop=True)
                    last.then_inc(s_scores, 1)

            def products(i):
                b, h = UNITS[i]
                nk = 1 if b == 0 else 5
                pe.wait_ge(s_w, i + 1)
                if i:
                    pe.wait_ge(s_wTc, i)
                for s in range(nk):
                    last = nc.tensor.transpose(ps[:, 4 + s // 4, (s % 4) * P:(s % 4) * P + P],
                                               Wt[:, i % 2, s * P:(s + 1) * P], ident[:, :])
                last.then_inc(s_wT, 1)
                pe.wait_ge(s_wTc, i + 1)
                if h == 0 and b:
                    pe.wait_ge(s_att, b)
                for s in range(nk):
                    vb = 0 if b == 0 else 1 + s
                    last = nc.tensor.matmul(ps[:, 6, h * P:(h + 1) * P], WtT[:, i % 2, s, :], V[:, vb, h * P:(h + 1) * P],
                                            start=(s == 0), stop=(s == nk - 1))
                last.then_inc(s_pv, 1)

            def attT(b):
                pe.wait_ge(s_att, b + 1)
                if b:
                    pe.wait_ge(s_mix, b)
                for h in range(H):
                    last = nc.tensor.transpose(ps[:, 7, h * P:(h + 1) * P], att[:, h * P:(h + 1) * P], ident[:, :])
                last.then_inc(s_attT, 1)

            scores(0)
            for i in range(len(UNITS)):
                if i + 1 < len(UNITS):
                    scores(i + 1)
                if i % H == 0 and i:
                    attT(i // H - 1)
                products(i)
            attT(NBLK - 1)

            def bank2(*name):
                i = B2.pos[name]
                if i >= 4:
                    who, n = B2.emptied(i - 4)
                    pe.wait_ge(s_act2 if who == "act" else s_dve2, n)
                return ps[:, i % 4, :]

            pe.wait_ge(s_mix, NBLK)
            pe.wait_ge(s_exp, 2 * len(UNITS))
            chunk_ready(OUT_C)
            chunk_ready(OUT_C + 1)
            for b in range(NBLK):
                for half in range(2):
                    out = bank2("merge", b, half)
                    for k in range(KD):
                        last = nc.tensor.matmul(out, mixT[:, k, b * P:(b + 1) * P], chunk[:, (OUT_C + half) % WRING, k, :],
                                                start=(k == 0), stop=(k == KD - 1))
                    last.then_inc(s_fill2, 1)

            for b in range(NBLK):
                pe.wait_ge(s_h2, b + 1)
                for half in range(2):
                    out = bank2("h2T", b, half)
                    for k in range(4):
                        last = nc.tensor.transpose(out[:, k * P:(k + 1) * P],
                                                   H2[:, b, (4 * half + k) * P:(4 * half + k + 1) * P], ident[:, :])
                    last.then_inc(s_fill2, 1)

            def queries(b):
                if b == 0:
                    pe.wait_ge(s_wq, 16)
                    pe.wait_ge(s_wq7, 16)
                    pe.wait_ge(s_keys, 16)
                    pe.wait_ge(s_act2, B2.emptied(B2.pos[("h2T", NBLK - 1, 1)])[1])
                for g in range(4):
                    out = bank2("query", b, g)
                    for j in range(4):
                        for k in range(KD):
                            c = (4 * g + j) * P
                            last = nc.tensor.matmul(out[:, j * P:(j + 1) * P], wq[:, k, c:c + P] if k < 7 else wq7[:, c:c + P],
                                                    h2T[:, k, b * P:(b + 1) * P],
                                                    start=(k == 0), stop=(k == KD - 1))
                    last.then_inc(s_fill2, 1)
                    out = bank2("score", b, g)
                    pe.wait_ge(s_act2, B2.emptied(B2.pos[("query", b, g)])[1])
                    for j in range(4):
                        last = nc.tensor.matmul(out[:, j * P:(j + 1) * P], qTq[:, j, :], keys[:, 4 * g + j, :],
                                                start=True, stop=True)
                    last.then_inc(s_fill2, 1)

            def dense_gates(b):
                pe.wait_ge(s_gate, b + 1)
                out = bank2("selT", b)
                for w, src in enumerate((sel[:, 0, :], sel[:, 1, :], gates[:, 1, :])):
                    last = nc.tensor.transpose(out[:, w * P:(w + 1) * P], src, ident[:, :])
                last.then_inc(s_fill2, 1)

                def four(it, u, first):
                    q = (b - 1) * 32 + it * 2 + u
                    pe.wait_ge(s_lhs1, q + 1)
                    pe.wait_ge(s_rhs1, q + 1)
                    if not first:
                        pe.wait_ge(s_gev, q - 1)
                    for t in range(4):
                        last = nc.tensor.matmul(ps[:, 4 + u, t * P:(t + 1) * P], lhs1[:, u, t, :], rhs1[:, u, t, :],
                                                start=True, stop=True)
                    last.then_inc(s_gq, 1)
                if b == 1:
                    for u in range(2):
                        four(0, u, True)
                with pe.Fori(1 if b == 1 else 0, 16) as it:
                    for u in range(2):
                        four(it, u, False)

            queries(0)
            queries(1)
            for b in range(1, NBLK):
                if b + 1 < NBLK:
                    queries(b + 1)
                dense_gates(b)

            def products3(out, hi, lo, rhi, rlo, start, stop):
                nc.tensor.matmul(out, hi, rhi, start=start, stop=False)
                nc.tensor.matmul(out, hi, rlo, start=False, stop=False)
                return nc.tensor.matmul(out, lo, rhi, start=False, stop=stop)

            def experts(i, first):
                for j in range(GRP):
                    n = i * GRP + j
                    pe.wait_ge(s_ulo, n + 1)
                    if not (first and j < 2):
                        pe.wait_ge(s_ge, n - 1)
                    for k in range(KD):
                        last = products3(ps[:, j % 2, :], U_hi[:, j % 2, k, :], U_lo[:, j % 2, k, :],
                                         hT_hi[:, k, :], hT_lo[:, k, :], k == 0, k == KD - 1)
                    last.then_inc(s_a, 1)
                for q in range(8):
                    if not (first and q < 4):
                        pe.wait_ge(s_flush, 8 * i + q - 3)
                    for j in range(GRP):
                        if q == 0:
                            pe.wait_ge(s_clo, i * GRP + j + 1)
                            pe.wait_ge(s_vlo, i * GRP + j + 1)
                        tok = slice((q // 2) * P, (q // 2 + 1) * P)
                        col = slice((q % 2) * NC, (q % 2 + 1) * NC)
                        last = products3(ps[:, 4 + q % 4, :], C_hi[:, j, tok], C_lo[:, j, tok],
                                         V_hi[:, j, col], V_lo[:, j, col], j == 0, j == GRP - 1)
                    last.then_inc(s_vb, 1)

            pe.wait_ge(s_hTlo, 1)
            pe.wait_ge(s_act2, B2.count("act"))
            pe.wait_ge(s_dve2, B2.count("dve"))
            pe.wait_ge(s_gev, 32 * NSMP)
            experts(0, True)
            with pe.Fori(1, NGRP) as i:
                experts(i, False)


def _constants():
    ident = np.eye(P, dtype=np.float32)
    t = np.arange(NSMP * P)
    nf = DH // 4
    inv = (np.float32(10000.0) ** (-np.arange(nf, dtype=np.float32) / np.float32(nf))).astype(np.float32)
    ar = (t // 64).astype(np.float32)[:, None] * inv
    ac = (t % 64).astype(np.float32)[:, None] * inv
    ang = np.concatenate([ar, ar, ac, ac], -1)
    sign = np.concatenate([-np.ones(16), np.ones(16)] * 2).astype(np.float32)
    cos = np.cos(ang).astype(np.float32).reshape(NSMP, P, DH).transpose(1, 0, 2)
    sin = (np.sin(ang).astype(np.float32) * sign).reshape(NSMP, P, DH).transpose(1, 0, 2)

    def dft(n):
        a = 2 * np.pi * ((np.arange(n)[:, None] * np.arange(n)[None, :]) % n) / n
        return np.cos(a) / np.sqrt(n), np.sin(a) / np.sqrt(n)
    c5, s5 = dft(NSMP * P)
    seq = np.stack([c5, s5]).reshape(2, NSMP, P, NSMP * P).transpose(2, 0, 1, 3).astype(np.float32)
    c1, s1 = dft(P)
    ch = np.stack([c1, s1, -s1]).transpose(1, 0, 2).astype(np.float32)
    return [np.ascontiguousarray(a) for a in (ident, cos, sin, seq, ch)]


def kernel(**inputs):
    import concourse.bacc as bacc
    from concourse.bass_utils import run_bass_kernel_spmd

    g = {k: np.asarray(v) for k, v in inputs.items()}
    ident, cos, sin, seq, ch = _constants()
    arrays = {
        "xall": np.concatenate([g["x_prompt"].reshape(P, D), g["x_sample"].reshape(NSMP * P, D)]),
        "condT": np.stack([g["c_ctx"].reshape(D), g["c"].reshape(D)]).reshape(2, KD, P).transpose(2, 1, 0),
        "w_mod": g["w_mod"][0], "b_mod": g["b_mod"], "norm1_g": g["norm1_g"][0], "w_in": g["w_in"][0],
        "lam4": np.stack([g["lam_q1"][0], g["lam_q2"][0], g["lam_k1"][0], g["lam_k2"][0]]),
        "subln_g": g["subln_g"][0], "w_fourier": g["w_fourier"][0].transpose(1, 0, 2), "w_out": g["w_out"][0],
        "norm2_g": g["norm2_g"][0], "w_query": g["w_query"][0],
        "keysT": g["sub_keys"][0].transpose(3, 0, 1, 2).reshape(P, 16, NKEY),
        "expert_u": g["expert_u"][0],
        "expert_uT": g["expert_u"][0].reshape(NB1, P, KD, P).transpose(0, 3, 2, 1), "expert_v": g["expert_v"][0], "final_g": g["final_g"],
        "cache_k": g["cache_k"].reshape(P, NC), "cache_v": g["cache_v"].reshape(P, NC),
        "ident": ident, "cos": cos, "sin": sin, "dft_seq": seq, "dft_ch": ch,
    }
    arrays = {k: np.ascontiguousarray(v) for k, v in arrays.items()}
    nc = bacc.Bacc("TRN2", target_bir_lowering=False, num_devices=1)
    f32 = mybir.dt.float32
    args = [nc.dram_tensor(f"in_{k}", v.shape, f32, kind="ExternalInput").ap() for k, v in arrays.items()]
    outs = {"y": (NBLK * P, D), "state_k": (P, NC), "state_v": (P, NC)}
    args += [nc.dram_tensor(f"out_{k}", s, f32, kind="ExternalOutput").ap() for k, s in outs.items()]
    program(nc, *args)
    r = run_bass_kernel_spmd(nc, [{f"in_{k}": v for k, v in arrays.items()}], core_ids=[0]).results[0]
    yy = r["out_y"]
    return (yy[:P].reshape(1, P, D), yy[P:].reshape(1, NSMP * P, D),
            r["out_state_k"].reshape(1, 1, P, H, 2 * DH), r["out_state_v"].reshape(1, 1, P, H, 2 * DH))
```

```python
import math
from contextlib import ExitStack

import numpy as np
import concourse.bass as bass
from concourse import mybir

ds = bass.ds

P = 128
D = 1024
KD = D // P
NBLK = 5
NSMP = 4
H = 4
DH = 64
NC = 512
MOD_CH = 12
IN_CH = 4
OUT_CH = 2
KEYS_S = 640
PH = 8
TOPK = 16
NKEY = 128
SLOTS = PH * TOPK
LAM_INIT = 0.8 - 0.6 * math.exp(-0.3 * 0)
EPS = 1e-6
NEG = -3.0e38
WRING = 3
NB1 = NKEY
GRP = 4
NGRP = NB1 // GRP
TS = NSMP * P
ROWS = 8
RR = 4
ORDER = (1, 2, 3, 4, 0)
QUAD = 4
QUADS = P // QUAD
PARTS = 8
PART = QUADS // PARTS
LR, RR1 = 4, 3


def _phase1_jobs():
    jobs = [(("mod", j), "act") for j in range(MOD_CH)]
    jobs.append((("keyT", "cache"), "act"))
    jobs += [(("hT", b, half), "act") for b in range(NBLK) for half in range(2)]
    for c in ("k", "q"):
        for b in range(NBLK):
            jobs.append((("z", c, b), "act" if b == 0 else "dve"))
            if b >= 1:
                jobs.append((("headT", c, b - 1), "act"))
        jobs.append((("headT", c, NBLK - 1), "act"))
    jobs += [(("z", c, b), "act") for c in ("v", "f") for b in range(NBLK)]
    jobs += [(("fold", 0), "act"), (("fold", 1), "dve")]
    units = [(s, g) for s in range(2) for g in range(4)]
    for i, u in enumerate(units):
        jobs += [(("fcos",) + u, "act"), (("fsin",) + u, "dve")]
        if i:
            jobs.append((("fmix",) + units[i - 1], "act"))
    jobs.append((("fmix",) + units[-1], "act"))
    return jobs


def _phase2_jobs():
    jobs = []
    for b in range(NBLK):
        jobs += [(("merge", b, half), "dve") for half in range(2)]
    for b in range(NBLK):
        jobs += [(("h2T", b, half), "act") for half in range(2)]
    def query(b, g):
        return [(("query", b, g), "act"), (("score", b, g), "dve")]
    jobs += query(ORDER[0], 0) + query(ORDER[0], 1)
    for n, b in enumerate(ORDER):
        if n:
            jobs.append((("selT", n), "act"))
        jobs += query(b, 2) + query(b, 3)
        if n + 1 < NBLK:
            jobs += query(ORDER[n + 1], 0) + query(ORDER[n + 1], 1)
    return jobs


class Banks:

    def __init__(self, jobs, nbanks):
        self.pos = {name: n for n, (name, _) in enumerate(jobs)}
        self.who = [w for _, w in jobs]
        self.nbanks = nbanks
        self.total = len(jobs)

    def emptied(self, n):
        return self.who[n], sum(w == self.who[n] for w in self.who[:n + 1])

    def count(self, who):
        return sum(w == who for w in self.who)


def program(nc, xall, condT, w_mod, b_mod, norm1_g, w_in, lam4, subln_g, w_fourier, w_out, norm2_g,
            w_query, keysT, expert_u, expert_uT, expert_v, final_g, cache_k, cache_v,
            ident_d, cos_d, sin_d, dft_seq_d, dft_ch_d, y, state_k, state_v):
    f32, u32, f32r, bf16 = mybir.dt.float32, mybir.dt.uint32, mybir.dt.float32r, mybir.dt.bfloat16
    ALU, ACT, AX = mybir.AluOpType, mybir.ActivationFunctionType, mybir.AxisListType
    B1, B2 = Banks(_phase1_jobs(), 8), Banks(_phase2_jobs(), 4)

    ctx = ExitStack()
    with ctx:
        def sb(name, shape, dt=f32):
            return ctx.enter_context(nc.sbuf_tensor(name, shape, dt))

        def sem(name):
            return ctx.enter_context(nc.semaphore(name))

        ident = sb("ident", [P, P])
        ones = sb("ones", [1, 33])
        lam = sb("lam", [P, 8])
        gsub = sb("gsub", [P, 1])
        powe = sb("powe", [P, 8])
        ss = sb("ss", [P, NBLK])
        rstd = sb("rstd", [P, NBLK])
        amax = sb("amax", [P, 2, 2])
        asum = sb("asum", [P, 2, 2])
        ss4 = sb("ss4", [P, 2, H])
        iota = sb("iota", [P, NKEY])
        places = sb("places", [P, TOPK], bf16)
        idx = sb("idx", [P, SLOTS], u32)
        idxn = sb("idxn", [P, 2, 2], u32)
        gates = sb("gates", [P, 2, SLOTS])
        dots = sb("dots", [P, SLOTS])
        coef = sb("coef", [P, SLOTS])
        sel = sb("sel", [P, 2, SLOTS])
        gsum = sb("gsum", [P, 2, PH])
        rhs_more = sb("rhs_more", [P, QUAD, NKEY])

        XO, G2O, MO, BO, WO, CO = 0, 5120, 7168, 13312, 18432, 35840
        ARENA = 51200
        arena = sb("arena", [P, WO])
        with nc.sbuf_tensor("arena_w", [P, ARENA - WO], f32) as arena_w:
            pass

        def cutout(lo, n, rows=slice(0, P)):
            return arena[rows, lo:lo + n] if lo < WO else arena_w[rows, lo - WO:lo - WO + n]

        X = cutout(XO, 5120).rearrange("p (b d) -> p b d", b=NBLK)
        F = cutout(XO, 2560).rearrange("p (b n) -> p b n", b=NBLK)
        fstage = cutout(XO + 2560, 2048).rearrange("p (r m n) -> p r m n", r=2, m=2)
        dftC = cutout(XO + 4608, 384).rearrange("p (m n) -> p m n", m=3)
        Wt = cutout(XO, 1280).rearrange("p (r n) -> p r n", r=2)
        probs = cutout(XO + 1280, 2560).rearrange("p (r m n) -> p r m n", r=2, m=2)
        junk = cutout(BO, D)
        HT = cutout(BO, 5120).rearrange("p (k t) -> p k t", k=KD)
        chunk = cutout(WO, WRING * KD * NC).rearrange("p (r k n) -> p r k n", r=WRING, k=KD)
        H1 = cutout(WO + WRING * KD * NC, 5120).rearrange("p (b d) -> p b d", b=NBLK)
        H2 = [cutout(BO, D)] + [cutout(WO + (MOD_CH + IN_CH) % WRING * KD * NC + b * D, D) for b in range(NSMP)]
        mixT = cutout(WO + WRING * KD * NC, 5120).rearrange("p (k t) -> p k t", k=KD)
        G2 = cutout(G2O, 2048).rearrange("p (c d) -> p c d", c=2)
        M = cutout(MO, 6144).rearrange("p (c w d) -> p c w d", c=2, w=3)
        SC2, SH2, G1 = range(3)
        h2T = cutout(MO, 5120).rearrange("p (k t) -> p k t", k=KD)
        fing = cutout(MO + 5120, 1024)
        wq7 = cutout(BO + 1024, 2048)
        wq = cutout(CO, 7 * 2048).rearrange("p (k n) -> p k n", k=7)
        keys = cutout(BO + 3072, 2048).rearrange("p (g n) -> p g n", g=16)
        gbuf = cutout(WO, NKEY * P).rearrange("p (i t) -> p i t", i=NKEY)
        lhs1 = [cutout(lo + w * 512, 512).rearrange("p (t n) -> p t n", t=QUAD)
                for lo in (WO + 16384, MO + 5120) for w in range(2)]
        rhs1 = [cutout(CO + 14336 + w * 512, 512).rearrange("p (t n) -> p t n", t=QUAD) for w in range(2)] + [rhs_more[:, :, :]]
        onehot = cutout(XO, 1024).bitcast(bf16).rearrange("p (s j) -> p s j", j=TOPK)
        cand = [cutout(lo, 256) for lo in (XO + 2048, XO)]
        rest = [cutout(lo, 256).rearrange("p (w n) -> p w n", w=2) for lo in (XO + 2304, XO + 256)]
        cand2 = [cutout(lo, 256) for lo in (XO + 2304, XO + 256)]
        idxf = cutout(XO + 2560, 128).bitcast(bf16).rearrange("p (h w j) -> p h w j", h=PH, w=2)
        top = cutout(XO + 2816, 128).rearrange("p (h j) -> p h j", h=PH)
        posf = cutout(XO + 2944, 64).bitcast(bf16)
        qTq = cutout(XO + 3072, 512).rearrange("p (g t) -> p g t", g=4)
        selT = cutout(XO + 3584, 768).rearrange("p (r w t) -> p r w t", r=2, w=3)
        best = cutout(XO + 4352, 256).rearrange("p (h w j) -> p h w j", h=PH, w=2)
        besti = cutout(XO + 4608, 256).bitcast(u32).rearrange("p (h w j) -> p h w j", h=PH, w=2)
        pos = cutout(XO + 4864, 128).bitcast(u32).rearrange("p (h j) -> p h j", h=PH)
        posb = cutout(XO + 4992, 128).bitcast(u32).rearrange("p (h j) -> p h j", h=PH)
        acc = cutout(XO, 4096).rearrange("p (b d) -> p b d", b=NSMP)
        acc0 = cutout(XO + 4096, 1024)
        XF = cutout(MO, 5120).rearrange("p (b d) -> p b d", b=NBLK)
        rowr = cutout(BO + 1024, RR * D).rearrange("p (r d) -> p r d", r=RR)

        V_hi, V_lo = sb("V_hi", [P, GRP, D], f32r), sb("V_lo", [P, GRP, D], f32r)
        C_hi, C_lo = sb("C_hi", [P, GRP, TS], f32r), sb("C_lo", [P, GRP, TS], f32r)
        V_in, gate_in = sb("V_in", [P, 2, D]), sb("gate_in", [P, GRP, TS])
        act_t = sb("act_t", [P, 2, TS])
        hT_hi, hT_lo = sb("hT_hi", [P, KD, TS], f32r), sb("hT_lo", [P, KD, TS], f32r)
        U_hi, U_lo = sb("U_hi", [P, 2, KD, P], f32r), sb("U_lo", [P, 2, KD, P], f32r)
        U_in = sb("U_in", [P, 2, KD, P])
        creg = cutout(CO, 15360)
        bmod = cutout(CO, 6144, slice(0, 1))
        gbc = creg[:, 6144:8192].rearrange("p (w d) -> p w d", w=2)
        rows = cutout(CO + 8192, 1024, slice(0, 33)).rearrange("p (r n) -> p r n", r=2)
        M1 = creg[:, 9216:13312].rearrange("p (c w d) -> p c w d", c=2, w=2)
        sil = creg[:, 13824:14088].rearrange("p (k c) -> p k c", k=KD)
        cond = creg[:, 14088:14104].rearrange("p (k c) -> p k c", k=KD)
        lamv = creg[:, 14104:14360].rearrange("p (w e) -> p w e", w=4)
        kT = creg[:, 0:3072].rearrange("p (h t) -> p h t", h=H)
        qT = creg[:, 3072:5632].rearrange("p (h t) -> p h t", h=H)
        V = creg[:, 5632:8704].rearrange("p (b n) -> p b n", b=6)
        WtT = creg[:, 8704:9984].rearrange("p (r s n) -> p r s n", r=2, s=5)
        ropet = creg[:, 9984:11008].rearrange("p (w n) -> p w n", w=2)
        heads = creg[:, 11008:12032].rearrange("p (r n) -> p r n", r=2)
        ropec = creg[:, 12032:12544].rearrange("p (w b e) -> p w b e", w=2, b=NSMP)
        ktc = creg[:, 13312:13824]
        att = creg[:, 12544:13056]
        squares = creg[:, 9984:10496]
        fold = creg[:, 13824:14848].rearrange("p (m g n) -> p m g n", m=2, g=4)
        wf = creg[:, 14848:15360].rearrange("p (g n) -> p g n", g=4)

        x1_d = nc.dram_tensor("x1_scratch", (NBLK * P, D), f32, kind="Internal").ap()
        gates_d = nc.dram_tensor("gates_scratch", (NB1, P, TS), f32, kind="Internal").ap()

        ps = ctx.enter_context(nc.psum_tensor("ps", [P, 8, NC], f32))

        s_x = sem("s_x"); s_cond = sem("s_cond"); s_const = sem("s_const"); s_bmod = sem("s_bmod")
        s_gbc = sem("s_gbc"); s_kc = sem("s_kc"); s_vc = sem("s_vc"); s_rope = sem("s_rope")
        s_dft = sem("s_dft"); s_wq = sem("s_wq"); s_keys = sem("s_keys"); s_fing = sem("s_fing")
        s_chunk = [sem(f"s_chunk{i}") for i in range(WRING)]
        s_chunk_used = sem("s_chunk_used")
        s_xr = [sem(f"s_xr{b}") for b in range(NBLK)]
        s_out = sem("s_out")
        s_set = sem("s_set"); s_exps = sem("s_exps"); s_sil = sem("s_sil")
        s_lamsum = sem("s_lamsum"); s_lamexp = sem("s_lamexp"); s_lam = sem("s_lam")
        s_fill1 = sem("s_fill1"); s_act1 = sem("s_act1"); s_dve1 = sem("s_dve1")
        s_rows = sem("s_rows"); s_bc = sem("s_bc")
        s_sq1 = sem("s_sq1"); s_var1 = sem("s_var1"); s_rstd1 = sem("s_rstd1"); s_h1 = sem("s_h1"); s_mod2 = sem("s_mod2")
        
        s_scores = sem("s_scores"); s_amax = sem("s_amax"); s_exp = sem("s_exp"); s_w = sem("s_w")
        s_wT = sem("s_wT"); s_wTc = sem("s_wTc"); s_pv = sem("s_pv"); s_praw = sem("s_praw"); s_asq = sem("s_asq"); s_avar = sem("s_avar")
        s_arstd = sem("s_arstd"); s_att = sem("s_att"); s_attT = sem("s_attT"); s_mix = sem("s_mix")
        s_fill2 = sem("s_fill2"); s_act2 = sem("s_act2"); s_dve2 = sem("s_dve2")
        s_x1 = sem("s_x1"); s_sq2 = sem("s_sq2"); s_var2 = sem("s_var2"); s_rstd2 = sem("s_rstd2"); s_h2 = sem("s_h2")
        s_top = sem("s_top"); s_gexp = sem("s_gexp"); s_idx = sem("s_idx"); s_gate = sem("s_gate")
        s_staged = sem("s_staged"); s_ix = sem("s_ix")
        s_spill = sem("s_spill"); s_xf = sem("s_xf"); s_wq7 = sem("s_wq7")
        s_selT = sem("s_selT"); s_diff = sem("s_diff"); s_dsq = sem("s_dsq"); s_lhs1 = sem("s_lhs1"); s_rhs1 = sem("s_rhs1")
        s_gq = sem("s_gq"); s_gev = sem("s_gev"); s_gout = [sem(f"s_gout{i}") for i in range(2)]
        s_hThi = sem("s_hThi"); s_hTlo = sem("s_hTlo"); s_acc0 = sem("s_acc0")
        s_uin = [sem(f"s_uin{i}") for i in range(2)]
        s_vin = [sem(f"s_vin{i}") for i in range(2)]
        s_gin = [sem(f"s_gin{i}") for i in range(4)]
        s_uhi = sem("s_uhi"); s_ulo = sem("s_ulo"); s_vhi = sem("s_vhi"); s_vlo = sem("s_vlo")
        s_a = sem("s_a"); s_ge = sem("s_ge"); s_c = sem("s_c"); s_chi = sem("s_chi"); s_clo = sem("s_clo")
        s_vb = sem("s_vb"); s_flush = sem("s_flush")
        s_row = [sem(f"s_row{i}") for i in range(RR)]
        s_used = sem("s_used"); s_gelu = sem("s_gelu"); s_coef = sem("s_coef")
        s_x2 = sem("s_x2"); s_sq3 = sem("s_sq3"); s_var3 = sem("s_var3"); s_rstd3 = sem("s_rstd3"); s_y = sem("s_y")
        s_step = sem("s_step"); s_setp = sem("s_setp")

        DFT_C = MOD_CH + IN_CH
        OUT_C = DFT_C + 1
        CHUNKS = OUT_C + OUT_CH
        IN_ORDER = {"k": 0, "q": 1, "v": 2, "f": 3}
        IN_COL = {"q": 0, "k": 1, "v": 2, "f": 3}
        w_mod_v = w_mod.rearrange("(k p) n -> p k n", p=P)
        w_in_v = w_in.rearrange("(k p) n -> p k n", p=P)
        w_out_v = w_out.rearrange("(k p) n -> p k n", p=P)
        dftS = chunk[:, DFT_C % WRING].rearrange("p (m s) n -> p m s n", m=2)
        w_query_v = w_query.rearrange("(k p) n -> p k n", p=P)
        UNITS = [(b, h) for b in range(NBLK) for h in range(H)]

        block = ctx.enter_context(nc.Block())

        @block.sync
        def _(sp):
            for i in range(CHUNKS):
                if i == 1:
                    sp.dma_start(X, xall.rearrange("(b p) d -> p b d", p=P)).then_inc(s_x, 16)
                if i >= WRING:
                    sp.wait_ge(s_chunk_used, i - WRING + 1)
                if i < MOD_CH:
                    src = w_mod_v[:, :, i * NC:(i + 1) * NC]
                elif i < DFT_C:
                    c = [IN_COL[x] for x in ("k", "q", "v", "f")][i - MOD_CH]
                    src = w_in_v[:, :, c * NC:(c + 1) * NC]
                elif i == DFT_C:
                    src = dft_seq_d
                else:
                    c = i - OUT_C
                    src = w_out_v[:, :, c * NC:(c + 1) * NC]
                sp.dma_start(chunk[:, i % WRING], src).then_inc(s_chunk[i % WRING], 16)
                if i == DFT_C - 1:
                    sp.wait_ge(s_h1, NBLK)
                    sp.dma_start(dftC, dft_ch_d).then_inc(s_dft, 16)
                    sp.dma_start(wf, w_fourier).then_inc(s_dft, 16)
            sp.wait_ge(s_wT, len(UNITS))
            for b in range(NBLK):
                sp.dma_start(X[:, b], xall[b * P:(b + 1) * P, :]).then_inc(s_xr[b], 16)
            sp.wait_ge(s_mix, NBLK)
            sp.wait_ge(s_out, 32)
            sp.dma_start(wq, w_query_v[:, 0:7, :]).then_inc(s_wq, 16)
            sp.dma_start(wq7, w_query_v[:, 7, :]).then_inc(s_wq7, 16)
            sp.dma_start(keys, keysT).then_inc(s_keys, 16)
            for b in range(NBLK):
                sp.wait_ge(s_x1, 2 * (b + 1))
                sp.dma_start(x1_d[b * P:(b + 1) * P, :], X[:, b]).then_inc(s_spill, 16)
            def load_u(n, r):
                sp.dma_start(U_in[:, r], expert_uT[ds(n, 1)].rearrange("a p k n -> (a p) k n") if not isinstance(n, int)
                             else expert_uT[n]).then_inc(s_uin[r], 16)

            def load_v(n, r):
                sp.dma_start(V_in[:, r], expert_v[ds(n * P, P), :] if not isinstance(n, int)
                             else expert_v[n * P:(n + 1) * P, :]).then_inc(s_vin[r], 16)

            def load_gates(n, j):
                sp.dma_start(gate_in[:, j], gates_d[ds(n, 1)].rearrange("a p t -> (a p) t") if not isinstance(n, int)
                             else gates_d[n]).then_inc(s_gin[j], 16)

            for b in range(1, NBLK):
                for half in range(2):
                    if b == NBLK - 1 and half:
                        sp.wait_ge(s_fill2, B2.total)
                        for j in range(2):
                            load_u(j, j)
                    sp.wait_ge(s_gev, QUADS * (b - 1) + QUADS // 2 * (half + 1))
                    t0 = half * (P // 2)
                    sp.dma_start(gates_d[:, :, (b - 1) * P + t0:(b - 1) * P + t0 + P // 2].rearrange("i p t -> p i t"),
                                 gbuf[:, :, t0:t0 + P // 2]).then_inc(s_gout[half], 16)

            for half in range(2):
                sp.wait_ge(s_gout[half], 16 * NSMP)
            for j in range(2):
                load_v(j, j)
                load_gates(j, j)
            for j in range(2, GRP):
                sp.wait_ge(s_ulo, j - 1)
                load_u(j, j % 2)
                sp.wait_ge(s_vlo, j - 1)
                load_v(j, j % 2)
                load_gates(j, j)
            with sp.Fori(1, NGRP) as i:
                for j in range(GRP):
                    n = i * GRP + j
                    sp.wait_ge(s_ulo, n - 1)
                    load_u(n, j % 2)
                    sp.wait_ge(s_vlo, n - 1)
                    load_v(n, j % 2)
                    sp.wait_ge(s_c, n - 3)
                    load_gates(n, j)
            sp.dma_start(fing, final_g.unsqueeze(0).broadcast_to([P, D])).then_inc(s_fing, 16)
            sp.wait_ge(s_hTlo, 1)
            sp.dma_start(XF, x1_d.rearrange("(b p) d -> p b d", p=P)).then_inc(s_xf, 16)
            for n, b in enumerate(ORDER):
                sp.wait_ge(s_y, n + 1)
                sp.dma_start(y[b * P:(b + 1) * P, :], XF[:, b]).then_inc(s_out, 16)
            sp.wait_ge(s_out, 16 * (NBLK + 2))

        @block.gpsimd
        def _(pool):
            pool.iota(iota[:, :], pattern=[[1, NKEY]], base=0, channel_multiplier=0,
                      allow_small_or_imprecise_dtypes=True).then_inc(s_setp, 1)
            pool.memset(powe[:, :], -0.5).then_inc(s_setp, 1)
            pool.wait_ge(s_setp, 2)

            def spread_mod(j):
                pool.wait_ge(s_rows, j + 1)
                part, half = j // 2, j % 2
                cols = slice(half * NC, (half + 1) * NC)
                for c in range(2):
                    if part < 2:
                        dst = M1[:, c, 1 - part, cols]
                    else:
                        dst = G2[:, c, cols] if part == 5 else M[:, c, {2: G1, 3: SH2, 4: SC2}[part], cols]
                    pool.partition_broadcast(dst, rows[32 * c:32 * c + 1, j % 2, :], P).then_inc(s_bc, 1)

            for j in range(4):
                spread_mod(j)
            pool.wait_ge(s_bc, 8)
            pool.wait_ge(s_var1, 1)
            pool.tensor_tensor(rstd[:, :], ss[:, :], powe[:, 0:NBLK], ALU.pow).then_inc(s_rstd1, 1)
            pool.wait_ge(s_rstd1, 1)
            for j in range(4, MOD_CH):
                spread_mod(j)
            pool.wait_ge(s_bc, 2 * MOD_CH)
            for b in range(NBLK):
                pool.wait_ge(s_avar, b + 1)
                pool.tensor_tensor(ss4[:, 1, :], ss4[:, 0, :], powe[:, 0:H], ALU.pow).then_inc(s_arstd, 1)
            for b in range(NBLK):
                pool.wait_ge(s_var2, b + 1)
                pool.tensor_tensor(rstd[:, b:b + 1], ss[:, b:b + 1], powe[:, 0:1], ALU.pow).then_inc(s_rstd2, 1)

            for b in range(1, NBLK):
                pool.wait_ge(s_selT, b)
                for p in range(QUADS):
                    q = (b - 1) * QUADS + p
                    if q >= LR:
                        pool.wait_ge(s_gq, q - LR + 1)
                    pool.tensor_tensor(lhs1[q % LR], iota[:, :].unsqueeze(1).broadcast_to([P, QUAD, NKEY]),
                                       selT[:, b % 2, 1, p * QUAD:(p + 1) * QUAD].unsqueeze(2).broadcast_to([P, QUAD, NKEY]),
                                       ALU.subtract).then_inc(s_diff, 1)

            def fetch(table, i, t, first, base):
                st = i * (ROWS // 2) + t
                if not first:
                    pool.wait_ge(s_used, 2 * st - 2)
                at = (i - base) * ROWS + 2 * t
                src = idx[:, ds(at, 2)] if not isinstance(i, int) else idx[:, at:at + 2]
                pool.tensor_copy(idxn[:, t % 2, :], src).then_inc(s_ix, 1)
                pool.wait_ge(s_ix, st + 1)
                pool.sem_inc(s_staged, 1)
                for r in range(2):
                    row = 2 * (t % 2) + r
                    pool.indirect_dma_start(
                        out=rowr[:, row, :], out_offset=None, in_=table,
                        in_offset=bass.IndirectOffsetOnAxis(ap=idxn[:, t % 2, r:r + 1], axis=0)
                    ).then_inc(s_row[row], 16)

            pool.wait_ge(s_idx, 1)
            pool.wait_ge(s_fill2, B2.total)
            for t in range(ROWS // 2):
                fetch(expert_u, 0, t, t < 2, 0)
            with pool.Fori(1, NGRP // 2) as i:
                for t in range(ROWS // 2):
                    fetch(expert_u, i, t, False, 0)
            with pool.Fori(NGRP // 2, NGRP) as i:
                for t in range(ROWS // 2):
                    fetch(expert_v, i, t, False, NGRP // 2)
            for n, b in enumerate(ORDER):
                pool.wait_ge(s_var3, n + 1)
                pool.tensor_tensor(rstd[:, b:b + 1], ss[:, b:b + 1], powe[:, 0:1], ALU.pow).then_inc(s_rstd3, 1)

        @block.scalar
        def _(act):
            act.dma_start(cond[:, :, :], condT).then_inc(s_cond, 16)
            act.dma_start(bmod, b_mod).then_inc(s_bmod, 16)
            act.dma_start(ident[:, :], ident_d).then_inc(s_const, 16)
            act.dma_start(lamv[:, :, :], lam4.unsqueeze(0).broadcast_to([P, 4, DH])).then_inc(s_const, 16)
            act.dma_start(gsub[:, :], subln_g.unsqueeze(1)).then_inc(s_const, 16)
            act.dma_start(gbc[:, 0, :], norm1_g.unsqueeze(0).broadcast_to([P, D])).then_inc(s_gbc, 16)
            act.dma_start(gbc[:, 1, :], norm2_g.unsqueeze(0).broadcast_to([P, D])).then_inc(s_gbc, 16)
            act.dma_start(ktc, cache_k).then_inc(s_kc, 16)
            act.wait_ge(s_cond, 16)
            act.wait_ge(s_set, 1)
            act.activation(sil[:, :, 0:2], cond[:, :, :], ACT.Exp, scale=-1.0).then_inc(s_exps, 1)
            act.wait_ge(s_lamsum, 1)
            act.activation(lam[:, 2:4], lam[:, 0:2], ACT.Exp).then_inc(s_lamexp, 1)
            act.wait_ge(s_x, 16)
            for b in range(NBLK):
                if b:
                    act.wait_ge(s_sq1, b)
                act.activation(junk, X[:, b], ACT.Square, accum_out=ss[:, b:b + 1]).then_inc(s_sq1, 1)

            def bank1(*name):
                i = B1.pos[name]
                act.wait_ge(s_fill1, i + 1)
                return ps[:, i % 8, :]

            for j in range(MOD_CH):
                src = bank1("mod", j)
                if j >= 2:
                    act.wait_ge(s_bc, 2 * (j - 1))
                act.copy(rows[0:33, j % 2, :], src[0:33, :]).then_inc(s_rows, 1)
                act.wait_ge(s_rows, j + 1)
                act.nop().then_inc(s_act1, 1)

            def heads_out(name, dst):
                act.activation(dst, bank1(*name).rearrange("p (h t) -> p h t", h=H), ACT.Copy,
                               scale=DH ** -0.5 if name[1] == "q" else 1.0).then_inc(s_act1, 1)

            act.wait_ge(s_mod2, 1)
            act.wait_ge(s_h1, NBLK)
            act.dma_start(ropec[:, 0], cos_d).then_inc(s_rope, 16)
            act.dma_start(ropec[:, 1], sin_d).then_inc(s_rope, 16)
            act.dma_start(V[:, 1, :], cache_v).then_inc(s_vc, 16)
            heads_out(("keyT", "cache"), kT[:, :, P:2 * P])
            for b in range(NBLK):
                for half in range(2):
                    src = bank1("hT", b, half).rearrange("p (k t) -> p k t", k=4)
                    act.copy(HT[:, 4 * half:4 * half + 4, b * P:(b + 1) * P], src).then_inc(s_act1, 1)
            for ci, c in enumerate(("k", "q")):
                for b in range(NBLK):
                    if b == 0:
                        if ci:
                            act.wait_ge(s_fill1, B1.pos[("headT", "k", NBLK - 1)] + 1)
                            act.wait_ge(s_out, 16)
                        act.copy(heads[:, 0, :], bank1("z", c, 0)).then_inc(s_act1, 1)
                        if ci == 0:
                            act.wait_ge(s_act1, B1.emptied(B1.pos[("z", "k", 0)])[1])
                            act.dma_start(state_k, heads[:, 0, :]).then_inc(s_out, 16)
                    else:
                        dst = kT if c == "k" else qT
                        at = (b - 1) * P if c == "q" or b == 1 else b * P
                        heads_out(("headT", c, b - 1), dst[:, :, at:at + P])
                dst, at = (kT, 5 * P) if c == "k" else (qT, 4 * P)
                heads_out(("headT", c, NBLK - 1), dst[:, :, at:at + P])
            for b in range(NBLK):
                vb = 0 if b == 0 else b + 1
                act.copy(V[:, vb, :], bank1("z", "v", b)).then_inc(s_act1, 1)
                if b == 0:
                    act.wait_ge(s_act1, B1.emptied(B1.pos[("z", "v", 0)])[1])
                    act.dma_start(state_v, V[:, 0, :]).then_inc(s_out, 16)
            for b in range(NBLK):
                act.copy(F[:, b, :], bank1("z", "f", b)).then_inc(s_act1, 1)
            act.copy(fold[:, 0], bank1("fold", 0).rearrange("p (g n) -> p g n", g=4)).then_inc(s_act1, 1)
            units = [(s, g) for s in range(2) for g in range(4)]

            def mix_out(u):
                s, g = u
                src = bank1("fmix", s, g)
                if s == 0:
                    act.copy(mixT[:, 4 + g, 0:P], src[:, 0:P]).then_inc(s_act1, 1)
                else:
                    act.copy(mixT[:, 4 + g, P:NBLK * P], src).then_inc(s_act1, 1)

            for i, u in enumerate(units):
                w = NC if u[0] else P
                src = bank1("fcos", *u)
                act.copy(fstage[:, i % 2, 0, 0:w], src[:, 0:w]).then_inc(s_act1, 1)
                if i:
                    mix_out(units[i - 1])
            mix_out(units[-1])

            def keys_of(b):
                return P if b == 0 else KEYS_S // 2

            def exps(i):
                b, h = UNITS[i]
                for m in range(2):
                    act.wait_ge(s_amax, 2 * i + m + 1)
                    if i >= 2:
                        act.wait_ge(s_w, i - 1)
                    n_ = keys_of(b)
                    z_ = 1 if b == 0 else 2
                    dst = probs[:, i % 2, m, 0:z_ * n_].rearrange("p (z n) -> p z n", n=n_)
                    act.activation(dst, ps[:, 2 * m:2 * m + z_, 0:n_], ACT.Exp, bias=amax[:, i % 2, m:m + 1],
                                   accum_out=asum[:, i % 2, m:m + 1]).then_inc(s_exp, 1)

            def weights_out(i):
                b, h = UNITS[i]
                act.wait_ge(s_wT, i + 1)
                if i >= 2:
                    act.wait_ge(s_pv, i - 1)
                if b == 0:
                    act.copy(WtT[:, i % 2, 0, :], ps[:, 4, 0:P]).then_inc(s_wTc, 1)
                else:
                    act.copy(WtT[:, i % 2, 0:4, :], ps[:, 4, :].rearrange("p (s n) -> p s n", s=4))
                    act.copy(WtT[:, i % 2, 4, :], ps[:, 5, 0:P]).then_inc(s_wTc, 1)

            def att_squares(b):
                act.wait_ge(s_pv, H * (b + 1))
                if b:
                    act.wait_ge(s_attT, b)
                act.copy(att, ps[:, 6, :]).then_inc(s_praw, 1)
                act.wait_ge(s_praw, b + 1)
                for h in range(H):
                    ins = act.activation(squares[:, h * P:(h + 1) * P], att[:, h * P:(h + 1) * P], ACT.Square,
                                         accum_out=ss4[:, 0, h:h + 1])
                ins.then_inc(s_asq, 1)

            def att_out(b):
                act.wait_ge(s_attT, b + 1)
                act.activation(mixT[:, 0:4, b * P:(b + 1) * P], ps[:, 7, :].rearrange("p (h t) -> p h t", h=H),
                               ACT.Copy, scale=lam[:, 7:8]).then_inc(s_mix, 1)

            act.wait_ge(s_lam, 1)
            exps(0)
            for i in range(len(UNITS) + 3):
                if i + 1 < len(UNITS):
                    exps(i + 1)
                if i < len(UNITS):
                    weights_out(i)
                if i % H == 0 and i:
                    att_squares(i // H - 1)
                if i % H == 2 and i > H:
                    att_out(i // H - 1)

            for b in range(NBLK):
                act.wait_ge(s_x1, 2 * (b + 1))
                act.activation(H2[b], X[:, b], ACT.Square, accum_out=ss[:, b:b + 1]).then_inc(s_sq2, 1)

            def bank2(*name):
                i = B2.pos[name]
                act.wait_ge(s_fill2, i + 1)
                return ps[:, i % 4, :]

            act.wait_ge(s_h2, NBLK)
            for b in range(NBLK):
                for half in range(2):
                    src = bank2("h2T", b, half).rearrange("p (k t) -> p k t", k=4)
                    act.copy(h2T[:, 4 * half:4 * half + 4, b * P:(b + 1) * P], src).then_inc(s_act2, 1)

            def one_hot(q):
                act.wait_ge(s_diff, q + 1)
                act.activation(lhs1[q % LR], lhs1[q % LR], ACT.Square).then_inc(s_dsq, 1)
                act.wait_ge(s_dsq, q + 1)
                act.activation(lhs1[q % LR], lhs1[q % LR], ACT.Relu, bias=1.0, scale=-1.0).then_inc(s_lhs1, 1)

            def dense_gates(b, part):
                for p in range(part * PART, (part + 1) * PART):
                    q = (b - 1) * QUADS + p
                    act.wait_ge(s_gq, q + 1)
                    act.copy(gbuf[:, :, p * QUAD:(p + 1) * QUAD],
                             ps[:, 4 + q % 4, :].rearrange("p (t n) -> p n t", t=QUAD)).then_inc(s_gev, 1)
                    if p + LR - 1 < QUADS:
                        one_hot(q + LR - 1)

            def query_out(b, g):
                act.copy(qTq, bank2("query", b, g).rearrange("p (g t) -> p g t", g=4)).then_inc(s_act2, 1)

            def sel_out(b):
                act.copy(selT[:, b % 2], bank2("selT", b)[:, 0:3 * P].rearrange("p (w t) -> p w t", w=3)).then_inc(s_act2, 1)
                act.wait_ge(s_act2, B2.emptied(B2.pos[("selT", b)])[1])
                act.nop().then_inc(s_selT, 1)
                for p in range(LR - 1):
                    one_hot((b - 1) * QUADS + p)

            act.wait_ge(s_spill, 16 * NBLK)
            query_out(ORDER[0], 0)
            query_out(ORDER[0], 1)
            for n, b in enumerate(ORDER):
                if n:
                    sel_out(n)
                ahead = [(b, 2), (b, 3)] + ([(ORDER[n + 1], 0), (ORDER[n + 1], 1)] if n + 1 < NBLK else [])
                for part in range(PARTS):
                    if part % 2 and part // 2 < len(ahead):
                        query_out(*ahead[part // 2])
                    if part == PARTS - 3 and n + 1 == NBLK:
                        act.wait_ge(s_fill2, B2.total)
                        act.copy(hT_hi[:, :, :], h2T[:, :, P:]).then_inc(s_hThi, 1)
                    if part == PARTS - 2:
                        act.wait_ge(s_top, n + 1)
                        act.activation(top[:, :, :], top[:, :, :], ACT.Exp).then_inc(s_gexp, 1)
                    if n >= 2 and part in (0, PARTS // 2):
                        act.wait_ge(s_gout[2 * part // PARTS], 16 * (n - 1))
                    if n:
                        dense_gates(n, part)

            def split_u(n, r, k, first):
                act.wait_ge(s_uin[r], k)
                if not first:
                    act.wait_ge(s_a, n - 1)
                act.copy(U_hi[:, r], U_in[:, r]).then_inc(s_uhi, 1)

            def experts(i, first, last):
                for j in range(GRP):
                    n = i * GRP + j
                    if not (last and j == GRP - 1):
                        split_u(n + 1, (j + 1) % 2, 16 * (i * 2 + (j + 1) // 2 + 1), first and j == 0)
                    act.wait_ge(s_vin[j % 2], 16 * (i * 2 + j // 2 + 1))
                    if not first:
                        act.wait_ge(s_vb, 8 * i)
                    act.copy(V_hi[:, j], V_in[:, j % 2]).then_inc(s_vhi, 1)
                    act.wait_ge(s_a, n + 1)
                    if not (first and j < 2):
                        act.wait_ge(s_clo, n - 1)
                    act.activation(act_t[:, j % 2], ps[:, j % 2, :], ACT.Gelu).then_inc(s_ge, 1)
                    act.wait_ge(s_c, n + 1)
                    act.copy(C_hi[:, j], act_t[:, j % 2]).then_inc(s_chi, 1)

            split_u(0, 0, 16, True)
            experts(0, True, False)
            with act.Fori(1, NGRP // 2) as i:
                experts(i, False, False)
            act.wait_ge(s_used, SLOTS)
            act.activation(dots[:, :], dots[:, :], ACT.Gelu).then_inc(s_gelu, 1)
            with act.Fori(NGRP // 2, NGRP - 1) as i:
                experts(i, False, False)
            experts(NGRP - 1, False, True)
            for n, b in enumerate(ORDER):
                act.wait_ge(s_x2, n + 1)
                act.activation(acc0 if b == 0 else acc[:, b - 1], XF[:, b], ACT.Square, accum_out=ss[:, b:b + 1]).then_inc(s_sq3, 1)

        @block.vector
        def _(dve):
            steps = [0]

            def link(ins):
                steps[0] += 1
                ins.then_inc(s_step, 1)
                dve.wait_ge(s_step, steps[0])

            dve.wait_ge(s_setp, 1)
            dve.tensor_copy(places[:, :], iota[:, 0:TOPK])
            link(dve.memset(sil[:, :, :], 0.0))
            dve.memset(ones[:, :], 1.0).then_inc(s_set, 1)
            dve.wait_ge(s_exps, 1)
            link(dve.tensor_scalar(sil[:, :, 0:2], sil[:, :, 0:2], 1.0, None, ALU.add))
            link(dve.reciprocal(sil[:, :, 0:2], sil[:, :, 0:2]))
            link(dve.tensor_tensor(cond[:, :, :], cond[:, :, :], sil[:, :, 0:2], ALU.mult))
            link(dve.memset(sil[:, :, 0:2], 0.0))
            link(dve.tensor_copy(sil[:, :, 0:1], cond[:, :, 0:1]))
            dve.tensor_copy(sil[:, :, 32:33], cond[:, :, 1:2]).then_inc(s_sil, 1)
            dve.wait_ge(s_const, 48)
            link(dve.tensor_tensor(lamv[:, 0:2, :], lamv[:, 0:2, :], lamv[:, 2:4, :], ALU.mult))
            dve.tensor_reduce(lam[:, 0:2], lamv[:, 0:2, :], AX.X, ALU.add).then_inc(s_lamsum, 1)
            dve.wait_ge(s_lamexp, 1)
            link(dve.tensor_tensor(lam[:, 4:5], lam[:, 3:4], lam[:, 2:3], ALU.subtract))
            link(dve.tensor_scalar(lam[:, 5:6], lam[:, 4:5], -LAM_INIT, None, ALU.add))
            dve.tensor_scalar(lam[:, 7:8], gsub[:, :], 1.0 - LAM_INIT, None, ALU.mult).then_inc(s_lam, 1)
            dve.wait_ge(s_sq1, NBLK)
            dve.tensor_scalar(ss[:, :], ss[:, :], 1.0 / D, EPS, ALU.mult, ALU.add).then_inc(s_var1, 1)
            dve.wait_ge(s_bc, 8)
            dve.wait_ge(s_gbc, 32)
            for c in range(2):
                link(dve.scalar_tensor_tensor(out=M1[:, c, 0, :], in0=M1[:, c, 0, :], scalar=1.0,
                                              in1=gbc[:, 0, :], op0=ALU.add, op1=ALU.mult))
            dve.wait_ge(s_rstd1, 1)
            for b in range(NBLK):
                c = min(b, 1)
                link(dve.scalar_tensor_tensor(out=H1[:, b], in0=X[:, b], scalar=rstd[:, b:b + 1],
                                              in1=M1[:, c, 0, :], op0=ALU.mult, op1=ALU.mult))
                dve.tensor_tensor(H1[:, b], H1[:, b], M1[:, c, 1, :], ALU.add).then_inc(s_h1, 1)
            dve.wait_ge(s_bc, 2 * MOD_CH)
            for c in range(2):
                link(dve.scalar_tensor_tensor(out=M[:, c, SC2, :], in0=M[:, c, SC2, :], scalar=1.0,
                                              in1=gbc[:, 1, :], op0=ALU.add, op1=ALU.mult))
            dve.nop().then_inc(s_mod2, 1)

            def bank1(*name):
                i = B1.pos[name]
                dve.wait_ge(s_fill1, i + 1)
                return ps[:, i % 8, :]

            def rope(c, b, count):
                z = bank1("z", c, b)
                if b >= 2:
                    dve.wait_ge(s_fill1, B1.pos[("headT", c, b - 2)] + 1)
                elif c == "q":
                    dve.wait_ge(s_fill1, B1.pos[("headT", "k", 3)] + 1)
                if count:
                    dve.wait_ge(s_dve1, count)
                out = heads[:, b % 2, :]
                zg = z.rearrange("p (g e) -> p g e", g=8)
                t0 = ropet[:, 0, :].rearrange("p (g e) -> p g e", g=8)
                t1 = ropet[:, 1, :].rearrange("p (g u w e) -> p g u w e", g=8, u=2, w=2)
                zu = z.rearrange("p (g u w e) -> p g u w e", g=8, u=2, w=2)
                cos = ropec[:, 0, b - 1, :].unsqueeze(1).broadcast_to([P, 8, DH])
                sin = ropec[:, 1, b - 1, :].rearrange("p (u w e) -> p u w e", u=2, w=2)
                dve.tensor_tensor(t0, zg, cos, ALU.mult)
                for w in range(2):
                    sw = sin[:, :, w, :].unsqueeze(1).broadcast_to([P, 8, 2, 16])
                    ins = dve.tensor_tensor(t1[:, :, :, w, :], zu[:, :, :, 1 - w, :], sw, ALU.mult)
                steps[0] += 1
                ins.then_inc(s_step, 1)
                dve.wait_ge(s_step, steps[0])
                dve.tensor_tensor(out, ropet[:, 0, :], ropet[:, 1, :], ALU.add).then_inc(s_dve1, 1)

            dve.wait_ge(s_rope, 32)
            count = 0
            for c in ("k", "q"):
                for b in range(1, NBLK):
                    if b == 2 and c == "k":
                        dve.wait_ge(s_out, 16)
                    rope(c, b, count)
                    count += 1
            dve.tensor_copy(fold[:, 1], bank1("fold", 1).rearrange("p (g n) -> p g n", g=4)).then_inc(s_dve1, 1)
            units = [(s, g) for s in range(2) for g in range(4)]
            for i, u in enumerate(units):
                w = NC if u[0] else P
                src = bank1("fsin", *u)
                if i >= 2:
                    dve.wait_ge(s_fill1, B1.pos[("fmix",) + units[i - 2]] + 1)
                dve.tensor_copy(fstage[:, i % 2, 1, 0:w], src[:, 0:w]).then_inc(s_dve1, 1)

            dve.wait_ge(s_lam, 1)

            def neg_max(i):
                b, h = UNITS[i]
                z_, n_ = (1, P) if b == 0 else (2, KEYS_S // 2)
                for m in range(2):
                    dve.wait_ge(s_scores, 2 * i + m + 1)
                    if i >= 2:
                        dve.wait_ge(s_exp, 2 * (i - 2) + m + 1)
                    dve.tensor_reduce(amax[:, i % 2, m:m + 1], ps[:, 2 * m:2 * m + z_, 0:n_], AX.XY, ALU.max,
                                      negate=True).then_inc(s_amax, 1)

            def combine(i):
                b, h = UNITS[i]
                n_ = P if b == 0 else KEYS_S
                dve.wait_ge(s_exp, 2 * i + 2)
                link(dve.reciprocal(asum[:, i % 2, :], asum[:, i % 2, :]))
                dve.tensor_tensor(asum[:, i % 2, 1:2], asum[:, i % 2, 1:2], lam[:, 5:6], ALU.mult)
                if i >= 2:
                    dve.wait_ge(s_wT, i - 1)
                link(dve.tensor_scalar(Wt[:, i % 2, 0:n_], probs[:, i % 2, 0, 0:n_], asum[:, i % 2, 0:1], None, ALU.mult))
                dve.scalar_tensor_tensor(out=Wt[:, i % 2, 0:n_], in0=probs[:, i % 2, 1, 0:n_], scalar=asum[:, i % 2, 1:2],
                                         in1=Wt[:, i % 2, 0:n_], op0=ALU.mult, op1=ALU.add).then_inc(s_w, 1)

            def att_var(b):
                dve.wait_ge(s_asq, b + 1)
                dve.tensor_scalar(ss4[:, 0, :], ss4[:, 0, :], 1.0 / P, EPS, ALU.mult, ALU.add).then_inc(s_avar, 1)

            def att_norm(b):
                dve.wait_ge(s_arstd, b + 1)
                a = att.rearrange("p (h e) -> p h e", h=H)
                dve.tensor_tensor(a, a, ss4[:, 1, :].unsqueeze(2).broadcast_to([P, H, P]), ALU.mult).then_inc(s_att, 1)

            neg_max(0)
            for i in range(len(UNITS) + 2):
                if i < len(UNITS):
                    combine(i)
                if i % H == 1 and i > H:
                    att_var(i // H - 1)
                if i + 1 < len(UNITS):
                    neg_max(i + 1)
                if i % H == 1 and i > H:
                    att_norm(i // H - 1)

            def bank2(*name):
                i = B2.pos[name]
                dve.wait_ge(s_fill2, i + 1)
                return ps[:, i % 4, :]

            def make_h2(b):
                c = min(b, 1)
                dve.wait_ge(s_sq2, b + 1)
                dve.tensor_scalar(ss[:, b:b + 1], ss[:, b:b + 1], 1.0 / D, EPS, ALU.mult, ALU.add).then_inc(s_var2, 1)
                dve.wait_ge(s_rstd2, b + 1)
                link(dve.scalar_tensor_tensor(out=H2[b], in0=X[:, b], scalar=rstd[:, b:b + 1],
                                              in1=M[:, c, SC2, :], op0=ALU.mult, op1=ALU.mult))
                dve.tensor_tensor(H2[b], H2[b], M[:, c, SH2, :], ALU.add).then_inc(s_h2, 1)

            for b in range(NBLK):
                c = min(b, 1)
                dve.wait_ge(s_xr[b], 16)
                for half in range(2):
                    cols = slice(half * NC, (half + 1) * NC)
                    src = bank2("merge", b, half)
                    dve.tensor_tensor(H2[b][:, cols], src, M[:, c, G1, cols], ALU.mult).then_inc(s_dve2, 1)
                    dve.wait_ge(s_dve2, B2.emptied(B2.pos[("merge", b, half)])[1])
                    dve.tensor_tensor(X[:, b, cols], X[:, b, cols], H2[b][:, cols], ALU.add).then_inc(s_x1, 1)
                if b:
                    make_h2(b - 1)
            make_h2(NBLK - 1)

            def note(ins):
                steps[0] += 1
                ins.then_inc(s_step, 1)
                return steps[0]

            def key_tops(b, g):
                bank = bank2("score", b, g).rearrange("p (h w n) -> p h w n", h=2, w=2)
                chains = [(hh, w) for hh in range(2) for w in range(2)]
                done = [note(dve.max(best[:, 2 * g + hh, w, 0:8], bank[:, hh, w, :])) for hh, w in chains]
                for c, (hh, w) in enumerate(chains):
                    h = 2 * g + hh
                    dve.wait_ge(s_step, done[c])
                    dve.max_index(besti[:, h, w, 0:8], best[:, h, w, 0:8], bank[:, hh, w, :])
                    ins = dve.match_replace(rest[hh][:, w, :], best[:, h, w, 0:8], bank[:, hh, w, :], NEG)
                    done[c] = note(ins)
                for c, (hh, w) in enumerate(chains):
                    dve.wait_ge(s_step, done[c])
                    done[c] = note(dve.max(best[:, 2 * g + hh, w, 8:16], rest[hh][:, w, :]))
                for c, (hh, w) in enumerate(chains):
                    h = 2 * g + hh
                    dve.wait_ge(s_step, done[c])
                    ins = dve.max_index(besti[:, h, w, 8:16], best[:, h, w, 8:16], rest[hh][:, w, :])
                    if c == 3:
                        ins.then_inc(s_dve2, 1)

            def pair_tops(g):
                done = []
                for hh in range(2):
                    h = 2 * g + hh
                    c3 = cand[hh].rearrange("p (i j) -> p i j", i=TOPK)
                    done.append(note(dve.tensor_tensor(
                        c3, best[:, h, 0, :].unsqueeze(2).broadcast_to([P, TOPK, TOPK]),
                        best[:, h, 1, :].unsqueeze(1).broadcast_to([P, TOPK, TOPK]), ALU.add)))
                for hh in range(2):
                    dve.wait_ge(s_step, done[hh])
                    done[hh] = note(dve.max(top[:, 2 * g + hh, 0:8], cand[hh]))
                for hh in range(2):
                    h = 2 * g + hh
                    dve.wait_ge(s_step, done[hh])
                    dve.max_index(pos[:, h, 0:8], top[:, h, 0:8], cand[hh])
                    done[hh] = note(dve.match_replace(cand2[hh], top[:, h, 0:8], cand[hh], NEG))
                for hh in range(2):
                    dve.wait_ge(s_step, done[hh])
                    done[hh] = note(dve.max(top[:, 2 * g + hh, 8:16], cand2[hh]))
                for hh in range(2):
                    h = 2 * g + hh
                    dve.wait_ge(s_step, done[hh])
                    done[hh] = note(dve.max_index(pos[:, h, 8:16], top[:, h, 8:16], cand2[hh]))

            def select(n):
                b = ORDER[n]
                link(dve.tensor_copy(gsum[:, 1, :], top[:, :, 0]))
                dve.tensor_tensor(top[:, :, :], top[:, :, :],
                                  gsum[:, 1, :].unsqueeze(2).broadcast_to([P, PH, TOPK]),
                                  ALU.subtract).then_inc(s_top, 1)
                link(dve.tensor_copy(idxf.rearrange("p h w j -> p (h w j)"), besti[:, :, :, :].rearrange("p h w j -> p (h w j)")))
                link(dve.tensor_scalar(posb[:, :, :], pos[:, :, :], 4, None, ALU.logical_shift_right))
                link(dve.tensor_scalar(pos[:, :, :], pos[:, :, :], 15, None, ALU.bitwise_and))
                if n:
                    dve.wait_ge(s_fill2, B2.pos[("selT", n)] + 1)
                for w, source in ((0, posb), (1, pos)):
                    link(dve.tensor_copy(posf[:, :], source[:, :, :].rearrange("p h j -> p (h j)")))
                    link(dve.tensor_tensor(onehot, posf[:, :].unsqueeze(2).broadcast_to([P, SLOTS, TOPK]),
                                           places[:, :].unsqueeze(1).broadcast_to([P, SLOTS, TOPK]), ALU.is_equal))
                    o4 = onehot.rearrange("p (h s) j -> p h s j", h=PH)
                    link(dve.tensor_tensor(o4, o4, idxf[:, :, w, :].unsqueeze(2).broadcast_to([P, PH, TOPK, TOPK]), ALU.mult))
                    link(dve.tensor_reduce(sel[:, w, :], onehot, AX.X, ALU.add))
                if b == 0:
                    dve.scalar_tensor_tensor(out=idx[:, :], in0=sel[:, 0, :], scalar=float(NKEY), in1=sel[:, 1, :],
                                             op0=ALU.mult, op1=ALU.add).then_inc(s_idx, 1)

            def gate_weights(n):
                b = ORDER[n]
                dve.wait_ge(s_gexp, n + 1)
                link(dve.tensor_reduce(gsum[:, 0, :], top[:, :, :], AX.X, ALU.add))
                link(dve.reciprocal(gsum[:, 0, :], gsum[:, 0, :]))
                dve.tensor_tensor(gates[:, min(b, 1), :].rearrange("p (h j) -> p h j", h=PH), top[:, :, :],
                                  gsum[:, 0, :].unsqueeze(2).broadcast_to([P, PH, TOPK]), ALU.mult).then_inc(s_gate, 1)

            def gate_rows(b, part):
                if part == 0:
                    dve.wait_ge(s_selT, b)
                for p in range(part * PART, (part + 1) * PART):
                    q = (b - 1) * QUADS + p
                    if q >= RR1:
                        dve.wait_ge(s_gq, q - RR1 + 1)
                    for t in range(QUAD):
                        at = p * QUAD + t
                        ins = dve.tensor_scalar(rhs1[q % RR1][:, t, :], iota[:, :], selT[:, b % 2, 0, at:at + 1],
                                                selT[:, b % 2, 2, at:at + 1], ALU.is_equal, ALU.mult)
                    ins.then_inc(s_rhs1, 1)

            dve.wait_ge(s_out, 32)
            dve.wait_ge(s_spill, 16 * NBLK)
            for n, b in enumerate(ORDER):
                for g in range(4):
                    key_tops(b, g)
                    if n and g:
                        gate_rows(n, 2 * g - 2)
                    dve.wait_ge(s_step, steps[0])
                    pair_tops(g)
                    if n and g:
                        gate_rows(n, 2 * g - 1)
                dve.wait_ge(s_step, steps[0])
                select(n)
                if n:
                    gate_rows(n, PARTS - 2)
                    gate_rows(n, PARTS - 1)
                if n + 1 == NBLK:
                    dve.wait_ge(s_hThi, 1)
                    dve.tensor_tensor(hT_lo[:, :, :], h2T[:, :, P:], hT_hi[:, :, :].bitcast(f32),
                                      ALU.subtract).then_inc(s_hTlo, 1)
                gate_weights(n)

            def split_u(n, r, first):
                dve.wait_ge(s_uhi, n + 1)
                dve.tensor_tensor(U_lo[:, r], U_in[:, r], U_hi[:, r].bitcast(f32), ALU.subtract).then_inc(s_ulo, 1)

            def experts(i, first, last, prompt_row):
                for j in range(GRP):
                    n = i * GRP + j
                    if not (last and j == GRP - 1):
                        split_u(n + 1, (j + 1) % 2, False)
                    dve.wait_ge(s_vhi, n + 1)
                    dve.tensor_tensor(V_lo[:, j], V_in[:, j % 2], V_hi[:, j].bitcast(f32), ALU.subtract).then_inc(s_vlo, 1)
                    dve.wait_ge(s_gin[j], 16 * (i + 1))
                    dve.wait_ge(s_ge, n + 1)
                    dve.tensor_tensor(act_t[:, j % 2], act_t[:, j % 2], gate_in[:, j], ALU.mult).then_inc(s_c, 1)
                    dve.wait_ge(s_chi, n + 1)
                    dve.tensor_tensor(C_lo[:, j], act_t[:, j % 2], C_hi[:, j].bitcast(f32), ALU.subtract).then_inc(s_clo, 1)
                for q in range(8):
                    prompt_row(i, q)
                    dve.wait_ge(s_vb, 8 * i + q + 1)
                    part = acc[:, q // 2, (q % 2) * NC:(q % 2 + 1) * NC]
                    dve.tensor_tensor(part, part, ps[:, 4 + q % 4, :], ALU.add).then_inc(s_flush, 1)
                    if last and q % 2:
                        residual(q // 2)
                        if q > 1:
                            norm3(q // 2 - 1)

            def dot_row(i, q):
                r = q % RR
                dve.wait_ge(s_row[r], 16 * (2 * i + q // RR + 1))
                at = i * ROWS + q
                dst = dots[:, at:at + 1] if isinstance(at, int) else dots[:, ds(at, 1)]
                dve.scalar_tensor_tensor(out=rowr[:, r, :], in0=rowr[:, r, :], scalar=1.0, in1=H2[0],
                                         op0=ALU.mult, op1=ALU.mult, accum_out=dst).then_inc(s_used, 1)

            def add_row(i, q):
                r = q % RR
                dve.wait_ge(s_row[r], 16 * (2 * i + q // RR + 1))
                dve.wait_ge(s_used, i * ROWS + q)
                at = (i - NGRP // 2) * ROWS + q
                c = coef[:, at:at + 1] if isinstance(at, int) else coef[:, ds(at, 1)]
                dve.scalar_tensor_tensor(out=acc0, in0=rowr[:, r, :], scalar=c, in1=acc0,
                                         op0=ALU.mult, op1=ALU.add).then_inc(s_used, 1)

            def residual(n):
                b = ORDER[n]
                if n == 0:
                    dve.wait_ge(s_xf, 16)
                if b:
                    dve.wait_ge(s_flush, 8 * (NGRP - 1) + 2 * b)
                else:
                    dve.wait_ge(s_used, 2 * SLOTS)
                a = acc0 if b == 0 else acc[:, b - 1]
                link(dve.tensor_tensor(a, a, G2[:, min(b, 1), :], ALU.mult))
                dve.tensor_tensor(XF[:, b], XF[:, b], a, ALU.add).then_inc(s_x2, 1)

            def norm3(n):
                b = ORDER[n]
                if n == 0:
                    dve.wait_ge(s_fing, 16)
                dve.wait_ge(s_sq3, n + 1)
                dve.tensor_scalar(ss[:, b:b + 1], ss[:, b:b + 1], 1.0 / D, EPS, ALU.mult, ALU.add).then_inc(s_var3, 1)
                dve.wait_ge(s_rstd3, n + 1)
                dve.scalar_tensor_tensor(out=XF[:, b], in0=XF[:, b], scalar=rstd[:, b:b + 1], in1=fing,
                                         op0=ALU.mult, op1=ALU.mult).then_inc(s_y, 1)

            split_u(0, 0, True)
            dve.wait_ge(s_gate, NBLK)
            dve.wait_ge(s_gq, QUADS * NSMP)
            dve.memset(cutout(XO, 5120), 0.0).then_inc(s_acc0, 1)
            dve.wait_ge(s_acc0, 1)
            experts(0, True, False, dot_row)
            with dve.Fori(1, NGRP // 2) as i:
                experts(i, False, False, dot_row)
            dve.wait_ge(s_gelu, 1)
            dve.tensor_tensor(coef[:, :], dots[:, :], gates[:, 0, :], ALU.mult).then_inc(s_coef, 1)
            dve.wait_ge(s_coef, 1)
            with dve.Fori(NGRP // 2, NGRP - 1) as i:
                experts(i, False, False, add_row)
            experts(NGRP - 1, False, True, add_row)

            residual(NBLK - 1)
            norm3(NBLK - 2)
            norm3(NBLK - 1)

        @block.tensor
        def _(pe):
            def bank1(*name):
                i = B1.pos[name]
                if i >= 8:
                    who, n = B1.emptied(i - 8)
                    pe.wait_ge(s_act1 if who == "act" else s_dve1, n)
                return ps[:, i % 8, :]

            def chunk_ready(i):
                pe.wait_ge(s_chunk[i % WRING], 16 * (i // WRING + 1))

            pe.wait_ge(s_sil, 1)
            pe.wait_ge(s_set, 1)
            pe.wait_ge(s_bmod, 16)
            for j in range(MOD_CH):
                out = bank1("mod", j)
                chunk_ready(j)
                for k in range(KD):
                    last = nc.tensor.matmul(out[0:33, :], sil[:, k, :], chunk[:, j % WRING, k, :], start=(k == 0), stop=False)
                last.then_inc(s_chunk_used, 1)
                nc.tensor.matmul(out[0:33, :], ones[:, :], bmod[:, j * NC:(j + 1) * NC], start=False,
                                 stop=True).then_inc(s_fill1, 1)
            pe.wait_ge(s_const, 48)
            pe.wait_ge(s_kc, 16)
            out = bank1("keyT", "cache")
            for h in range(H):
                last = nc.tensor.transpose(out[:, h * P:(h + 1) * P], ktc[:, h * P:(h + 1) * P], ident[:, :])
            last.then_inc(s_fill1, 1)
            for b in range(NBLK):
                pe.wait_ge(s_h1, b + 1)
                for half in range(2):
                    out = bank1("hT", b, half)
                    for k in range(4):
                        last = nc.tensor.transpose(out[:, k * P:(k + 1) * P],
                                                   H1[:, b, (4 * half + k) * P:(4 * half + k + 1) * P], ident[:, :])
                    last.then_inc(s_fill1, 1)

            def z(c, b):
                i = MOD_CH + IN_ORDER[c]
                out = bank1("z", c, b)
                if b == 0:
                    chunk_ready(i)
                pe.wait_ge(s_act1, B1.emptied(B1.pos[("hT", b, 1)])[1])
                for k in range(KD):
                    last = nc.tensor.matmul(out, HT[:, k, b * P:(b + 1) * P], chunk[:, i % WRING, k, :],
                                            start=(k == 0), stop=(k == KD - 1))
                last.then_inc(s_fill1, 1)
                if b == NBLK - 1:
                    pe.wait_ge(s_fill1, B1.pos[("z", c, b)] + 1)
                    pe.nop().then_inc(s_chunk_used, 1)

            def headT(c, b):
                out = bank1("headT", c, b)
                who, n = B1.emptied(B1.pos[("z", c, b)])
                pe.wait_ge(s_act1 if who == "act" else s_dve1, n)
                for h in range(H):
                    last = nc.tensor.transpose(out[:, h * P:(h + 1) * P], heads[:, b % 2, h * P:(h + 1) * P], ident[:, :])
                last.then_inc(s_fill1, 1)

            for c in ("k", "q"):
                for b in range(NBLK):
                    z(c, b)
                    if b:
                        headT(c, b - 1)
                headT(c, NBLK - 1)
            for c in ("v", "f"):
                for b in range(NBLK):
                    z(c, b)

            pe.wait_ge(s_dft, 32)
            chunk_ready(DFT_C)
            for m in range(2):
                nc.tensor.matmul(bank1("fold", m), dftC[:, 2 * m, :], wf, start=True, stop=True).then_inc(s_fill1, 1)
            units = [(s, g) for s in range(2) for g in range(4)]

            def fourier_pos(u):
                s, g = u
                for m, name in enumerate(("fcos", "fsin")):
                    out = bank1(name, s, g)
                    fcols = slice(g * P, (g + 1) * P)
                    if s == 0:
                        last = nc.tensor.matmul(out[:, 0:P], F[:, 0, fcols], dftC[:, m, :], start=True, stop=True)
                    else:
                        for b in range(NSMP):
                            last = nc.tensor.matmul(out, F[:, 1 + b, fcols], dftS[:, m, b, :], start=(b == 0), stop=(b == NSMP - 1))
                    last.then_inc(s_fill1, 1)

            def fourier_ch(u):
                s, g = u
                i = units.index(u)
                w = NC if s else P
                out = bank1("fmix", s, g)
                pe.wait_ge(s_act1, B1.emptied(B1.pos[("fcos", s, g)])[1])
                pe.wait_ge(s_dve1, B1.emptied(B1.pos[("fsin", s, g)])[1])
                nc.tensor.matmul(out[:, 0:w], fold[:, 0, g, :], fstage[:, i % 2, 0, 0:w], start=True, stop=False)
                nc.tensor.matmul(out[:, 0:w], fold[:, 1, g, :], fstage[:, i % 2, 1, 0:w], start=False, stop=True).then_inc(s_fill1, 1)

            pe.wait_ge(s_act1, B1.emptied(B1.pos[("z", "f", NBLK - 1)])[1])
            for i, u in enumerate(units):
                fourier_pos(u)
                if i:
                    fourier_ch(units[i - 1])
            fourier_ch(units[-1])
            pe.wait_ge(s_fill1, B1.total)
            pe.nop().then_inc(s_chunk_used, 1)

            pe.wait_ge(s_act1, B1.count("act"))
            pe.wait_ge(s_dve1, B1.count("dve"))
            pe.wait_ge(s_vc, 16)

            def scores(i):
                b, h = UNITS[i]
                for m in range(2):
                    if i:
                        pe.wait_ge(s_exp, 2 * (i - 1) + m + 1)
                    part = slice(DH * m, DH * m + DH)
                    q = qT[part, h, b * P:(b + 1) * P]
                    if b == 0:
                        last = nc.tensor.matmul(ps[:, 2 * m, 0:P], q, kT[part, h, 0:P], start=True, stop=True)
                    else:
                        for z_ in range(2):
                            k0 = P + z_ * (KEYS_S // 2)
                            last = nc.tensor.matmul(ps[:, 2 * m + z_, 0:KEYS_S // 2], q, kT[part, h, k0:k0 + KEYS_S // 2],
                                                    start=True, stop=True)
                    last.then_inc(s_scores, 1)

            def key_blocks(b):
                return 1 if b == 0 else 5

            def weightsT(i):
                pe.wait_ge(s_w, i + 1)
                if i:
                    pe.wait_ge(s_wTc, i)
                for s in range(key_blocks(UNITS[i][0])):
                    last = nc.tensor.transpose(ps[:, 4 + s // 4, (s % 4) * P:(s % 4) * P + P],
                                               Wt[:, i % 2, s * P:(s + 1) * P], ident[:, :])
                last.then_inc(s_wT, 1)

            def products(i):
                b, h = UNITS[i]
                nk = key_blocks(b)
                pe.wait_ge(s_wTc, i + 1)
                if h == 0 and b:
                    pe.wait_ge(s_praw, b)
                for s in range(nk):
                    vb = 0 if b == 0 else 1 + s
                    last = nc.tensor.matmul(ps[:, 6, h * P:(h + 1) * P], WtT[:, i % 2, s, :], V[:, vb, h * P:(h + 1) * P],
                                            start=(s == 0), stop=(s == nk - 1))
                last.then_inc(s_pv, 1)

            def attT(b):
                pe.wait_ge(s_att, b + 1)
                if b:
                    pe.wait_ge(s_mix, b)
                for h in range(H):
                    last = nc.tensor.transpose(ps[:, 7, h * P:(h + 1) * P], att[:, h * P:(h + 1) * P], ident[:, :])
                last.then_inc(s_attT, 1)

            scores(0)
            for i in range(len(UNITS) + 3):
                if i + 1 < len(UNITS):
                    scores(i + 1)
                if i < len(UNITS):
                    weightsT(i)
                if 0 < i <= len(UNITS):
                    products(i - 1)
                if i % H == 2 and i > H:
                    attT(i // H - 1)

            def bank2(*name):
                i = B2.pos[name]
                if i >= 4:
                    who, n = B2.emptied(i - 4)
                    pe.wait_ge(s_act2 if who == "act" else s_dve2, n)
                return ps[:, i % 4, :]

            pe.wait_ge(s_mix, NBLK)
            pe.wait_ge(s_exp, 2 * len(UNITS))
            chunk_ready(OUT_C)
            chunk_ready(OUT_C + 1)
            for b in range(NBLK):
                for half in range(2):
                    out = bank2("merge", b, half)
                    for k in range(KD):
                        last = nc.tensor.matmul(out, mixT[:, k, b * P:(b + 1) * P], chunk[:, (OUT_C + half) % WRING, k, :],
                                                start=(k == 0), stop=(k == KD - 1))
                    last.then_inc(s_fill2, 1)

            for b in range(NBLK):
                pe.wait_ge(s_h2, b + 1)
                for half in range(2):
                    out = bank2("h2T", b, half)
                    for k in range(4):
                        last = nc.tensor.transpose(out[:, k * P:(k + 1) * P],
                                                   H2[b][:, (4 * half + k) * P:(4 * half + k + 1) * P], ident[:, :])
                    last.then_inc(s_fill2, 1)

            def query(b, g, half):
                i = B2.pos[("query", b, g)]
                out = bank2("query", b, g) if half == 0 else ps[:, i % 4, :]
                for j in (2 * half, 2 * half + 1):
                    for k in range(KD):
                        c = (4 * g + j) * P
                        last = nc.tensor.matmul(out[:, j * P:(j + 1) * P], wq[:, k, c:c + P] if k < 7 else wq7[:, c:c + P],
                                                h2T[:, k, b * P:(b + 1) * P],
                                                start=(k == 0), stop=(k == KD - 1))
                if half:
                    last.then_inc(s_fill2, 1)
                    out = bank2("score", b, g)
                    pe.wait_ge(s_act2, B2.emptied(i)[1])
                    for j in range(4):
                        last = nc.tensor.matmul(out[:, j * P:(j + 1) * P], qTq[:, j, :], keys[:, 4 * g + j, :],
                                                start=True, stop=True)
                    last.then_inc(s_fill2, 1)

            def selT_fill(b):
                pe.wait_ge(s_gate, b)
                out = bank2("selT", b)
                for w, src in enumerate((sel[:, 0, :], sel[:, 1, :], gates[:, 1, :])):
                    last = nc.tensor.transpose(out[:, w * P:(w + 1) * P], src, ident[:, :])
                last.then_inc(s_fill2, 1)

            def dense_gates(b, part):
                for p in range(part * PART, (part + 1) * PART):
                    q = (b - 1) * QUADS + p
                    pe.wait_ge(s_lhs1, q + 1)
                    pe.wait_ge(s_rhs1, q + 1)
                    if q >= 4:
                        pe.wait_ge(s_gev, q - 3)
                    for t in range(QUAD):
                        last = nc.tensor.matmul(ps[:, 4 + q % 4, t * P:(t + 1) * P], lhs1[q % LR][:, t, :],
                                                rhs1[q % RR1][:, t, :], start=True, stop=True)
                    last.then_inc(s_gq, 1)

            pe.wait_ge(s_wq, 16)
            pe.wait_ge(s_wq7, 16)
            pe.wait_ge(s_keys, 16)
            pe.wait_ge(s_act2, B2.emptied(B2.pos[("h2T", NBLK - 1, 1)])[1])
            for g in range(2):
                query(ORDER[0], g, 0)
                query(ORDER[0], g, 1)
            for n, b in enumerate(ORDER):
                if n:
                    selT_fill(n)
                ahead = [(b, 2, 0), (b, 2, 1), (b, 3, 0), (b, 3, 1)]
                if n + 1 < NBLK:
                    ahead += [(ORDER[n + 1], 0, 0), (ORDER[n + 1], 0, 1), (ORDER[n + 1], 1, 0), (ORDER[n + 1], 1, 1)]
                for part in range(PARTS):
                    if part < len(ahead):
                        query(*ahead[part])
                    if n:
                        dense_gates(n, part)

            def products3(out, hi, lo, rhi, rlo, start, stop):
                nc.tensor.matmul(out, hi, rhi, start=start, stop=False)
                nc.tensor.matmul(out, hi, rlo, start=False, stop=False)
                return nc.tensor.matmul(out, lo, rhi, start=False, stop=stop)

            def experts(i, first):
                for j in range(GRP):
                    n = i * GRP + j
                    pe.wait_ge(s_ulo, n + 1)
                    if not (first and j < 2):
                        pe.wait_ge(s_ge, n - 1)
                    for k in range(KD):
                        last = products3(ps[:, j % 2, :], U_hi[:, j % 2, k, :], U_lo[:, j % 2, k, :],
                                         hT_hi[:, k, :], hT_lo[:, k, :], k == 0, k == KD - 1)
                    last.then_inc(s_a, 1)
                order = [(q, j) for q in range(2) for j in range(GRP - 1)] + [(q, GRP - 1) for q in range(2)]
                order += [(q, j) for q in range(2, 8) for j in range(GRP)]
                for q, j in order:
                    if j == 0 and not (first and q < 4):
                        pe.wait_ge(s_flush, 8 * i + q - 3)
                    if q == 0:
                        pe.wait_ge(s_clo, i * GRP + j + 1)
                        pe.wait_ge(s_vlo, i * GRP + j + 1)
                    tok = slice((q // 2) * P, (q // 2 + 1) * P)
                    col = slice((q % 2) * NC, (q % 2 + 1) * NC)
                    last = products3(ps[:, 4 + q % 4, :], C_hi[:, j, tok], C_lo[:, j, tok],
                                     V_hi[:, j, col], V_lo[:, j, col], j == 0, j == GRP - 1)
                    if j == GRP - 1:
                        last.then_inc(s_vb, 1)

            pe.wait_ge(s_hTlo, 1)
            pe.wait_ge(s_act2, B2.count("act"))
            pe.wait_ge(s_dve2, B2.count("dve"))
            pe.wait_ge(s_gev, QUADS * NSMP)
            experts(0, True)
            with pe.Fori(1, NGRP) as i:
                experts(i, False)


def _constants():
    ident = np.eye(P, dtype=np.float32)
    t = np.arange(NSMP * P)
    nf = DH // 4
    inv = (np.float32(10000.0) ** (-np.arange(nf, dtype=np.float32) / np.float32(nf))).astype(np.float32)
    ar = (t // 64).astype(np.float32)[:, None] * inv
    ac = (t % 64).astype(np.float32)[:, None] * inv
    ang = np.concatenate([ar, ar, ac, ac], -1)
    sign = np.concatenate([-np.ones(16), np.ones(16)] * 2).astype(np.float32)
    cos = np.cos(ang).astype(np.float32).reshape(NSMP, P, DH).transpose(1, 0, 2)
    sin = (np.sin(ang).astype(np.float32) * sign).reshape(NSMP, P, DH).transpose(1, 0, 2)

    def dft(n):
        a = 2 * np.pi * ((np.arange(n)[:, None] * np.arange(n)[None, :]) % n) / n
        return np.cos(a) / np.sqrt(n), np.sin(a) / np.sqrt(n)
    c5, s5 = dft(NSMP * P)
    seq = np.stack([c5, s5]).reshape(2, NSMP, P, NSMP * P).transpose(2, 0, 1, 3).astype(np.float32)
    c1, s1 = dft(P)
    ch = np.stack([c1, s1, -s1]).transpose(1, 0, 2).astype(np.float32)
    return [np.ascontiguousarray(a) for a in (ident, cos, sin, seq, ch)]


def kernel(**inputs):
    import concourse.bacc as bacc
    from concourse.bass_utils import run_bass_kernel_spmd

    g = {k: np.asarray(v) for k, v in inputs.items()}
    ident, cos, sin, seq, ch = _constants()
    arrays = {
        "xall": np.concatenate([g["x_prompt"].reshape(P, D), g["x_sample"].reshape(NSMP * P, D)]),
        "condT": np.stack([g["c_ctx"].reshape(D), g["c"].reshape(D)]).reshape(2, KD, P).transpose(2, 1, 0),
        "w_mod": g["w_mod"][0], "b_mod": g["b_mod"], "norm1_g": g["norm1_g"][0], "w_in": g["w_in"][0],
        "lam4": np.stack([g["lam_q1"][0], g["lam_q2"][0], g["lam_k1"][0], g["lam_k2"][0]]),
        "subln_g": g["subln_g"][0], "w_fourier": g["w_fourier"][0].transpose(1, 0, 2), "w_out": g["w_out"][0],
        "norm2_g": g["norm2_g"][0], "w_query": g["w_query"][0],
        "keysT": g["sub_keys"][0].transpose(3, 0, 1, 2).reshape(P, 16, NKEY),
        "expert_u": g["expert_u"][0],
        "expert_uT": g["expert_u"][0].reshape(NB1, P, KD, P).transpose(0, 3, 2, 1), "expert_v": g["expert_v"][0], "final_g": g["final_g"],
        "cache_k": g["cache_k"].reshape(P, NC), "cache_v": g["cache_v"].reshape(P, NC),
        "ident": ident, "cos": cos, "sin": sin, "dft_seq": seq, "dft_ch": ch,
    }
    arrays = {k: np.ascontiguousarray(v) for k, v in arrays.items()}
    nc = bacc.Bacc("TRN2", target_bir_lowering=False, num_devices=1)
    f32 = mybir.dt.float32
    args = [nc.dram_tensor(f"in_{k}", v.shape, f32, kind="ExternalInput").ap() for k, v in arrays.items()]
    outs = {"y": (NBLK * P, D), "state_k": (P, NC), "state_v": (P, NC)}
    args += [nc.dram_tensor(f"out_{k}", s, f32, kind="ExternalOutput").ap() for k, s in outs.items()]
    program(nc, *args)
    r = run_bass_kernel_spmd(nc, [{f"in_{k}": v for k, v in arrays.items()}], core_ids=[0]).results[0]
    yy = r["out_y"]
    return (yy[:P].reshape(1, P, D), yy[P:].reshape(1, NSMP * P, D),
            r["out_state_k"].reshape(1, 1, P, H, 2 * DH), r["out_state_v"].reshape(1, 1, P, H, 2 * DH))
```
